# Optimizing a Trainium2 kernel written in Bass

```python
import math
import jax, jax.numpy as jnp
from jax import lax
import numpy as np

"""Hybrid decoder layer (parallel head groups, Hymba-style).

x (BATCH, SEQ, D_MODEL) -> pre-RMSNorm -> ONE combined input projection whose columns are
partitioned between two head groups reading the same normalised input:
  group A: native sparse attention (8 query heads, 2 GQA kv groups, head_dim 64) with
           compressed-block, selected-block (top-16 gathered) and sliding-window branches,
           each with its own K/V projection, mixed by per-head sigmoid gates; QK-norm; NoPE.
  group B: gated DeltaNet (4 heads, head_dim 128) with short causal conv on q/k/v,
           per-head decay, chunked delta rule, gated RMSNorm output.
Group outputs are normalised, concatenated and mapped by ONE output projection (residual).
Then pre-RMSNorm -> top-4-of-32 MoE with clamped SwiGLU and a biased softmax router (residual).
Parameters carry a leading DEPTH axis. Output: (BATCH, SEQ, D_MODEL).
"""

D_MODEL = 1024
BATCH = 1
SEQ = 256
DEPTH = 1

NSA_HEADS = 8
NSA_KV_GROUPS = 2
NSA_HPG = NSA_HEADS // NSA_KV_GROUPS
NSA_HEAD_DIM = 64
CMP_BLOCK = 32
CMP_STRIDE = 16
CMP_HIDDEN = 256
SLC_BLOCK = 64
SLC_TOPK = 16
WINDOW = 512
Q_BLOCK = 128
GDN_HEADS = 4
GDN_HEAD_DIM = 128
GDN_CONV = 4
GDN_CHUNK = 64
N_EXPERTS = 32
TOP_K = 4
D_EXPERT = 1024
SWIGLU_LIMIT = 7.0
SWIGLU_ALPHA = 1.702
MOE_ROW_BLOCK = 256

EPS = 1e-6
NEG = -1e30
NSA_WIDTH = NSA_HEADS * NSA_HEAD_DIM
NSA_KV_WIDTH = NSA_KV_GROUPS * NSA_HEAD_DIM
GDN_WIDTH = GDN_HEADS * GDN_HEAD_DIM
MIX_WIDTH = NSA_WIDTH + GDN_WIDTH
IN_SPLITS = (NSA_WIDTH, NSA_KV_WIDTH, NSA_KV_WIDTH, NSA_KV_WIDTH, NSA_KV_WIDTH, NSA_KV_WIDTH,
             NSA_KV_WIDTH, 3 * NSA_HEADS, 3 * GDN_WIDTH, GDN_WIDTH, GDN_HEADS, GDN_HEADS)
IN_WIDTH = sum(IN_SPLITS)

kernel_name = 'hybrid_nsa_gdn_moe_block'

def rms_norm(x, g):
    xf = x.astype(jnp.float32)
    y = xf * lax.rsqrt(jnp.mean(xf * xf, axis=-1, keepdims=True) + EPS)
    return (y * g.astype(jnp.float32)).astype(x.dtype)

def l2_norm(x):
    return x * lax.rsqrt(jnp.sum(x * x, axis=-1, keepdims=True) + EPS)

def masked_probs(s, mask):
    s = jnp.where(mask, s.astype(jnp.float32), NEG)
    m = jnp.max(s, axis=-1, keepdims=True)
    p = jnp.where(mask, jnp.exp(s - m), 0.0)
    return p / jnp.maximum(jnp.sum(p, axis=-1, keepdims=True), 1e-30)

def nsa_compress(u, pos, w1, b1, w2, b2):
    B, T = u.shape[:2]
    n_cmp = (T - CMP_BLOCK) // CMP_STRIDE + 1
    idx = jnp.arange(n_cmp)[:, None] * CMP_STRIDE + jnp.arange(CMP_BLOCK)[None, :]
    kv = u.reshape(B, T, NSA_KV_GROUPS, NSA_HEAD_DIM)
    blocks = kv[:, idx] + pos[:, None, :]
    blocks = blocks.transpose(0, 3, 1, 2, 4).reshape(B, NSA_KV_GROUPS, n_cmp, CMP_BLOCK * NSA_HEAD_DIM)
    hid = jax.nn.gelu(blocks @ w1 + b1)
    return hid @ w2 + b2

def nsa_mixer(u_q, u_kc, u_vc, u_ks, u_vs, u_kw, u_vw, u_gate, q_norm_g, kc_norm_g, ks_norm_g, kw_norm_g,
              ck_pos, ck_w1, ck_b1, ck_w2, ck_b2, cv_pos, cv_w1, cv_b1, cv_w2, cv_b2):
    B, T = u_q.shape[:2]
    G, HPG, DH = NSA_KV_GROUPS, NSA_HPG, NSA_HEAD_DIM
    n_slc = T // SLC_BLOCK
    n_top = min(SLC_TOPK, n_slc)
    q = rms_norm(u_q.reshape(B, T, G, HPG, DH), q_norm_g) * (DH ** -0.5)
    q = q.transpose(0, 2, 3, 1, 4)
    gate = jax.nn.sigmoid(u_gate.reshape(B, T, G, HPG, 3)).transpose(0, 2, 3, 1, 4)
    kc = rms_norm(nsa_compress(u_kc, ck_pos, ck_w1, ck_b1, ck_w2, ck_b2), kc_norm_g)
    vc = nsa_compress(u_vc, cv_pos, cv_w1, cv_b1, cv_w2, cv_b2)
    n_cmp = kc.shape[2]
    ks = rms_norm(u_ks.reshape(B, T, G, DH), ks_norm_g).transpose(0, 2, 1, 3).reshape(B, G, n_slc, SLC_BLOCK, DH)
    vs = u_vs.reshape(B, T, G, DH).transpose(0, 2, 1, 3).reshape(B, G, n_slc, SLC_BLOCK, DH)
    pad = ((0, 0), (0, 0), (WINDOW, 0), (0, 0))
    kw = jnp.pad(rms_norm(u_kw.reshape(B, T, G, DH), kw_norm_g).transpose(0, 2, 1, 3), pad)
    vw = jnp.pad(u_vw.reshape(B, T, G, DH).transpose(0, 2, 1, 3), pad)

    cmp_start = jnp.arange(n_cmp) * CMP_STRIDE
    cmp_end = cmp_start + CMP_BLOCK - 1
    slc_start = jnp.arange(n_slc) * SLC_BLOCK
    overlap = ((cmp_start[:, None] < slc_start[None, :] + SLC_BLOCK) &
               (cmp_start[:, None] + CMP_BLOCK > slc_start[None, :])).astype(jnp.float32)
    blk = jnp.arange(n_slc)
    bi = jnp.arange(B)[:, None, None, None]
    gi = jnp.arange(G)[None, :, None, None]

    def q_block(i):
        s0 = i * Q_BLOCK
        qb = lax.dynamic_slice_in_dim(q, s0, Q_BLOCK, axis=3)
        gb = lax.dynamic_slice_in_dim(gate, s0, Q_BLOCK, axis=3)
        t = s0 + jnp.arange(Q_BLOCK)
        sc = jnp.einsum('bghqd,bgcd->bghqc', qb, kc)
        pc = masked_probs(sc, cmp_end[None, :] <= t[:, None])
        oc = jnp.einsum('bghqc,bgcd->bghqd', pc.astype(vc.dtype), vc)
        imp = jnp.einsum('bghqc,cn->bgqn', pc, overlap)
        cur = t // SLC_BLOCK
        imp = jnp.where(slc_start[None, :] > t[:, None], NEG, imp)
        forced = (blk[None, :] == 0) | (blk[None, :] == cur[:, None]) | (blk[None, :] == cur[:, None] - 1)
        imp = jnp.where(forced, -NEG, imp)
        _, sel = lax.top_k(imp, n_top)
        ksel = ks[bi, gi, sel]
        vsel = vs[bi, gi, sel].reshape(B, G, Q_BLOCK, n_top * SLC_BLOCK, DH)
        pos = sel[..., None] * SLC_BLOCK + jnp.arange(SLC_BLOCK)
        smask = (pos <= t[None, None, :, None, None]).reshape(B, G, 1, Q_BLOCK, n_top * SLC_BLOCK)
        ss = jnp.einsum('bghqd,bgqnsd->bghqns', qb, ksel).reshape(B, G, HPG, Q_BLOCK, n_top * SLC_BLOCK)
        ps = masked_probs(ss, smask)
        osl = jnp.einsum('bghqk,bgqkd->bghqd', ps.astype(vsel.dtype), vsel)
        kwb = lax.dynamic_slice_in_dim(kw, s0, WINDOW + Q_BLOCK, axis=2)
        vwb = lax.dynamic_slice_in_dim(vw, s0, WINDOW + Q_BLOCK, axis=2)
        kpos = s0 - WINDOW + jnp.arange(WINDOW + Q_BLOCK)
        wmask = (kpos[None, :] <= t[:, None]) & (kpos[None, :] > t[:, None] - WINDOW) & (kpos[None, :] >= 0)
        sw = jnp.einsum('bghqd,bgkd->bghqk', qb, kwb)
        pw = masked_probs(sw, wmask)
        ow = jnp.einsum('bghqk,bgkd->bghqd', pw.astype(vwb.dtype), vwb)
        return gb[..., 0:1] * oc + gb[..., 1:2] * osl + gb[..., 2:3] * ow

    outs = lax.map(q_block, jnp.arange(T // Q_BLOCK))
    return outs.transpose(1, 0, 4, 2, 3, 5).reshape(B, T, NSA_WIDTH)

def causal_dwconv(x, w):
    k = w.shape[0]
    return lax.conv_general_dilated(x, w[:, None, :], window_strides=(1,), padding=[(k - 1, 0)],
                                    dimension_numbers=('NWC', 'WIO', 'NWC'), feature_group_count=x.shape[-1])

def chunk_gated_delta(q, k, v, g, beta):
    B, H, T, DK = q.shape
    DV = v.shape[-1]
    C = GDN_CHUNK
    N = T // C
    q = q.reshape(B, H, N, C, DK)
    k = k.reshape(B, H, N, C, DK)
    v = v.reshape(B, H, N, C, DV)
    g = jnp.cumsum(g.reshape(B, H, N, C), axis=-1)
    beta = beta.reshape(B, H, N, C)
    kb = k * beta[..., None]
    vb = v * beta[..., None]
    incl = jnp.tril(jnp.ones((C, C), bool))
    strict = jnp.tril(jnp.ones((C, C), bool), -1)
    decay = jnp.exp(jnp.where(incl, g[..., :, None] - g[..., None, :], -jnp.inf))
    lmat = jnp.where(strict, jnp.einsum('bhncd,bhnsd->bhncs', kb, k) * decay, 0.0)
    eye = jnp.broadcast_to(jnp.eye(C, dtype=q.dtype), lmat.shape)
    tinv = lax.linalg.triangular_solve(eye + lmat, eye, left_side=True, lower=True, unit_diagonal=True)
    u = jnp.einsum('bhncs,bhnse->bhnce', tinv, vb)
    w = jnp.einsum('bhncs,bhnsd->bhncd', tinv, kb * jnp.exp(g)[..., None])
    qk = jnp.where(incl, jnp.einsum('bhncd,bhnsd->bhncs', q, k) * decay, 0.0)
    qg = q * jnp.exp(g)[..., None]
    kd = k * jnp.exp(g[..., -1:] - g)[..., None]
    gl = jnp.exp(g[..., -1])

    def step(S, xs):
        qg_i, kd_i, u_i, w_i, qk_i, gl_i = xs
        v_new = u_i - jnp.einsum('bhcd,bhde->bhce', w_i, S)
        o_i = jnp.einsum('bhcd,bhde->bhce', qg_i, S) + jnp.einsum('bhcs,bhse->bhce', qk_i, v_new)
        S = S * gl_i[..., None, None] + jnp.einsum('bhcd,bhce->bhde', kd_i, v_new)
        return S, o_i

    xs = (jnp.moveaxis(qg, 2, 0), jnp.moveaxis(kd, 2, 0), jnp.moveaxis(u, 2, 0),
          jnp.moveaxis(w, 2, 0), jnp.moveaxis(qk, 2, 0), jnp.moveaxis(gl, 2, 0))
    s0 = jnp.zeros((B, H, DK, DV), jnp.float32)
    _, o = lax.scan(step, s0, xs)
    return jnp.moveaxis(o, 0, 2).reshape(B, H, T, DV)

def gdn_mixer(u_qkv, u_z, u_a, u_b, conv_w, a_log, dt_bias, out_norm_g):
    B, T = u_qkv.shape[:2]
    H, D = GDN_HEADS, GDN_HEAD_DIM
    qkv = jax.nn.silu(causal_dwconv(u_qkv, conv_w)).astype(jnp.float32)
    q, k, v = jnp.split(qkv, 3, axis=-1)
    q, k, v = (a.reshape(B, T, H, D).transpose(0, 2, 1, 3) for a in (q, k, v))
    q = l2_norm(q) * (D ** -0.5)
    k = l2_norm(k)
    beta = jax.nn.sigmoid(u_b.astype(jnp.float32)).transpose(0, 2, 1)
    g = (-jnp.exp(a_log.astype(jnp.float32)) *
         jax.nn.softplus(u_a.astype(jnp.float32) + dt_bias.astype(jnp.float32))).transpose(0, 2, 1)
    o = chunk_gated_delta(q, k, v, g, beta).transpose(0, 2, 1, 3)
    o = rms_norm(o, out_norm_g) * jax.nn.silu(u_z.astype(jnp.float32).reshape(B, T, H, D))
    return o.reshape(B, T, GDN_WIDTH).astype(u_qkv.dtype)

def expert_ffn(xb, wg, bg, wu, bu, wd, bd):
    gate = jnp.minimum(xb @ wg + bg, SWIGLU_LIMIT)
    up = jnp.clip(xb @ wu + bu, -SWIGLU_LIMIT, SWIGLU_LIMIT)
    glu = gate * jax.nn.sigmoid(gate * SWIGLU_ALPHA)
    return ((up + 1.0) * glu) @ wd + bd

def moe_ffn(h, w_router, b_router, w_gate, b_gate, w_up, b_up, w_down, b_down):
    N, D = h.shape
    R = MOE_ROW_BLOCK
    logits = (h @ w_router + b_router).astype(jnp.float32)
    top_val, top_idx = lax.top_k(logits, TOP_K)
    gates = jax.nn.softmax(top_val, axis=-1)
    nk = N * TOP_K
    flat_e = top_idx.reshape(-1)
    order = jnp.argsort(flat_e)
    e_sorted = flat_e[order]
    tok_sorted = order // TOP_K
    gate_sorted = gates.reshape(-1)[order]
    counts = jnp.bincount(flat_e, length=N_EXPERTS)
    starts = jnp.cumsum(counts) - counts
    pcounts = (counts + R - 1) // R * R
    pends = jnp.cumsum(pcounts)
    pstarts = pends - pcounts
    dest = pstarts[e_sorted] + jnp.arange(nk) - starts[e_sorted]
    n_rows = (nk + R - 1) // R * R + N_EXPERTS * R
    n_blocks = n_rows // R
    row_tok = jnp.zeros((n_rows,), jnp.int32).at[dest].set(tok_sorted.astype(jnp.int32))
    row_gate = jnp.zeros((n_rows,), jnp.float32).at[dest].set(gate_sorted)
    blk_e = jnp.minimum(jnp.searchsorted(pends, jnp.arange(n_blocks) * R, side='right'), N_EXPERTS - 1)
    xs = h[row_tok].reshape(n_blocks, R, D)

    def run(args):
        xb, e = args
        return expert_ffn(xb, w_gate[e], b_gate[e], w_up[e], b_up[e], w_down[e], b_down[e])

    ys = lax.map(run, (xs, blk_e)).reshape(n_rows, D)
    ys = ys * row_gate[:, None].astype(ys.dtype)
    return jnp.zeros((N, D), h.dtype).at[row_tok].add(ys)

def setup_inputs(seed: int = 0) -> dict:
    key = jax.random.key(seed)
    keys = iter(list(jax.random.split(key, 64)))

    def normal(shape, scale):
        return jax.random.normal(next(keys), shape, jnp.float32) * scale

    def gain(shape):
        return 1.0 + normal(shape, 0.02)

    L, D, DH = DEPTH, D_MODEL, NSA_HEAD_DIM
    flat = CMP_BLOCK * DH
    dt = jnp.exp(jax.random.uniform(next(keys), (L, GDN_HEADS), jnp.float32, math.log(1e-3), math.log(1e-1)))
    a_log = jnp.log(jax.random.uniform(next(keys), (L, GDN_HEADS), jnp.float32, 1.0, 16.0))
    return {
        'x': normal((BATCH, SEQ, D), 1.0),
        'attn_norm_g': gain((L, D)),
        'w_in': normal((L, D, IN_WIDTH), D ** -0.5),
        'nsa_q_norm_g': gain((L, DH)),
        'nsa_kc_norm_g': gain((L, DH)),
        'nsa_ks_norm_g': gain((L, DH)),
        'nsa_kw_norm_g': gain((L, DH)),
        'cmp_k_pos': normal((L, CMP_BLOCK, DH), 0.1),
        'cmp_k_w1': normal((L, flat, CMP_HIDDEN), flat ** -0.5),
        'cmp_k_b1': normal((L, CMP_HIDDEN), 0.01),
        'cmp_k_w2': normal((L, CMP_HIDDEN, DH), CMP_HIDDEN ** -0.5),
        'cmp_k_b2': normal((L, DH), 0.01),
        'cmp_v_pos': normal((L, CMP_BLOCK, DH), 0.1),
        'cmp_v_w1': normal((L, flat, CMP_HIDDEN), flat ** -0.5),
        'cmp_v_b1': normal((L, CMP_HIDDEN), 0.01),
        'cmp_v_w2': normal((L, CMP_HIDDEN, DH), CMP_HIDDEN ** -0.5),
        'cmp_v_b2': normal((L, DH), 0.01),
        'nsa_out_norm_g': gain((L, NSA_WIDTH)),
        'gdn_conv_w': normal((L, GDN_CONV, 3 * GDN_WIDTH), GDN_CONV ** -0.5),
        'gdn_a_log': a_log,
        'gdn_dt_bias': dt + jnp.log(-jnp.expm1(-dt)),
        'gdn_out_norm_g': gain((L, GDN_HEAD_DIM)),
        'w_out': normal((L, MIX_WIDTH, D), MIX_WIDTH ** -0.5),
        'ffn_norm_g': gain((L, D)),
        'router_w': normal((L, D, N_EXPERTS), D ** -0.5),
        'router_b': normal((L, N_EXPERTS), 0.01),
        'exp_w_gate': normal((L, N_EXPERTS, D, D_EXPERT), D ** -0.5),
        'exp_b_gate': normal((L, N_EXPERTS, D_EXPERT), 0.01),
        'exp_w_up': normal((L, N_EXPERTS, D, D_EXPERT), D ** -0.5),
        'exp_b_up': normal((L, N_EXPERTS, D_EXPERT), 0.01),
        'exp_w_down': normal((L, N_EXPERTS, D_EXPERT, D), D_EXPERT ** -0.5),
        'exp_b_down': normal((L, N_EXPERTS, D), 0.01),
    }

def reference(x, attn_norm_g, w_in, nsa_q_norm_g, nsa_kc_norm_g, nsa_ks_norm_g, nsa_kw_norm_g,
              cmp_k_pos, cmp_k_w1, cmp_k_b1, cmp_k_w2, cmp_k_b2,
              cmp_v_pos, cmp_v_w1, cmp_v_b1, cmp_v_w2, cmp_v_b2,
              nsa_out_norm_g, gdn_conv_w, gdn_a_log, gdn_dt_bias, gdn_out_norm_g, w_out,
              ffn_norm_g, router_w, router_b, exp_w_gate, exp_b_gate, exp_w_up, exp_b_up,
              exp_w_down, exp_b_down):
    B, T, D = x.shape
    splits = [int(s) for s in np.cumsum(IN_SPLITS)[:-1]]
    for l in range(DEPTH):
        h = rms_norm(x, attn_norm_g[l])
        u = h @ w_in[l]
        (u_q, u_kc, u_vc, u_ks, u_vs, u_kw, u_vw, u_gate,
         u_qkv, u_z, u_a, u_b) = jnp.split(u, splits, axis=-1)
        o_nsa = nsa_mixer(u_q, u_kc, u_vc, u_ks, u_vs, u_kw, u_vw, u_gate,
                          nsa_q_norm_g[l], nsa_kc_norm_g[l], nsa_ks_norm_g[l], nsa_kw_norm_g[l],
                          cmp_k_pos[l], cmp_k_w1[l], cmp_k_b1[l], cmp_k_w2[l], cmp_k_b2[l],
                          cmp_v_pos[l], cmp_v_w1[l], cmp_v_b1[l], cmp_v_w2[l], cmp_v_b2[l])
        o_nsa = rms_norm(o_nsa, nsa_out_norm_g[l])
        o_gdn = gdn_mixer(u_qkv, u_z, u_a, u_b, gdn_conv_w[l], gdn_a_log[l], gdn_dt_bias[l], gdn_out_norm_g[l])
        x = x + jnp.concatenate([o_nsa, o_gdn], axis=-1) @ w_out[l]
        h = rms_norm(x, ffn_norm_g[l])
        y = moe_ffn(h.reshape(B * T, D), router_w[l], router_b[l], exp_w_gate[l], exp_b_gate[l],
                    exp_w_up[l], exp_b_up[l], exp_w_down[l], exp_b_down[l])
        x = x + y.reshape(B, T, D)
    return x


_drawn_inputs = setup_inputs


def setup_inputs(seed=0):
    import zlib

    import numpy as np

    out = dict(_drawn_inputs(seed))
    spreads = {}
    factors = {'nsa_q_norm_g': 2.773,
     'nsa_kc_norm_g': 18.996,
     'nsa_ks_norm_g': 2.676,
     'nsa_kw_norm_g': 5.609,
     'cmp_k_b1': 5.755,
     'cmp_k_b2': 37.003,
     'gdn_out_norm_g': 12.6,
     'exp_b_gate': 30.189,
     'exp_b_up': 29.943,
     'exp_b_down': 29.556,
     'cmp_v_b1': 6.129,
     'cmp_v_b2': 6.952,
     'nsa_out_norm_g': 9.609,
     'router_b': 2.729,
     'ffn_norm_g': 3.165}
    for name, (base, spread) in spreads.items():
        noise = np.random.default_rng([zlib.crc32(name.encode()), seed]).standard_normal(out[name].shape)
        drawn = base * np.exp(spread * noise) if base else spread * noise
        out[name] = __import__('jax').numpy.asarray(drawn.astype(out[name].dtype))
    for name, factor in factors.items():
        out[name] = (out[name] * factor).astype(out[name].dtype)
    return out
```

```python
from contextlib import ExitStack

import concourse.bass as bass
from concourse import mybir

F32 = mybir.dt.float32
I32 = mybir.dt.int32
ACT = mybir.ActivationFunctionType
ALU = mybir.AluOpType
AX = mybir.AxisListType

P = 128
SEQ = 256
D = 1024
T2 = SEQ // P
KC = D // P
EPS = 1e-6
BIG = 1e30
DH = 64
NE = 32
CAP = 64
ROUNDS = SEQ // CAP
SLOTS = 4
PAIRS = NE // 2
HD = 128
LEVELS = 7
NCMP = 15

C_ID = 0
C_ONE = C_ID + P
C_TRI = C_ONE + P
C_STR = C_TRI + P
C_CM = C_STR + P
C_DM = C_CM + 2 * P
C_LV = C_DM + P
C_M0 = C_LV + (LEVELS - 1) * P
C_CA = C_M0 + P
C_CX = C_CA + 2 * 16
C_IO = C_CX + 2 * 16
C_END = C_IO + CAP

V_CONV = 0
V_OUTG = 48
V_POS = 52
V_END = 84

B_G12 = 0
B_KCG = B_G12 + 12 * DH
B_GDN = B_KCG + DH
B_RB = B_GDN + HD
B_AL = B_RB + NE
B_DT = B_AL + 4
B_B1 = B_DT + 4
B_B2 = B_B1 + 256
B_END = B_B2 + 2 * DH

SLABS = ["q0", "q1", "q2", "c", "b", "a", "z", "w1k", "w1v", "wo_gdn", "wo_nsa"]
PIECES = {"c": 2, "wo_nsa": 2}
LAST_USER = {("qkv", 1): "q0", ("qkv", 3): "q1", ("qkv", 5): "q2", ("uc", 1): "c", ("ub", 1): "b", ("ua", 1): "a",
             ("uz", 1): "z", ("hid",): "w1v", ("yg", 1, 1): "wo_gdn", ("yn", 1, 1): "wo_nsa"}


def slab_plan():
    uses, landed, plan = [0] * SLOTS, [0] * SLOTS, {}
    for i, name in enumerate(SLABS):
        s = i % SLOTS
        landed[s] += 16 * PIECES.get(name, 1)
        plan[name] = (s, landed[s], uses[s])
        uses[s] += 1
    return plan, uses, landed


def expert_plan():
    count, out = [0] * SLOTS, []
    for q in range(12):
        s = (len(SLABS) + q) % SLOTS
        out.append((s, count[s]))
        count[s] += 1
    assert count == [3] * SLOTS
    return out


def front_jobs():
    j = [("hT", t, i) for t in range(T2) for i in range(2)] + [("vecT",)]
    j += [("qkv", i) for i in range(6)]
    j += [("uc", t) for t in range(T2)] + [("ub", t) for t in range(T2)]
    j += [("gc",)] + [("gb", t) for t in range(T2)]
    j += [("ua", t) for t in range(T2)] + [("uz", t) for t in range(T2)]
    j += [("nat", t, k) for t in range(T2) for k in range(3)]
    j += [("cmpT",)]
    j += [("xT", t, k) for t in range(T2) for k in range(2)]
    j += [("kk", t) for t in range(T2)] + [("qk", t) for t in range(T2)]
    j += [("T0", t) for t in range(T2)]
    for lv in range(1, LEVELS):
        j += [("P", lv, t) for t in range(T2)]
        for t in range(T2):
            j += ([("TP", lv, t)] if lv < LEVELS - 1 else []) + [("PU", lv, t)]
    j += [("uv",), ("wT",), ("s1",), ("v1",), ("o", 0), ("o", 1)]
    j += [("qT", t) for t in range(T2)] + [("kT", t) for t in range(T2)]
    j += [("hid",), ("hidT",), ("cmp2",), ("kcT",)]
    for t in range(T2):
        j += [("sc", t), ("pcT", t)]
    for t in range(T2):
        for b in range(2):
            for g in range(2):
                j += [("s", t, b, g, k) for k in range(2)]
    j += [("pT", t, b, g, s) for t in range(T2) for b in range(2) for g in range(2) for s in range(t + 1)]
    j += [("OT", t) for t in range(T2)]
    j += [("oT", t) for t in range(T2)]
    j += [("ss", t) for t in range(T2)]
    j += [("yg", t, n) for t in range(T2) for n in range(2)]
    j += [("yn", t, n) for t in range(T2) for n in range(2)]
    j += [("h2T", t, i) for t in range(T2) for i in range(2)]
    j += [("lg",), ("pos",), ("GT",)] + [("bd", t, n) for t in range(T2) for n in range(2)]
    return j


def attn_steps():
    return [(t, b, g) for t in range(T2) for b in range(2) for g in range(2)]


def pe_front_order():
    j = front_jobs()
    i0 = j.index(("s", 0, 0, 0, 0))
    i1 = j.index(("oT", 0))
    out = j[:i0]
    steps = attn_steps()
    for i in range(len(steps) + 1):
        if i < len(steps):
            t, b, g = steps[i]
            out += [("s", t, b, g, k) for k in range(2)]
        if i > 0:
            t, b, g = steps[i - 1]
            out += [("pT", t, b, g, s) for s in range(t + 1)]
            if (b, g) == (1, 1):
                out += [("OT", t)]
    return out + j[i1:]


def bank_plan():
    used, plan, turn = [0] * 8, {}, 0
    for job in pe_front_order():
        if job[0] == "OT":
            b = 6 + job[1]
        else:
            b = turn % 6
            turn += 1
        plan[job] = (b, used[b])
        used[b] += 1
    return plan


def hybrid_block(nc, a, out):
    slab, front_uses, front_landed = slab_plan()
    chunks = expert_plan()
    bank = bank_plan()
    fulls, seen = {}, [0] * 8
    for job in pe_front_order():
        if job not in LAST_USER:
            seen[bank[job][0]] += 1
            fulls[job] = seen[bank[job][0]]

    ctx = ExitStack()
    with ctx:
        def sb(name, cols, dt=F32):
            return ctx.enter_context(nc.sbuf_tensor(name, [P, cols], dt))

        sems = {}

        def sem(name):
            if name not in sems:
                sems[name] = ctx.enter_context(nc.semaphore(name))
            return sems[name]

        ring = sb("ring", SLOTS * 4096)
        cst = sb("cst", C_END)
        bc = sb("bc", B_END)
        vT = sb("vT", V_END)
        w2 = sb("w2", 4 * DH)
        rw = sb("rw", KC * NE)
        btab = sb("btab", D)
        gain = sb("gain", D)
        x = sb("x", T2 * D)
        rA = sb("rA", 2048)
        rB = sb("rB", 2048)
        rC = sb("rC", 12 * (SEQ + 3))
        rD = sb("rD", 3072)
        vn = sb("vn", 1024)
        dec = sb("dec", 1024)
        qkm = sb("qkm", 1024)
        bst = sb("bst", 1024)
        scan = sb("scan", 2560)
        vec = scan[:, 0:P]
        nsa = sb("nsa", 8064)
        attn = sb("attn", 3072)
        st = sb("st", 600)
        cnt_i = sb("cnt_i", 1, I32)

        ident = cst[:, C_ID:C_ID + P]
        ones = cst[:, C_ONE:C_ONE + P]
        xt = x[:, :].rearrange("p (t d) -> p t d", t=T2)
        h = rA[:, :].rearrange("p (t d) -> p t d", t=T2)
        hT = rB[:, :].rearrange("p (c t) -> p c t", c=KC)
        cin = rC[:, :].rearrange("p (m t) -> p m t", m=12)
        cv = rD[:, :].rearrange("p (m t) -> p m t", m=12)
        qkn = rA[:, :].rearrange("p (t h d) -> p t h d", t=T2, h=8)
        qkT = rD[:, 0:2048].rearrange("p (h t) -> p h t", h=8)
        kg = rD[:, 2048:2560].rearrange("p (h d) -> p h d", h=4)
        kd = rD[:, 2560:3072].rearrange("p (h d) -> p h d", h=4)
        invT = [rC[:, 512 * t:512 * t + 512].rearrange("p (h s) -> p h s", h=4) for t in range(T2)]
        invU = [rC[:, 1024 + 512 * t:1536 + 512 * t].rearrange("p (h s) -> p h s", h=4) for t in range(T2)]
        invP = [rC[:, 2048 + 512 * t:2560 + 512 * t].rearrange("p (h s) -> p h s", h=4) for t in range(T2)]
        v4 = vn[:, :].rearrange("p (t h d) -> p t h d", t=T2, h=4)
        dec4 = dec[:, :].rearrange("p (t h c) -> p t h c", t=T2, h=4)
        qkm4 = qkm[:, :].rearrange("p (t h c) -> p t h c", t=T2, h=4)
        bst4 = bst[:, :].rearrange("p (t h c) -> p t h c", t=T2, h=4)
        nwT = scan[:, 0:512].rearrange("p (h c) -> p h c", h=4)
        qg = scan[:, 512:1024].rearrange("p (h c) -> p h c", h=4)
        S1 = scan[:, 1024:1536].rearrange("p (h e) -> p h e", h=4)
        vnew = scan[:, 1536:2560].rearrange("p (t h e) -> p t h e", t=T2, h=4)
        og = bst4
        mixT = rB[:, :].rearrange("p (k t) -> p k t", k=8)
        ub = nsa[:, 0:1024].rearrange("p (t n) -> p t n", t=T2)
        uc = nsa[:, 1024:1344].rearrange("p (t n) -> p t n", t=T2)
        nrm = nsa[:, 1344:2880].rearrange("p (t h d) -> p t h d", t=T2, h=12)
        z = nsa[:, 2880:3904].rearrange("p (t h d) -> p t h d", t=T2, h=4)
        qT = nsa[:, 3904:4928].rearrange("p (k t) -> p k t", k=4)
        kbd = nsa[:, 4928:6976].rearrange("p (b g q s) -> p b g q s", b=2, g=2, q=2)
        pcT = nsa[:, 6976:7488]
        vcb = nsa[:, 7488:7616]
        kcb = nsa[:, 7616:7680].rearrange("p (g q c) -> p g q c", g=2, q=2)
        pc = nsa[:, 7680:7936].rearrange("p (h g c) -> p h g c", h=4, g=2)
        smc = nsa[:, 7936:8064].rearrange("p (h c) -> p h c", h=8)
        kv2 = scan[:, 2048:2176]
        kcn = scan[:, 2176:2240]
        pr = [attn[:, 1024 * i:1024 * i + 1024].rearrange("p (h s) -> p h s", h=4) for i in range(2)]
        pT = attn[:, 2048:3072].rearrange("p (s n) -> p s n", s=2)
        cx = attn[:, 0:2048].rearrange("p (v j n) -> p v j n", v=2, j=16)
        cz = attn[:, 2048:3072].rearrange("p (v g t) -> p v g t", v=2, g=2)
        hid = scan[:, 0:256]
        hidT = scan[:, 256:512].rearrange("p (j n) -> p j n", j=2)
        oraw = scan[:, 0:1024].rearrange("p (t h n) -> p t h n", t=T2, h=4)
        osq = scan[:, 1024:2048].rearrange("p (t h n) -> p t h n", t=T2, h=4)
        pos_ = [0]

        def stat(n):
            pos_[0] += n
            assert pos_[0] <= 600
            return st[:, pos_[0] - n:pos_[0]]

        ssx, ssx2 = stat(T2), stat(T2)
        sc32 = stat(64).rearrange("p (t n) -> p t n", t=T2)
        gdt = stat(8).rearrange("p (t n) -> p t n", t=T2)
        gg = stat(8).rearrange("p (t n) -> p t n", t=T2)
        gcs = stat(8).rearrange("p (t n) -> p t n", t=T2)
        glast = stat(4)
        eal = stat(4)
        ssq = stat(16).rearrange("p (t n) -> p t n", t=T2)
        ssn = stat(24).rearrange("p (t n) -> p t n", t=T2)
        ssk = stat(1)
        sso = stat(8).rearrange("p (t n) -> p t n", t=T2)
        rsn = stat(T2)
        mx = [stat(4), stat(4)]
        den = [stat(4), stat(4)]
        mc, dc = stat(8), stat(8)
        lg = stat(64).rearrange("p (t n) -> p t n", t=T2)
        m8 = stat(16).rearrange("p (t n) -> p t n", t=T2)
        gt_ = stat(64).rearrange("p (t n) -> p t n", t=T2)
        eq_ = stat(64).rearrange("p (t n) -> p t n", t=T2)
        cum = stat(64).rearrange("p (t n) -> p t n", t=T2)
        need = stat(2)
        posm = stat(2 * (NE + 1)).rearrange("p (t n) -> p t n", t=T2)
        gates = stat(2 * (NE + 1)).rearrange("p (t n) -> p t n", t=T2)
        gsum = stat(2)
        cmax = stat(1)
        h2 = h
        h2T = hT
        gpad = attn[:, 0:256].rearrange("p (t n) -> p t n", t=T2)
        gTs = scan[:, 2048:2304]
        m_hg = nsa[:, 0:512]
        m_hT = [nsa[:, 512:1024], nsa[:, 1024:1536]]
        m_g = nsa[:, 1536:2048]
        m_sg = nsa[:, 2048:2560]
        m_gs = nsa[:, 2560:3072]
        m_uc = nsa[:, 3072:3584]
        m_act = nsa[:, 3584:4096]
        m_aT = nsa[:, 4096:4608]
        m_y = nsa[:, 4608:5632]
        m_selw = nsa[:, 5632:5888].rearrange("p (t n) -> p t n", t=T2)
        m_selwT = nsa[:, 5888:6144].rearrange("p (t n) -> p t n", t=T2)
        m_sel = [nsa[:, 6144 + 128 * i:6272 + 128 * i].rearrange("p (t n) -> p t n", t=T2) for i in range(2)]
        m_eb = [nsa[:, 6400 + 128 * i:6528 + 128 * i].rearrange("p (w n) -> p w n", w=2) for i in range(2)]

        ps = [ctx.enter_context(nc.psum_tensor(f"bank{b}", [P, 512], F32)) for b in range(8)]
        bG, bU, bA, bT1, bT2, bD, bS0, bS1 = ps

        bank_full = [sem(f"bank_full{b}") for b in range(8)]
        bank_read = [sem(f"bank_read{b}") for b in range(8)]
        landed = [sem(f"slot_landed{s}") for s in range(SLOTS)]
        freed = [sem(f"slot_freed{s}") for s in range(SLOTS)]

        def ringv(s, **k):
            return ring[:, s * 4096:(s + 1) * 4096]

        def signal_of(job):
            if job in LAST_USER:
                s, _, uses = slab[LAST_USER[job]]
                return freed[s], uses + 1
            b = bank[job][0]
            return bank_full[b], fulls[job]

        def full(eng, job):
            eng.wait_ge(*signal_of(job))
            return ps[bank[job][0]]

        def read(ins, job):
            ins.then_inc(bank_read[bank[job][0]], 1)

        def copied(eng, job):
            b, n = bank[job]
            eng.wait_ge(bank_read[b], n + 1)

        def used(eng, it, q):
            s, k = chunks[q]
            eng.wait_ge(freed[s], it * 3 + (front_uses[s] + k + 1))

        def bcast(ap, shape):
            return ap.to_broadcast(shape)

        def two_heads(ap):
            return ap.rearrange("p a b -> p (a b)")

        w_in = a["w_in"][0]
        wi = w_in.rearrange("(c p) n -> p c n", p=P)
        w_out = a["w_out"][0]
        wexp = [a[n][0].rearrange("e (h c p) f -> e h p c f", h=2, p=P)
                for n in ("exp_w_gate", "exp_w_up", "exp_w_down")]

        block = ctx.enter_context(nc.Block())

        @block.sync
        def _(sp):
            cols = {"q0": 1304, "q1": 1816, "q2": 2328, "b": 512, "a": 0, "z": 2840}
            for name in SLABS:
                s, _, uses = slab[name]
                if uses > 0:
                    sp.wait_ge(freed[s], uses)
                dst = ringv(s)
                if name in cols:
                    v = dst.rearrange("p (c n) -> p c n", c=KC)
                    sp.dma_start(v, wi[:, :, cols[name]:cols[name] + 512]).then_inc(landed[s], 16)
                elif name == "c":
                    v = dst.rearrange("p (c n) -> p c n", c=KC)
                    sp.dma_start(v[:, :, 0:280], wi[:, :, 1024:1304]).then_inc(landed[s], 16)
                    sp.dma_start(v[:, :, 280:288], wi[:, :, 3352:3360]).then_inc(landed[s], 16)
                    sp.wait_ge(sem("h_ready"), T2)
                    sp.dma_start(gain[:, :], a["ffn_norm_g"][0].partition_broadcast(P)).then_inc(sem("gain2_landed"), 16)
                elif name in ("w1k", "w1v"):
                    src = a["cmp_k_w1" if name == "w1k" else "cmp_v_w1"][0]
                    sp.dma_start(dst.rearrange("p (j n) -> p j n", j=16),
                                 src.rearrange("(j p) n -> p j n", p=P)).then_inc(landed[s], 16)
                elif name == "wo_gdn":
                    sp.dma_start(dst.rearrange("p (k n) -> p k n", k=4),
                                 w_out[512:1024, :].rearrange("(k p) n -> p k n", p=P)).then_inc(landed[s], 16)
                else:
                    v = w_out[0:512, :].rearrange("(g k d) n -> g d k n", g=2, k=4)
                    for g in range(2):
                        sp.dma_start(dst[64 * g:64 * g + 64, :].rearrange("p (k n) -> p k n", k=4),
                                     v[g]).then_inc(landed[s], 16)

            def pair(it, ip):
                for q in range(12):
                    s, k = chunks[q]
                    par, j = q // 6, q % 6
                    sp.wait_ge(freed[s], it * 3 + (front_uses[s] + k))
                    sp.dma_start(ringv(s).rearrange("p (c f) -> p c f", c=4),
                                 wexp[j // 2][ip * 2 + par, j % 2]).then_inc(landed[s], 16)

            with sp.Fori(0, PAIRS) as ip:
                pair(ip, ip)
            sp.wait_ge(sem("counts_ready"), 1)
            most = sp.value_load(cnt_i[0:1, 0:1], min_val=0, max_val=SEQ)
            with sp.Fori(1, ROUNDS) as r:
                with sp.If(most > r * CAP):
                    with sp.Fori(0, PAIRS) as ip:
                        pair(r * PAIRS + ip, ip)
            sp.wait_ge(sem("result_ready"), 1)
            sp.dma_start(out[0].rearrange("(t p) d -> p t d", p=P), xt).then_inc(sem("out_written"), 16)
            sp.wait_ge(sem("out_written"), 16)

        @block.tensor
        def _(pe):
            order = iter(pe_front_order())

            def take(job):
                nxt = next(order)
                assert nxt == job, (nxt, job)
                b, n = bank[job]
                if n > 0:
                    pe.wait_ge(bank_read[b], n)
                return ps[b]

            def done(ins, job):
                ins.then_inc(signal_of(job)[0], 1)

            pe.wait_ge(sem("x_landed"), 48)
            for t in range(T2):
                pe.wait_ge(sem("h_ready"), t + 1)
                for i in range(2):
                    o = take(("hT", t, i))
                    for c in range(4):
                        m = pe.transpose(o[:, c * P:(c + 1) * P], h[:, t, (4 * i + c) * P:(4 * i + c + 1) * P], ident)
                    done(m, ("hT", t, i))
            pe.wait_ge(sem("vec_landed"), 64)
            o = take(("vecT",))
            done(pe.transpose(o[:, 0:V_END], vec[0:V_END, :], ident[0:V_END, 0:V_END]), ("vecT",))
            copied(pe, ("hT", 0, 0)), copied(pe, ("hT", 0, 1)), copied(pe, ("hT", 1, 0)), copied(pe, ("hT", 1, 1))
            for i in range(6):
                s, val, uses = slab[f"q{i // 2}"]
                w = ringv(s).rearrange("p (c n) -> p c n", c=KC)
                if i % 2 == 0:
                    pe.wait_ge(landed[s], val)
                o = take(("qkv", i))
                for u in range(2):
                    mc0 = (2 * i + u) % 4 * P
                    for c in range(KC):
                        m = pe.matmul(o[:, u * SEQ:(u + 1) * SEQ], w[:, c, mc0:mc0 + P], hT[:, c, :],
                                      start=(c == 0), stop=(c == KC - 1))
                done(m, ("qkv", i))

            def natural(job, name, n):
                s, val, _ = slab[name]
                w = ringv(s).rearrange("p (c n) -> p c n", c=KC)
                pe.wait_ge(landed[s], val)
                for t in range(T2):
                    o = take((job, t))
                    for c in range(KC):
                        m = pe.matmul(o[:, 0:n], hT[:, c, t * P:(t + 1) * P], w[:, c, 0:n],
                                      start=(c == 0), stop=(c == KC - 1))
                    done(m, (job, t))

            natural("uc", "c", 288)
            natural("ub", "b", 512)
            pe.wait_ge(sem("g_ready"), 1)
            o = take(("gc",))
            for t in range(T2):
                m = pe.matmul(o[:, 4 * t:4 * t + 4], cst[:, C_TRI:C_TRI + P], gg[:, t, :], start=True, stop=True)
            done(m, ("gc",))
            for t in range(T2):
                o = take(("gb", t))
                for hd in range(4):
                    m = pe.matmul(o[:, hd * P:(hd + 1) * P], bcast(gg[:, t, hd:hd + 1], [P, P]),
                                  cst[:, C_TRI:C_TRI + P], start=True, stop=True)
                done(m, ("gb", t))
            natural("ua", "a", 512)
            natural("uz", "z", 512)
            pe.wait_ge(sem("silu_ready"), 6)
            for t in range(T2):
                for k in range(3):
                    o = take(("nat", t, k))
                    for hd in range(4):
                        m = pe.transpose(o[:, hd * P:(hd + 1) * P], cv[:, 4 * k + hd, t * P:(t + 1) * P], ident)
                    done(m, ("nat", t, k))
            for t in range(T2):
                copied(pe, ("ub", t))
            o = take(("cmpT",))
            for v in range(2):
                for t in range(T2):
                    m = pe.transpose(o[:, v * SEQ + t * P:v * SEQ + (t + 1) * P], ub[:, t, v * P:(v + 1) * P], ident)
            done(m, ("cmpT",))
            for t in range(T2):
                pe.wait_ge(sem("qkn_ready"), t + 1)
                for k in range(2):
                    o = take(("xT", t, k))
                    for hd in range(4):
                        m = pe.transpose(o[:, hd * P:(hd + 1) * P], qkn[:, t, 4 * k + hd, :], ident)
                    done(m, ("xT", t, k))
            for name, lo in (("kk", 4), ("qk", 0)):
                for t in range(T2):
                    copied(pe, ("xT", t, 0)), copied(pe, ("xT", t, 1))
                    o = take((name, t))
                    for hd in range(4):
                        m = pe.matmul(o[:, hd * P:(hd + 1) * P], qkT[:, 4 + hd, t * P:(t + 1) * P],
                                      qkT[:, lo + hd, t * P:(t + 1) * P], start=True, stop=True)
                    done(m, (name, t))
            for t in range(T2):
                pe.wait_ge(sem("U_ready"), t + 1)
                o = take(("T0", t))
                for hd in range(4):
                    m = pe.transpose(o[:, hd * P:(hd + 1) * P], invU[t][:, hd, :], ident)
                done(m, ("T0", t))
            for lv in range(1, LEVELS):
                for t in range(T2):
                    copied(pe, ("T0", t) if lv == 1 else ("TP", lv - 1, t))
                    o = take(("P", lv, t))
                    for hd in range(4):
                        m = pe.matmul(o[:, hd * P:(hd + 1) * P], dec4[:, t, hd, :], invT[t][:, hd, :],
                                      start=True, stop=True)
                    done(m, ("P", lv, t))
                for t in range(T2):
                    copied(pe, ("P", lv, t))
                    if lv > 1:
                        copied(pe, ("PU", lv - 1, t))
                    if lv < LEVELS - 1:
                        o = take(("TP", lv, t))
                        for hd in range(4):
                            m = pe.matmul(o[:, hd * P:(hd + 1) * P], invU[t][:, hd, :], invP[t][:, hd, :],
                                          start=True, stop=True)
                        done(m, ("TP", lv, t))
                    o = take(("PU", lv, t))
                    for hd in range(4):
                        m = pe.matmul(o[:, hd * P:(hd + 1) * P], invP[t][:, hd, :], invU[t][:, hd, :],
                                      start=True, stop=True)
                    done(m, ("PU", lv, t))
            for t in range(T2):
                copied(pe, ("PU", LEVELS - 1, t))

            def heads(job, lhs, rhs):
                o = take(job)
                for hd in range(4):
                    n = len(lhs)
                    for i in range(n):
                        m = pe.matmul(o[:, hd * P:(hd + 1) * P], lhs[i][:, hd, :], rhs[i][:, hd, :],
                                      start=(i == 0), stop=(i == n - 1))
                done(m, job)

            copied(pe, ("nat", 0, 2)), copied(pe, ("nat", 1, 2))
            heads(("uv",), [invU[0]], [v4[:, 0]])
            pe.wait_ge(sem("kgd_ready"), 1)
            heads(("wT",), [kg], [invU[1]])
            copied(pe, ("uv",))
            heads(("s1",), [kd], [vnew[:, 0]])
            copied(pe, ("s1",)), copied(pe, ("wT",))
            heads(("v1",), [invU[1], nwT], [v4[:, 1], S1])
            copied(pe, ("qk", 0)), copied(pe, ("qk", 1))
            heads(("o", 0), [qkm4[:, 0]], [vnew[:, 0]])
            pe.wait_ge(sem("qg_ready"), 1)
            copied(pe, ("v1",))
            heads(("o", 1), [qg, qkm4[:, 1]], [S1, vnew[:, 1]])

            pe.wait_ge(sem("nrm_ready"), 1)
            for t in range(T2):
                o = take(("qT", t))
                for k in range(4):
                    m = pe.transpose(o[:, k * P:(k + 1) * P], two_heads(nrm[:, t, 2 * k:2 * k + 2, :]), ident)
                done(m, ("qT", t))
            for t in range(T2):
                o = take(("kT", t))
                for b in range(2):
                    m = pe.transpose(o[:, b * P:(b + 1) * P], two_heads(nrm[:, t, 8 + 2 * b:10 + 2 * b, :]), ident)
                done(m, ("kT", t))
            pe.wait_ge(sem("cx_ready"), 1)
            (sk, vk, _), (sv, vv, _) = slab["w1k"], slab["w1v"]
            pe.wait_ge(landed[sk], vk)
            pe.wait_ge(landed[sv], vv)
            o = take(("hid",))
            for j in range(16):
                for v, s in ((0, sk), (1, sv)):
                    m = pe.matmul(o[64 * v:64 * v + 64, 0:256], cx[:, v, j, :],
                                  ringv(s).rearrange("p (j n) -> p j n", j=16)[:, j, :],
                                  start=(j == 0), stop=(j == 15), skip_group_check=True)
                    if (v, j) == (0, 15):
                        m.then_inc(freed[sk], 1)
            done(m, ("hid",))
            pe.wait_ge(sem("hid_ready"), 1)
            o = take(("hidT",))
            for j in range(2):
                m = pe.transpose(o[:, j * P:(j + 1) * P], hid[:, j * P:(j + 1) * P], ident)
            done(m, ("hidT",))
            copied(pe, ("hidT",))
            pe.wait_ge(sem("w2_landed"), 32)
            o = take(("cmp2",))
            for v in range(2):
                for j in range(2):
                    m = pe.matmul(o[0:64, v * DH:(v + 1) * DH], hidT[:, j, 64 * v:64 * v + 64],
                                  w2[:, (2 * v + j) * DH:(2 * v + j + 1) * DH], start=(j == 0), stop=(j == 1))
            done(m, ("cmp2",))
            pe.wait_ge(sem("kcn_ready"), 1)
            o = take(("kcT",))
            done(pe.transpose(o[0:64, 0:64], kcn[0:64, :], ident[0:64, 0:64]), ("kcT",))
            copied(pe, ("kcT",))
            for t in range(T2):
                copied(pe, ("qT", t))
                o = take(("sc", t))
                for k in range(4):
                    m = pe.matmul(o[:, 32 * k:32 * k + 32], qT[:, k, t * P:(t + 1) * P], kcb[:, k // 2, :, :],
                                  start=True, stop=True)
                done(m, ("sc", t))
                pe.wait_ge(sem("pc_ready"), t + 1)
                o = take(("pcT", t))
                for k in range(4):
                    m = pe.transpose(o[0:64, k * P:(k + 1) * P], two_heads(pc[:, k, :, :]), ident)
                done(m, ("pcT", t))
                copied(pe, ("pcT", t))
                pe.matmul(ps[6 + t][:, :], vcb[0:64, :], pcT[0:64, :], start=True, stop=False,
                          skip_group_check=True).then_inc(sem("pc_used"), 1)
            steps = attn_steps()
            copied(pe, ("kT", 0)), copied(pe, ("kT", 1))
            for i in range(len(steps) + 1):
                if i < len(steps):
                    t, b, g = steps[i]
                    for k in range(2):
                        o = take(("s", t, b, g, k))
                        n = P * (t + 1)
                        m = pe.matmul(o[:, 0:2 * n], qT[:, 2 * g + k, t * P:(t + 1) * P], kbd[:, b, g, :, 0:n],
                                      start=True, stop=True)
                        done(m, ("s", t, b, g, k))
                if i > 0:
                    t, b, g = steps[i - 1]
                    pe.wait_ge(sem("pr_ready"), i)
                    for s in range(t + 1):
                        o = take(("pT", t, b, g, s))
                        for hh in range(4):
                            m = pe.transpose(o[:, hh * P:(hh + 1) * P], pr[(i - 1) % 2][:, hh, s * P:(s + 1) * P], ident)
                        done(m, ("pT", t, b, g, s))
                    if (b, g) == (1, 1):
                        take(("OT", t))
                    for s in range(t + 1):
                        copied(pe, ("pT", t, b, g, s))
                        vals = (ub[:, s, 384 + DH * g:384 + DH * (g + 1)], uc[:, s, DH * g:DH * (g + 1)])[b]
                        m = pe.matmul(ps[6 + t][64 * g:64 * g + 64, :], vals, pT[:, s, :], start=False,
                                      stop=((b, s) == (1, t)), skip_group_check=True)
                    if (b, g) == (1, 1):
                        done(m, ("OT", t))
                    else:
                        m.then_inc(sem("pT_used"), 1)

            for t in range(T2):
                pe.wait_ge(sem("og_ready"), t + 1)
                o = take(("oT", t))
                for hd in range(4):
                    m = pe.transpose(o[:, hd * P:(hd + 1) * P], og[:, t, hd, :], ident)
                done(m, ("oT", t))
            for t in range(T2):
                pe.wait_ge(sem("osq_ready"), t + 1)
                o = take(("ss", t))
                for k in range(4):
                    m = pe.matmul(o[:, 0:1], osq[:, t, k, :], ones[:, 0:1], start=(k == 0), stop=(k == 3))
                done(m, ("ss", t))
            for name, lo, sl in (("yg", 4, "wo_gdn"), ("yn", 0, "wo_nsa")):
                s, val, _ = slab[sl]
                w = ringv(s).rearrange("p (k n) -> p k n", k=4)
                pe.wait_ge(landed[s], val)
                for t in range(T2):
                    if lo:
                        copied(pe, ("oT", t))
                    else:
                        pe.wait_ge(sem("mixn_ready"), t + 1)
                    for n in range(2):
                        o = take((name, t, n))
                        for k in range(4):
                            m = pe.matmul(o[:, :], mixT[:, lo + k, t * P:(t + 1) * P], w[:, k, n * 512:(n + 1) * 512],
                                          start=(k == 0), stop=(k == 3))
                        done(m, (name, t, n))
            for t in range(T2):
                pe.wait_ge(sem("h2_ready"), t + 1)
                for i in range(2):
                    o = take(("h2T", t, i))
                    for c in range(4):
                        m = pe.transpose(o[:, c * P:(c + 1) * P], h2[:, t, (4 * i + c) * P:(4 * i + c + 1) * P], ident)
                    done(m, ("h2T", t, i))
            pe.wait_ge(sem("moe_landed"), 64)
            for t in range(T2):
                copied(pe, ("h2T", t, 0)), copied(pe, ("h2T", t, 1))
            o = take(("lg",))
            for t in range(T2):
                for c in range(KC):
                    m = pe.matmul(o[:, NE * t:NE * (t + 1)], h2T[:, c, t * P:(t + 1) * P], rw[:, c * NE:(c + 1) * NE],
                                  start=(c == 0), stop=(c == KC - 1))
            done(m, ("lg",))
            pe.wait_ge(sem("mask_ready"), 1)
            o = take(("pos",))
            pe.matmul(o[:, 0:NE], cst[:, C_STR:C_STR + P], gt_[:, 0, :], start=True, stop=True)
            pe.matmul(o[:, NE:2 * NE], cst[:, C_STR:C_STR + P], gt_[:, 1, :], start=True, stop=False)
            pe.matmul(o[:, NE:2 * NE], ones, gt_[:, 0, :], start=False, stop=True)
            pe.matmul(o[:, 2 * NE:3 * NE], ones, gt_[:, 0, :], start=True, stop=False)
            done(pe.matmul(o[:, 2 * NE:3 * NE], ones, gt_[:, 1, :], start=False, stop=True), ("pos",))
            pe.wait_ge(sem("gpad_ready"), 1)
            o = take(("GT",))
            for t in range(T2):
                m = pe.transpose(o[:, t * P:(t + 1) * P], gpad[:, t, :], ident)
            done(m, ("GT",))
            copied(pe, ("GT",))
            pe.wait_ge(sem("btab_ready"), 1)
            for t in range(T2):
                for n in range(2):
                    o = take(("bd", t, n))
                    done(pe.matmul(o[:, :], gTs[:, t * P:(t + 1) * P], btab[:, n * 512:(n + 1) * 512],
                                   start=True, stop=True), ("bd", t, n))
            for b in range(8):
                pe.wait_ge(bank_read[b], max(n for bb, n in bank.values() if bb == b) + 1)

            def gather(buf, m):
                pe.wait_ge(sem("sel_ready"), m + 1)
                pe.wait_ge(sem("hg_read"), m)
                for t in range(T2):
                    for hf in range(2):
                        i = pe.matmul(bA[64 * hf:64 * hf + 64, :], m_sel[buf][:, t, :], h2[:, t, 512 * hf:512 * hf + 512],
                                      start=(t == 0), stop=(t == 1), skip_group_check=True)
                i.then_inc(sem("gathered"), 1)

            def turn_rows(m):
                pe.wait_ge(sem("hg_read"), m + 1)
                pe.wait_ge(sem("eT_read"), m)
                for j in range(4):
                    i = pe.transpose(bT1[:, j * P:(j + 1) * P], m_hg[:, j * P:(j + 1) * P], ident)
                i.then_inc(sem("rows_turned"), 1)

            def stream(o, it, q0, lhs, first):
                for q in (q0, q0 + 1):
                    s, k = chunks[q]
                    pe.wait_ge(landed[s], it * 48 + (front_landed[s] + 16 * (k + 1)))
                    w = ringv(s).rearrange("p (c f) -> p c f", c=4)
                    for c in range(4):
                        cc = (q - q0) * 4 + c
                        lt = lhs[:, (cc % 4) * P + (cc // 4) * CAP:(cc % 4) * P + (cc // 4) * CAP + CAP]
                        for fh in range(2):
                            i = pe.matmul(o[64 * fh:64 * fh + 64, :], lt, w[:, c, 512 * fh:512 * fh + 512],
                                          start=(first and cc == 0), stop=(cc == 7), skip_group_check=True)
                            if fh == 1 and c == 3:
                                i.then_inc(freed[s], 1)
                return i

            def pair(r, it):
                for par in range(2):
                    n = it * 2 + par
                    m = n + r
                    for w, (o, rd) in enumerate(((bG, "gate_read"), (bU, "up_read"))):
                        if w == 0:
                            pe.wait_ge(sem("eT_read"), m + 1)
                        pe.wait_ge(sem(rd), n)
                        for fh in range(2):
                            pe.matmul(o[64 * fh:64 * fh + 64, :], m_eb[par][:, w, :], btab[:, 512 * fh:512 * fh + 512],
                                      start=True, stop=False, skip_group_check=True)
                        stream(o, it, 6 * par + 2 * w, m_hT[par], False)
                    gather(1 - par, m + 1)
                    if par == 0:
                        pe.wait_ge(sem("selw_ready"), it + 1)
                        pe.wait_ge(sem("added"), it * 4)
                        for t in range(T2):
                            i = pe.transpose(bS0[:, t * P:(t + 1) * P], m_selw[:, t, :], ident)
                        i.then_inc(sem("selw_turned"), 1)
                    pe.wait_ge(sem("act_ready"), n + 1)
                    pe.wait_ge(sem("aT_read"), n)
                    for j in range(4):
                        i = pe.transpose(bT2[:, j * P:(j + 1) * P], m_act[:, j * P:(j + 1) * P], ident)
                    i.then_inc(sem("act_turned"), 1)
                    turn_rows(m + 1)
                    pe.wait_ge(sem("aT_read"), n + 1)
                    pe.wait_ge(sem("y_read"), n)
                    stream(bD, it, 6 * par + 4, m_aT, True)
                pe.wait_ge(sem("selwT_read"), it + 1)
                pe.wait_ge(sem("y_read"), it * 2 + 2)
                for t in range(T2):
                    for hf in range(2):
                        if t > 0:
                            pe.wait_ge(sem("added"), it * 4 + (hf + 1))
                        pe.matmul((bS0, bS1)[hf][:, :], m_selwT[:, t, :], m_y[:, 512 * hf:512 * hf + 512],
                                  start=True, stop=True).then_inc(sem("scattered"), 1)

            gather(0, 0)
            turn_rows(0)
            with pe.Fori(0, PAIRS) as ip:
                pair(0, ip)
            pe.wait_ge(sem("counts_ready"), 1)
            most = pe.value_load(cnt_i[0:1, 0:1], min_val=0, max_val=SEQ)
            with pe.Fori(1, ROUNDS) as r:
                with pe.If(most > r * CAP):
                    gather(0, r * (NE + 1))
                    turn_rows(r * (NE + 1))
                    with pe.Fori(0, PAIRS) as ip:
                        pair(r, r * PAIRS + ip)

        @block.scalar
        def _(act):
            nchain = [0]

            def link(ins):
                nchain[0] += 1
                ins.then_inc(sem("act_chain"), 1)
                act.wait_ge(sem("act_chain"), nchain[0])

            def act_(o, i, f, **k):
                return nc.scalar.activation(o, i, f, **k)

            def copy(o, i):
                return nc.scalar.activation(o, i, ACT.Copy)

            act.dma_start(xt, a["x"][0].rearrange("(t p) d -> p t d", p=P)).then_inc(sem("x_landed"), 16)
            act.dma_start(cst[:, :], a["const_table"]).then_inc(sem("x_landed"), 16)
            act.dma_start(gain[:, :], a["attn_norm_g"][0].partition_broadcast(P)).then_inc(sem("x_landed"), 16)
            act.dma_start(vec[V_CONV:V_CONV + 48, :],
                          a["gdn_conv_w"][0].rearrange("j (m p) -> (j m) p", p=P)).then_inc(sem("vec_landed"), 16)
            act.dma_start(vec[V_OUTG:V_OUTG + 4, :].rearrange("k (g d) -> k g d", g=2),
                          a["nsa_out_norm_g"][0].rearrange("(g k d) -> k g d", g=2, k=4)).then_inc(sem("vec_landed"), 16)
            for v, nm in enumerate(("cmp_k_pos", "cmp_v_pos")):
                act.dma_start(vec[V_POS + 16 * v:V_POS + 16 * v + 16, :].rearrange("j (i d) -> j i d", i=2),
                              a[nm][0].rearrange("(j i) d -> j i d", i=2)).then_inc(sem("vec_landed"), 16)
            nb = [0]

            def row(lo, n, name, rep=1, part=(0, P)):
                nb[0] += 1
                src = a[name][0].partition_broadcast(part[1])
                for k in range(rep):
                    if k:
                        nb[0] += 1
                    act.dma_start(bc[part[0]:part[0] + part[1], lo + k * n:lo + (k + 1) * n], src)\
                       .then_inc(sem("bc_landed"), 16)

            row(B_DT, 4, "gdn_dt_bias")
            row(B_AL, 4, "gdn_a_log")
            row(B_G12, DH, "nsa_q_norm_g", rep=8)
            row(B_G12 + 8 * DH, DH, "nsa_ks_norm_g", rep=2)
            row(B_G12 + 10 * DH, DH, "nsa_kw_norm_g", rep=2)
            row(B_KCG, DH, "nsa_kc_norm_g")
            row(B_GDN, HD, "gdn_out_norm_g")
            row(B_RB, NE, "router_b")
            row(B_B1, 256, "cmp_k_b1", part=(0, 64))
            row(B_B1, 256, "cmp_v_b1", part=(64, 64))
            row(B_B2, DH, "cmp_k_b2")
            row(B_B2 + DH, DH, "cmp_v_b2")
            assert nb[0] == NBC
            for v, nm in enumerate(("cmp_k_w2", "cmp_v_w2")):
                act.dma_start(w2[:, 2 * v * DH:2 * (v + 1) * DH].rearrange("p (j n) -> p j n", j=2),
                              a[nm][0].rearrange("(j p) n -> p j n", p=P)).then_inc(sem("w2_landed"), 16)
            act.dma_start(rw[:, :].rearrange("p (c n) -> p c n", c=KC),
                          a["router_w"][0].rearrange("(c p) n -> p c n", p=P)).then_inc(sem("moe_landed"), 16)
            for i, nm in enumerate(("exp_b_gate", "exp_b_down", "exp_b_up")):
                act.dma_start(btab[NE * i:NE * (i + 1), :], a[nm][0]).then_inc(sem("moe_landed"), 16)

            act.wait_ge(sem("x_landed"), 48)
            for t in range(T2):
                i = act_(h[:, t, :], xt[:, t, :], ACT.Square, accum_out=ssx[:, t:t + 1])
            i.then_inc(sem("ssx_ready"), 1)
            act.wait_ge(sem("msx_ready"), 1)
            act_(ssx, ssx, ACT.Sqrt).then_inc(sem("rms_ready"), 1)
            for t in range(T2):
                for i in range(2):
                    o = full(act, ("hT", t, i))
                    read(copy(hT[:, 4 * i:4 * i + 4, t * P:(t + 1) * P], o[:, :].rearrange("p (c t) -> p c t", c=4)),
                         ("hT", t, i))
            o = full(act, ("vecT",))
            read(copy(vT[:, :], o[:, 0:V_END]), ("vecT",))

            def evac(job, dst, src):
                for d_, s_ in zip(dst, src):
                    ins = copy(d_, s_)
                read(ins, job)

            def ev_qkv(i):
                o = full(act, ("qkv", i))
                evac(("qkv", i), [cin[:, 2 * i:2 * i + 2, 3:]], [o[:, :].rearrange("p (u t) -> p u t", u=2)])

            def silu(i):
                act.wait_ge(sem("conv_ready"), i + 1)
                act_(cv[:, 2 * i:2 * i + 2, :], cv[:, 2 * i:2 * i + 2, :], ACT.Silu).then_inc(sem("silu_ready"), 1)

            act.wait_ge(sem("cin_zeroed"), 1)
            for i in range(6):
                ev_qkv(i)
            for t in range(T2):
                o = full(act, ("uc", t))
                evac(("uc", t), [nrm[:, t, 10:12, :], uc[:, t, :]],
                     [o[:, 0:128].rearrange("p (h d) -> p h d", h=2), o[:, 128:288]])
            for i in range(3):
                silu(i)
            act.wait_ge(sem("sc_ready"), 1)
            act.wait_ge(sem("bc_landed"), 16 * NBC)
            link(act_(sc32, sc32, ACT.Exp))
            act_(eal, bc[:, B_AL:B_AL + 4], ACT.Exp).then_inc(sem("exp_ready"), 1)
            act.wait_ge(sem("sc1_ready"), 1)
            act_(gdt, sc32[:, :, 24:28], ACT.Ln).then_inc(sem("ln_ready"), 1)
            for t in range(T2):
                o = full(act, ("ub", t))
                evac(("ub", t), [nrm[:, t, 8:10, :], ub[:, t, :]],
                     [o[:, 256:384].rearrange("p (h d) -> p h d", h=2), o[:, :]])
            act.wait_ge(sem("gdiff_ready"), 1)
            for t in range(T2):
                link(act_(dec4[:, t], dec4[:, t], ACT.Exp))
            link(act_(qg, qg, ACT.Exp))
            link(act_(gcs[:, 1, :], gcs[:, 1, :], ACT.Exp))
            act_(glast, glast, ACT.Exp).then_inc(sem("decay_ready"), 1)
            for i in range(3, 6):
                silu(i)
            for t in range(T2):
                o = full(act, ("ua", t))
                evac(("ua", t), [nrm[:, t, 0:8, :]], [o[:, :].rearrange("p (h d) -> p h d", h=8)])
            for t in range(T2):
                o = full(act, ("uz", t))
                read(act_(z[:, t], o[:, :].rearrange("p (h d) -> p h d", h=4), ACT.Silu), ("uz", t))
            for t in range(T2):
                for k in range(3):
                    o = full(act, ("nat", t, k))
                    dst = qkn[:, t, 4 * k:4 * k + 4, :] if k < 2 else v4[:, t]
                    evac(("nat", t, k), [dst], [o[:, :].rearrange("p (h d) -> p h d", h=4)])
            act.wait_ge(sem("ssn_ready"), 1)
            act_(ssn, ssn, ACT.Sqrt).then_inc(sem("sqn_ready"), 1)
            act.wait_ge(sem("ssq_ready"), 1)
            act_(ssq, ssq, ACT.Sqrt).then_inc(sem("sqq_ready"), 1)
            for t in range(T2):
                for k in range(2):
                    o = full(act, ("xT", t, k))
                    evac(("xT", t, k), [qkT[:, 4 * k:4 * k + 4, t * P:(t + 1) * P]],
                         [o[:, :].rearrange("p (h d) -> p h d", h=4)])
            for t in range(T2):
                o = full(act, ("T0", t))
                evac(("T0", t), [invT[t]], [o[:, :].rearrange("p (h d) -> p h d", h=4)])
            o = full(act, ("wT",))
            read(nc.scalar.mul(nwT, o[:, :].rearrange("p (h d) -> p h d", h=4), -1.0), ("wT",))
            o = full(act, ("s1",))
            evac(("s1",), [S1], [o[:, :].rearrange("p (h d) -> p h d", h=4)])
            for t in range(T2):
                o = full(act, ("o", t))
                evac(("o", t), [og[:, t]], [o[:, :].rearrange("p (h d) -> p h d", h=4)])
            act.wait_ge(sem("sso_ready"), 1)
            act_(sso, sso, ACT.Sqrt).then_inc(sem("sqo_ready"), 1)
            for t in range(T2):
                o = full(act, ("qT", t))
                evac(("qT", t), [qT[:, :, t * P:(t + 1) * P]], [o[:, :].rearrange("p (k t) -> p k t", k=4)])
            act.wait_ge(sem("zeroed"), 1)
            for t in range(T2):
                o = full(act, ("kT", t))
                ov = o[:, 0:256].rearrange("p (b t) -> p b t", b=2)
                evac(("kT", t), [kbd[64 * p:64 * p + 64, :, g, p, t * P:(t + 1) * P] for g in range(2) for p in range(2)],
                     [ov[64 * g:64 * g + 64] for g in range(2) for p in range(2)])
            copied(act, ("hid",))
            act_(hid, hid, ACT.Gelu_apprx_tanh).then_inc(sem("hid_ready"), 1)
            o = full(act, ("hidT",))
            evac(("hidT",), [hidT], [o[:, 0:256].rearrange("p (j n) -> p j n", j=2)])
            act.wait_ge(sem("ssk_ready"), 1)
            act_(ssk[0:64, :], ssk[0:64, :], ACT.Sqrt).then_inc(sem("sqk_ready"), 1)
            o = full(act, ("kcT",))
            evac(("kcT",), [kcb[64 * p:64 * p + 64, g, p, :] for g in range(2) for p in range(2)],
                 [o[0:64, 32 * g:32 * g + 16] for g in range(2) for p in range(2)])
            for t in range(T2):
                act.wait_ge(sem("smc_ready"), t + 1)
                act_(smc, smc, ACT.Exp).then_inc(sem("ec_ready"), 1)
                o = full(act, ("pcT", t))
                if t:
                    act.wait_ge(sem("pc_used"), t)
                evac(("pcT", t), [pcT[0:64, :]], [o[0:64, :]])
            steps = attn_steps()
            for i in range(len(steps) + 1):
                if i < len(steps):
                    t, b, g = steps[i]
                    n = P * (t + 1)
                    act.wait_ge(sem("max_ready"), i + 1)
                    for hh in range(4):
                        ins = act_(pr[i % 2][:, hh, 0:n], pr[i % 2][:, hh, 0:n], ACT.Exp,
                                   bias=mx[i % 2][:, hh:hh + 1], accum_out=den[i % 2][:, hh:hh + 1])
                    ins.then_inc(sem("exp_done"), 1)
                if i > 0:
                    t, b, g = steps[i - 1]
                    if i > 1:
                        if steps[i - 2][1:] == (1, 1):
                            full(act, ("OT", steps[i - 2][0]))
                        else:
                            act.wait_ge(sem("pT_used"), sum(x_[1:] != (1, 1) for x_ in steps[:i - 1]))
                    for s in range(t + 1):
                        o = full(act, ("pT", t, b, g, s))
                        evac(("pT", t, b, g, s), [pT[:, s, :]], [o[:, :]])
            for t in range(T2):
                o = full(act, ("OT", t))
                evac(("OT", t), [oraw[:, t]], [o[:, :].rearrange("p (h n) -> p h n", h=4)])
            for t in range(T2):
                o = full(act, ("oT", t))
                evac(("oT", t), [mixT[:, 4:8, t * P:(t + 1) * P]], [o[:, :].rearrange("p (h n) -> p h n", h=4)])
            copied(act, ("ss", 0)), copied(act, ("ss", 1))
            act_(rsn, rsn, ACT.Sqrt).then_inc(sem("rsn_sqrt"), 1)
            for t in range(T2):
                copied(act, ("yn", t, 1))
                act_(h2[:, t, :], xt[:, t, :], ACT.Square, accum_out=ssx2[:, t:t + 1]).then_inc(sem("ssx2_ready"), 1)
            act.wait_ge(sem("msx2_ready"), 1)
            act_(ssx2, ssx2, ACT.Sqrt).then_inc(sem("rms2_ready"), 1)
            for t in range(T2):
                for i in range(2):
                    o = full(act, ("h2T", t, i))
                    evac(("h2T", t, i), [h2T[:, 4 * i:4 * i + 4, t * P:(t + 1) * P]],
                         [o[:, :].rearrange("p (c t) -> p c t", c=4)])
            act.wait_ge(sem("lgm_ready"), 1)
            act_(lg, lg, ACT.Exp).then_inc(sem("lge_ready"), 1)
            o = full(act, ("GT",))
            evac(("GT",), [gTs], [o[:, 0:256]])

            def rows_out(m):
                act.wait_ge(sem("gathered"), m + 1)
                act.wait_ge(sem("rows_turned"), m)
                copy(m_hg, bA[:, :]).then_inc(sem("hg_read"), 1)

            def turned_out(buf, m):
                act.wait_ge(sem("rows_turned"), m + 1)
                copy(m_hT[buf], bT1[:, :]).then_inc(sem("eT_read"), 1)

            def pair(r, it):
                for par in range(2):
                    n = it * 2 + par
                    m = n + r
                    act.wait_ge(sem("gate_read"), n + 1)
                    act.wait_ge(sem("gs_done"), n)
                    act_(m_sg, m_g, ACT.Sigmoid, scale=1.702).then_inc(sem("sg_ready"), 1)
                    rows_out(m + 1)
                    if par == 0:
                        act.wait_ge(sem("selw_turned"), it + 1)
                        act.wait_ge(sem("scattered"), it * 4)
                        copy(m_selwT, bS0[:, 0:256].rearrange("p (t n) -> p t n", t=T2)).then_inc(sem("selwT_read"), 1)
                    act.wait_ge(sem("act_turned"), n + 1)
                    copy(m_aT, bT2[:, :]).then_inc(sem("aT_read"), 1)
                    turned_out(1 - par, m + 1)
                    used(act, it, 6 * par + 5)
                    for hf in range(2):
                        i = copy(m_y[64 * par:64 * par + 64, 512 * hf:512 * hf + 512], bD[64 * hf:64 * hf + 64, :])
                    i.then_inc(sem("y_read"), 1)

            rows_out(0)
            turned_out(0, 0)
            with act.Fori(0, PAIRS) as ip:
                pair(0, ip)
            act.wait_ge(sem("counts_ready"), 1)
            most = act.value_load(cnt_i[0:1, 0:1], min_val=0, max_val=SEQ)
            with act.Fori(1, ROUNDS) as r:
                with act.If(most > r * CAP):
                    rows_out(r * (NE + 1))
                    turned_out(0, r * (NE + 1))
                    with act.Fori(0, PAIRS) as ip:
                        pair(r, r * PAIRS + ip)

        @block.gpsimd
        def _(pool):
            nchain = [0]

            def link(ins):
                nchain[0] += 1
                ins.then_inc(sem("pool_chain"), 1)
                pool.wait_ge(sem("pool_chain"), nchain[0])

            nc.gpsimd.memset(cin[:, :, 0:3], 0.0).then_inc(sem("cin_zeroed"), 1)
            pool.wait_ge(sem("cin_zeroed"), 1)
            for v in (kbd, vcb, kcb, pc):
                link(nc.gpsimd.memset(v, 0.0))
            nc.gpsimd.memset(cx, 0.0).then_inc(sem("zeroed"), 1)
            pool.wait_ge(sem("zeroed"), 1)
            nc.gpsimd.memset(btab[96:128, :], 0.0).then_inc(sem("btab_ready"), 1)

        @block.vector
        def _(dve):
            nchain = [0]
            V = nc.vector

            def link(ins):
                nchain[0] += 1
                ins.then_inc(sem("dve_chain"), 1)
                dve.wait_ge(sem("dve_chain"), nchain[0])

            told = {}

            def link_as(ins, name):
                told[name] = told.get(name, 0) + 1
                ins.then_inc(sem(name), 1)
                dve.wait_ge(sem(name), told[name])

            def link_read(ins, job):
                read(ins, job)
                copied(dve, job)

            def rstd(ap, n, wait, sqrt):
                link_as(V.tensor_scalar(ap, ap, 1.0 / n, EPS, ALU.mult, ALU.add), wait)
                dve.wait_ge(sem(sqrt), 1)
                link(V.reciprocal(ap, ap))

            def h4(ap):
                return ap.rearrange("p (h s) -> p h s", h=4)

            dve.wait_ge(sem("ssx_ready"), 1)
            rstd(ssx, D, "msx_ready", "rms_ready")
            for t in range(T2):
                V.scalar_tensor_tensor(out=h[:, t, :], in0=xt[:, t, :], scalar=ssx[:, t:t + 1], in1=gain[:, :],
                                       op0=ALU.mult, op1=ALU.mult).then_inc(sem("h_ready"), 1)
            dve.wait_ge(sem("h_ready"), T2)
            copied(dve, ("vecT",))
            for i in range(6):
                copied(dve, ("qkv", i))
                for tap in range(4):
                    for u in range(2):
                        m = 2 * i + u
                        w = vT[:, V_CONV + 12 * tap + m:V_CONV + 12 * tap + m + 1]
                        src = cin[:, m, tap:tap + SEQ]
                        if tap == 0:
                            ins = V.tensor_scalar(cv[:, m, :], src, w, None, ALU.mult)
                        else:
                            ins = V.scalar_tensor_tensor(out=cv[:, m, :], in0=src, scalar=w, in1=cv[:, m, :],
                                                         op0=ALU.mult, op1=ALU.add)
                    if tap < 3:
                        link(ins)
                    else:
                        ins.then_inc(sem("conv_ready"), 1)
            copied(dve, ("uc", 0)), copied(dve, ("uc", 1))
            dve.wait_ge(sem("bc_landed"), 16 * NBC)
            link(V.tensor_tensor(gdt, uc[:, :, 152:156], bcast(bc[:, B_DT:B_DT + 4].unsqueeze(1), [P, T2, 4]), ALU.add))
            V.tensor_scalar(sc32[:, :, 0:24], uc[:, :, 128:152], -1.0, None, ALU.mult)
            V.tensor_scalar(sc32[:, :, 28:32], uc[:, :, 156:160], -1.0, None, ALU.mult)
            link(V.scalar_tensor_tensor(out=sc32[:, :, 24:28], in0=gdt, scalar=-1.0, in1=gdt, op0=ALU.mult, op1=ALU.min))
            link_as(V.tensor_scalar(gg, gdt, 0.0, None, ALU.max), "sc_ready")
            dve.wait_ge(sem("exp_ready"), 1)
            link_as(V.tensor_scalar(sc32, sc32, 1.0, None, ALU.add), "sc1_ready")
            dve.wait_ge(sem("ln_ready"), 1)
            link(V.tensor_tensor(gg, gg, gdt, ALU.add))
            link_as(V.scalar_tensor_tensor(out=gg, in0=gg, scalar=-1.0, in1=bcast(eal.unsqueeze(1), [P, T2, 4]),
                                        op0=ALU.mult, op1=ALU.mult), "g_ready")
            link(V.reciprocal(sc32, sc32))
            for t in range(T2):
                link(V.tensor_copy(bst4[:, t], bcast(sc32[:, t, 28:32].unsqueeze(2), [P, 4, P])))
                link(V.tensor_tensor(bst4[:, t], bst4[:, t],
                                     bcast(cst[:, C_STR:C_STR + P].unsqueeze(1), [P, 4, P]), ALU.mult))
            o = full(dve, ("gc",))
            link_read(V.tensor_copy(gcs, o[:, 0:8].rearrange("p (t n) -> p t n", t=T2)), ("gc",))
            for t in range(T2):
                o = full(dve, ("gb", t))
                ov = h4(o[:, :])
                if t == 0:
                    V.tensor_copy(glast, ov[:, :, P - 1])
                else:
                    V.tensor_copy(qg, ov)
                link_read(V.tensor_tensor(dec4[:, t], ov, bcast(cst[:, C_DM:C_DM + P].unsqueeze(1), [P, 4, P]), ALU.add), ("gb", t))
                link(V.tensor_tensor(dec4[:, t], dec4[:, t], bcast(gcs[:, t, :].unsqueeze(2), [P, 4, P]), ALU.subtract))
            link_as(V.tensor_tensor(glast, glast, gcs[:, 0, :], ALU.subtract), "gdiff_ready")
            o = full(dve, ("cmpT",))
            ov = o[:, :].rearrange("p (v t) -> p v t", v=2)
            for g in range(2):
                V.tensor_copy(cz[0:64, :, g, :], ov[64 * g:64 * g + 64])
                ins = V.tensor_copy(cz[64:128, :, g, 0:SEQ - 1], ov[64 * g:64 * g + 64, :, 1:SEQ])
            link_read(ins, ("cmpT",))
            dve.wait_ge(sem("zeroed"), 1)
            for v in range(2):
                for g in range(2):
                    pairs = cz[:, v, g, :].rearrange("p (c j i) -> p j c i", j=8, i=2)[:, :, :, 0]
                    for u in range(2):
                        rows = vT[:, V_POS + 16 * v + 8 * u:V_POS + 16 * v + 8 * u + 8].unsqueeze(2)
                        ins = V.tensor_tensor(cx[:, v, 8 * u:8 * u + 8, 32 * g:32 * g + NCMP],
                                              pairs[:, :, u:u + NCMP], bcast(rows, [P, 8, NCMP]), ALU.add)
            link_as(ins, "cx_ready")
            sq = scan[:, 1536:1536 + 768].rearrange("p (h d) -> p h d", h=12)
            copied(dve, ("ua", 0)), copied(dve, ("ua", 1))
            for t in range(T2):
                link(V.tensor_tensor(sq, nrm[:, t], nrm[:, t], ALU.mult))
                link(V.tensor_reduce(ssn[:, t, :], sq, AX.X, ALU.add))
            rstd(ssn, DH, "ssn_ready", "sqn_ready")
            sq = scan[:, 1536:2560].rearrange("p (h d) -> p h d", h=8)
            for t in range(T2):
                copied(dve, ("nat", t, 0)), copied(dve, ("nat", t, 1))
                link(V.tensor_tensor(sq, qkn[:, t], qkn[:, t], ALU.mult))
                link(V.tensor_reduce(ssq[:, t, :], sq, AX.X, ALU.add))
            link(V.tensor_scalar(ssq, ssq, EPS, None, ALU.add))
            link_as(V.tensor_scalar(ssq[:, :, 0:4], ssq[:, :, 0:4], float(HD), None, ALU.mult), "ssq_ready")
            dve.wait_ge(sem("sqq_ready"), 1)
            link(V.reciprocal(ssq, ssq))
            for t in range(T2):
                link_as(V.tensor_tensor(qkn[:, t], qkn[:, t], bcast(ssq[:, t, :].unsqueeze(2), [P, 8, HD]), ALU.mult), "qkn_ready")
            dve.wait_ge(sem("decay_ready"), 1)
            copied(dve, ("nat", 0, 2)), copied(dve, ("nat", 1, 2))
            V.tensor_tensor(kg, qkn[:, 1, 4:8, :], bcast(gcs[:, 1, :].unsqueeze(2), [P, 4, HD]), ALU.mult)
            link_as(V.tensor_tensor(kd, qkn[:, 0, 4:8, :], bcast(glast.unsqueeze(2), [P, 4, HD]), ALU.mult), "kgd_ready")
            for t in range(T2):
                link(V.tensor_tensor(nrm[:, t], nrm[:, t], bcast(ssn[:, t, :].unsqueeze(2), [P, 12, DH]), ALU.mult))
                link_as(V.tensor_tensor(nrm[:, t], nrm[:, t],
                                     bc[:, B_G12:B_G12 + 768].rearrange("p (h d) -> p h d", h=12), ALU.mult), "nrm_ready")
            for t in range(T2):
                ov = h4(full(dve, ("kk", t))[:, :])
                link(V.tensor_tensor(invP[t], dec4[:, t], bst4[:, t], ALU.mult))
                link_read(V.tensor_tensor(invP[t], ov, invP[t], ALU.mult), ("kk", t))
                ov = h4(full(dve, ("qk", t))[:, :])
                link_read(V.tensor_tensor(qkm4[:, t], ov, dec4[:, t], ALU.mult), ("qk", t))
                link(V.tensor_copy(dec4[:, t], invP[t]))
                link(V.tensor_tensor(invP[t], dec4[:, t], bcast(cst[:, C_M0:C_M0 + P].unsqueeze(1), [P, 4, P]), ALU.mult))
                link_as(V.tensor_tensor(invU[t], bcast(ident.unsqueeze(1), [P, 4, P]), invP[t], ALU.subtract), "U_ready")
            link_as(V.tensor_tensor(qg, qg, qkT[:, 0:4, P:2 * P], ALU.mult), "qg_ready")
            for lv in range(1, LEVELS):
                mask = bcast(cst[:, C_LV + (lv - 1) * P:C_LV + lv * P].unsqueeze(1), [P, 4, P])
                for t in range(T2):
                    link_read(V.tensor_tensor(invP[t], h4(full(dve, ("P", lv, t))[:, :]), mask, ALU.mult), ("P", lv, t))
                for t in range(T2):
                    if lv < LEVELS - 1:
                        tp = h4(full(dve, ("TP", lv, t))[:, :])
                    pu = h4(full(dve, ("PU", lv, t))[:, :])
                    if lv < LEVELS - 1:
                        link_read(V.tensor_tensor(invT[t], invT[t], tp, ALU.subtract), ("TP", lv, t))
                    link_read(V.tensor_tensor(invU[t], invU[t], pu, ALU.subtract), ("PU", lv, t))
            for t, job in ((0, ("uv",)), (1, ("v1",))):
                ov = h4(full(dve, job)[:, :])
                link_read(V.tensor_tensor(vnew[:, t], ov, bcast(sc32[:, t, 28:32].unsqueeze(2), [P, 4, HD]), ALU.mult), job)
            copied(dve, ("uz", 0)), copied(dve, ("uz", 1))
            for t in range(T2):
                link(V.tensor_tensor(z[:, t], z[:, t], bcast(bc[:, B_GDN:B_GDN + HD].unsqueeze(1), [P, 4, HD]), ALU.mult))
            copied(dve, ("o", 0)), copied(dve, ("o", 1))
            for t in range(T2):
                link(V.tensor_tensor(qkm4[:, t], og[:, t], og[:, t], ALU.mult))
                link(V.tensor_reduce(sso[:, t, :], qkm4[:, t], AX.X, ALU.add))
            rstd(sso, HD, "sso_ready", "sqo_ready")
            for t in range(T2):
                link(V.tensor_tensor(og[:, t], og[:, t], bcast(sso[:, t, :].unsqueeze(2), [P, 4, HD]), ALU.mult))
                link_as(V.tensor_tensor(og[:, t], og[:, t], z[:, t], ALU.mult), "og_ready")
            o = full(dve, ("hid",))
            link_read(V.tensor_tensor(hid, o[:, 0:256], bc[:, B_B1:B_B1 + 256], ALU.add), ("hid",))
            o = full(dve, ("cmp2",))
            link_read(V.tensor_tensor(kv2[0:64, :], o[0:64, 0:128], bc[0:64, B_B2:B_B2 + 128], ALU.add), ("cmp2",))
            for g in range(2):
                V.tensor_copy(vcb[32 * g:32 * g + 32, 64 * g:64 * g + 64], kv2[32 * g:32 * g + 32, 64:128])
            link(V.tensor_tensor(kcn[0:64, :], kv2[0:64, 0:64], kv2[0:64, 0:64], ALU.mult))
            link(V.tensor_reduce(ssk[0:64, :], kcn[0:64, :], AX.X, ALU.add))
            rstd(ssk[0:64, :], DH, "ssk_ready", "sqk_ready")
            link_as(V.scalar_tensor_tensor(out=kcn[0:64, :], in0=kv2[0:64, 0:64], scalar=ssk[0:64, :],
                                        in1=bc[0:64, B_KCG:B_KCG + DH], op0=ALU.mult, op1=ALU.mult), "kcn_ready")

            def gate(t, b):
                return sc32[:, t, 0:24].rearrange("p (h b) -> p h b", b=3)[:, :, b]

            for t in range(T2):
                ov = full(dve, ("sc", t))[:, 0:128].rearrange("p (h c) -> p h c", h=8)
                link_read(V.scalar_tensor_tensor(out=smc, in0=ov, scalar=DH ** -0.5,
                                            in1=bcast(cst[:, C_CA + 16 * t:C_CA + 16 * t + 16].unsqueeze(1), [P, 8, 16]),
                                            op0=ALU.mult, op1=ALU.add), ("sc", t))
                link(V.tensor_reduce(mc, smc, AX.X, ALU.max))
                link_as(V.tensor_tensor(smc, smc, bcast(mc.unsqueeze(2), [P, 8, 16]), ALU.subtract), "smc_ready")
                dve.wait_ge(sem("ec_ready"), t + 1)
                link(V.tensor_tensor(smc, smc, bcast(cst[:, C_CX + 16 * t:C_CX + 16 * t + 16].unsqueeze(1), [P, 8, 16]),
                                     ALU.mult))
                link(V.tensor_reduce(dc, smc, AX.X, ALU.add))
                link(V.tensor_scalar(dc, dc, 1e-30, None, ALU.max))
                link(V.reciprocal(dc, dc))
                link(V.tensor_tensor(dc, dc, gate(t, 0), ALU.mult))
                if t:
                    full(dve, ("pcT", t - 1))
                for g in range(2):
                    ins = V.tensor_tensor(pc[:, :, g, 0:16], smc[:, 4 * g:4 * g + 4, :],
                                          bcast(dc[:, 4 * g:4 * g + 4].unsqueeze(2), [P, 4, 16]), ALU.mult)
                link_as(ins, "pc_ready")
            steps = attn_steps()
            for i in range(len(steps) + 1):
                if i < len(steps):
                    t, b, g = steps[i]
                    n = P * (t + 1)
                    p_ = pr[i % 2]
                    if i > 1:
                        tt, bb, gg_ = steps[i - 2]
                        full(dve, ("pT", tt, bb, gg_, tt))
                    mask = cst[:, C_CM + 2 * P - n:C_CM + 2 * P]
                    for k in range(2):
                        o = full(dve, ("s", t, b, g, k))
                        link_read(V.scalar_tensor_tensor(out=p_[:, 2 * k:2 * k + 2, 0:n],
                                                    in0=o[:, 0:2 * n].rearrange("p (q s) -> p q s", q=2),
                                                    scalar=DH ** -0.5, in1=bcast(mask.unsqueeze(1), [P, 2, n]),
                                                    op0=ALU.mult, op1=ALU.add), ("s", t, b, g, k))
                    link(V.tensor_reduce(mx[i % 2], p_[:, :, 0:n], AX.X, ALU.max))
                    link_as(V.tensor_scalar(mx[i % 2], mx[i % 2], -1.0, None, ALU.mult), "max_ready")
                if i > 0:
                    t, b, g = steps[i - 1]
                    n = P * (t + 1)
                    p_, d_ = pr[(i - 1) % 2], den[(i - 1) % 2]
                    dve.wait_ge(sem("exp_done"), i)
                    link(V.reciprocal(d_, d_))
                    link(V.tensor_tensor(d_, d_, gate(t, 1 + b)[:, 4 * g:4 * g + 4], ALU.mult))
                    link_as(V.tensor_tensor(p_[:, :, 0:n], p_[:, :, 0:n], bcast(d_.unsqueeze(2), [P, 4, n]), ALU.mult), "pr_ready")
            for t in range(T2):
                copied(dve, ("OT", t))
                link_as(V.tensor_tensor(osq[:, t], oraw[:, t], oraw[:, t], ALU.mult), "osq_ready")
                link_as(V.tensor_tensor(mixT[:, 0:4, t * P:(t + 1) * P], oraw[:, t],
                                     bcast(vT[:, V_OUTG:V_OUTG + 4].unsqueeze(2), [P, 4, P]), ALU.mult), "mixn_ready")
            for t in range(T2):
                o = full(dve, ("ss", t))
                link_read(V.tensor_scalar(rsn[:, t:t + 1], o[:, 0:1], 1.0 / 512, EPS, ALU.mult, ALU.add), ("ss", t))
            dve.wait_ge(sem("rsn_sqrt"), 1)
            link(V.reciprocal(rsn, rsn))
            for t in range(T2):
                for n in range(2):
                    o = full(dve, ("yg", t, n))
                    xs = xt[:, t, n * 512:(n + 1) * 512]
                    link_read(V.tensor_tensor(xs, xs, o[:, :], ALU.add), ("yg", t, n))
            for t in range(T2):
                for n in range(2):
                    o = full(dve, ("yn", t, n))
                    xs = xt[:, t, n * 512:(n + 1) * 512]
                    link_read(V.scalar_tensor_tensor(out=xs, in0=o[:, :], scalar=rsn[:, t:t + 1], in1=xs,
                                                op0=ALU.mult, op1=ALU.add), ("yn", t, n))
            dve.wait_ge(sem("ssx2_ready"), T2)
            rstd(ssx2, D, "msx2_ready", "rms2_ready")
            dve.wait_ge(sem("gain2_landed"), 16)
            for t in range(T2):
                V.scalar_tensor_tensor(out=h2[:, t, :], in0=xt[:, t, :], scalar=ssx2[:, t:t + 1], in1=gain[:, :],
                                       op0=ALU.mult, op1=ALU.mult).then_inc(sem("h2_ready"), 1)
            o = full(dve, ("lg",))
            link_read(V.tensor_tensor(lg, o[:, 0:64].rearrange("p (t n) -> p t n", t=T2),
                                 bcast(bc[:, B_RB:B_RB + NE].unsqueeze(1), [P, T2, NE]), ALU.add), ("lg",))
            for t in range(T2):
                link(V.max(m8[:, t, :], lg[:, t, :]))
            thr = bcast(m8[:, :, 3:4], [P, T2, NE])
            link(V.tensor_tensor(gt_, lg, thr, ALU.is_gt))
            link(V.tensor_tensor(eq_, lg, thr, ALU.is_equal))
            link(V.tensor_reduce(need, gt_, AX.X, ALU.add))
            link(V.tensor_scalar(need, need, -1.0, 4.0, ALU.mult, ALU.add))
            for t in range(T2):
                link(V.tensor_tensor_scan(cum[:, t, :], ones[:, 0:NE], eq_[:, t, :], 0.0, ALU.mult, ALU.add))
            link(V.tensor_tensor(cum, cum, bcast(need.unsqueeze(2), [P, T2, NE]), ALU.is_le))
            link(V.tensor_tensor(eq_, eq_, cum, ALU.mult))
            link_as(V.tensor_tensor(gt_, gt_, eq_, ALU.add), "mask_ready")
            link_as(V.tensor_tensor(lg, lg, bcast(m8[:, :, 0:1], [P, T2, NE]), ALU.subtract), "lgm_ready")
            dve.wait_ge(sem("lge_ready"), 1)
            link(V.tensor_tensor(lg, lg, gt_, ALU.mult))
            link(V.tensor_reduce(gsum, lg, AX.X, ALU.add))
            link(V.reciprocal(gsum, gsum))
            link(V.memset(gpad, 0.0))
            link(V.memset(gates, 0.0))
            link(V.tensor_tensor(gates[:, :, 0:NE], lg, bcast(gsum.unsqueeze(2), [P, T2, NE]), ALU.mult))
            link_as(V.tensor_copy(gpad[:, :, NE:2 * NE], gates[:, :, 0:NE]), "gpad_ready")
            link(V.memset(posm, 0.0))
            o = full(dve, ("pos",))
            link(V.scalar_tensor_tensor(out=posm[:, :, 0:NE], in0=o[:, 0:64].rearrange("p (t n) -> p t n", t=T2),
                                        scalar=1.0, in1=gt_, op0=ALU.add, op1=ALU.mult))
            link_read(V.tensor_reduce(cmax, o[:, 64:96], AX.X, ALU.max), ("pos",))
            link(V.tensor_scalar(posm, posm, -1.0, None, ALU.add))
            link_as(V.tensor_copy(cnt_i[:, :], cmax), "counts_ready")
            for t in range(T2):
                for n in range(2):
                    o = full(dve, ("bd", t, n))
                    xs = xt[:, t, n * 512:(n + 1) * 512]
                    link_read(V.tensor_tensor(xs, xs, o[:, :], ALU.add), ("bd", t, n))

            iota = cst[:, C_IO:C_IO + CAP]

            def select(buf, e):
                for t in range(T2):
                    V.tensor_scalar(m_sel[buf][:, t, :], iota, posm[:, t, bass.ds(e, 1)], None, ALU.is_equal)
                V.tensor_copy(m_eb[buf][:, 0, :], bcast(ident[:, bass.ds(e, 1)], [P, CAP]))
                V.tensor_copy(m_eb[buf][:, 1, :], bcast(cst[:, bass.ds(e + (C_ID + 2 * NE), 1)], [P, CAP]))\
                    .then_inc(sem("sel_ready"), 1)

            def pair(r, it, ip):
                for par in range(2):
                    n = it * 2 + par
                    if par == 0:
                        for t in range(T2):
                            for u in range(2):
                                ins = V.tensor_scalar(m_selw[:, t, u * CAP:(u + 1) * CAP], iota,
                                                      posm[:, t, bass.ds(ip * 2 + u, 1)],
                                                      gates[:, t, bass.ds(ip * 2 + u, 1)], ALU.is_equal, ALU.mult)
                        ins.then_inc(sem("selw_ready"), 1)
                    select(1 - par, ip * 2 + (par + 1))
                    used(dve, it, 6 * par + 1)
                    V.tensor_scalar(m_g, bG[:, :], 7.0, None, ALU.min).then_inc(sem("gate_read"), 1)
                    dve.wait_ge(sem("sg_ready"), n + 1)
                    V.tensor_tensor(m_gs, m_g, m_sg, ALU.mult).then_inc(sem("gs_done"), 1)
                    used(dve, it, 6 * par + 3)
                    V.tensor_scalar(m_uc, bU[:, :], -7.0, 7.0, ALU.max, ALU.min).then_inc(sem("up_read"), 1)
                    dve.wait_ge(sem("gs_done"), n + 1)
                    dve.wait_ge(sem("up_read"), n + 1)
                    dve.wait_ge(sem("act_turned"), n)
                    V.scalar_tensor_tensor(out=m_act, in0=m_uc, scalar=1.0, in1=m_gs, op0=ALU.add, op1=ALU.mult)\
                        .then_inc(sem("act_ready"), 1)
                for t in range(T2):
                    for hf in range(2):
                        dve.wait_ge(sem("scattered"), it * 4 + (2 * t + hf + 1))
                        xs = xt[:, t, 512 * hf:512 * hf + 512]
                        V.tensor_tensor(xs, xs, (bS0, bS1)[hf][:, :], ALU.add).then_inc(sem("added"), 1)
                dve.wait_ge(sem("added"), it * 4 + 4)

            select(0, 0)
            with dve.Fori(0, PAIRS) as ip:
                pair(0, ip, ip)
            most = dve.value_load(cnt_i[0:1, 0:1], min_val=0, max_val=SEQ)
            with dve.Fori(1, ROUNDS) as r:
                with dve.If(most > r * CAP):
                    dve.wait_ge(sem("gathered"), r * (NE + 1))
                    V.tensor_scalar(posm, posm, float(-CAP), None, ALU.add).then_inc(sem("shifted"), 1)
                    dve.wait_ge(sem("shifted"), r)
                    select(0, 0)
                    with dve.Fori(0, PAIRS) as ip:
                        pair(r, r * PAIRS + ip, ip)
            V.memset(cmax, 0.0).then_inc(sem("result_ready"), 1)


NBC = 2 + 8 + 2 + 2 + 1 + 1 + 1 + 2 + 2


_INS = ['x', 'attn_norm_g', 'w_in', 'nsa_q_norm_g', 'nsa_kc_norm_g', 'nsa_ks_norm_g', 'nsa_kw_norm_g',
        'cmp_k_pos', 'cmp_k_w1', 'cmp_k_b1', 'cmp_k_w2', 'cmp_k_b2', 'cmp_v_pos', 'cmp_v_w1', 'cmp_v_b1',
        'cmp_v_w2', 'cmp_v_b2', 'nsa_out_norm_g', 'gdn_conv_w', 'gdn_a_log', 'gdn_dt_bias', 'gdn_out_norm_g',
        'w_out', 'ffn_norm_g', 'router_w', 'router_b', 'exp_w_gate', 'exp_b_gate', 'exp_w_up', 'exp_b_up',
        'exp_w_down', 'exp_b_down']


def const_table():
    import numpy as np
    c = np.zeros((P, C_END), np.float32)
    i, j = np.arange(P)[:, None], np.arange(P)[None, :]
    c[:, C_ID:C_ID + P] = i == j
    c[:, C_ONE:C_ONE + P] = 1.0
    c[:, C_TRI:C_TRI + P] = i <= j
    c[:, C_STR:C_STR + P] = i < j
    c[:, C_CM + P:C_CM + 2 * P] = np.where(j <= i, 0.0, -BIG)
    c[:, C_DM:C_DM + P] = np.where(i <= j, 0.0, -BIG)
    for lv in range(1, LEVELS):
        b = 1 << lv
        c[:, C_LV + (lv - 1) * P:C_LV + lv * P] = ((i // b) % 2 == 1) & (j // b == i // b - 1)
    c[:, C_M0:C_M0 + P] = (j % 2 == 1) & (i == j - 1)
    blk = np.arange(16)[None, :]
    for t in range(T2):
        seen = (blk < NCMP) & (16 * blk + 31 <= t * P + np.arange(P)[:, None])
        c[:, C_CA + 16 * t:C_CA + 16 * t + 16] = np.where(seen, 0.0, -BIG)
        c[:, C_CX + 16 * t:C_CX + 16 * t + 16] = seen
    c[:, C_IO:C_IO + CAP] = np.arange(CAP)[None, :]
    return c


def kernel(**inputs):
    import numpy as _np
    import concourse.bacc as _bacc
    from concourse import mybir as _mybir
    from concourse.bass_utils import run_bass_kernel_spmd as _run

    nc = _bacc.Bacc("TRN2", target_bir_lowering=False, num_devices=1)
    arrays, aps = {}, {}
    for name in _INS + ["const_table"]:
        v = const_table() if name == "const_table" else _np.ascontiguousarray(inputs[name])
        arrays[f"in_{name}_dram"] = v
        aps[name] = nc.dram_tensor(f"in_{name}_dram", v.shape, _mybir.dt.from_np(v.dtype), kind="ExternalInput").ap()
    out = nc.dram_tensor("out_0_dram", (1, SEQ, D), _mybir.dt.from_np(_np.dtype("float32")), kind="ExternalOutput").ap()
    hybrid_block(nc, aps, out)
    r = _run(nc, [arrays], core_ids=[0])
    return r.results[0]["out_0_dram"]
```

```python
from contextlib import ExitStack

import concourse.bass as bass
from concourse import mybir

F32 = mybir.dt.float32
I32 = mybir.dt.int32
ACT = mybir.ActivationFunctionType
ALU = mybir.AluOpType
AX = mybir.AxisListType

P = 128
SEQ = 256
D = 1024
T2 = SEQ // P
KC = D // P
EPS = 1e-6
BIG = 1e30
DH = 64
NE = 32
CAP = 64
ROUNDS = SEQ // CAP
SLOTS = 4
PAIRS = NE // 2
HD = 128
LEVELS = 7
NCMP = 15

C_ID = 0
C_ONE = C_ID + P
C_TRI = C_ONE + P
C_STR = C_TRI + P
C_CM = C_STR + P
C_DM = C_CM + 2 * P
C_LV = C_DM + P
C_M0 = C_LV + (LEVELS - 1) * P
C_CA = C_M0 + P
C_CX = C_CA + 2 * 16
C_IO = C_CX + 2 * 16
C_END = C_IO + CAP

V_CONV = 0
V_OUTG = 48
V_POS = 52
V_FG = 84
V_END = 92

B_G12 = 0
B_KCG = B_G12 + 12 * DH
B_GDN = B_KCG + DH
B_RB = B_GDN + HD
B_AL = B_RB + NE
B_DT = B_AL + 4
B_B1 = B_DT + 4
B_B2 = B_B1 + 256
B_END = B_B2 + 2 * DH

SLABS = ["c", "b", "a", "q1", "q0", "q2", "z", "w1k", "w1v", "wo_nsa", "wo_gdn"]
PIECES = {"c": 2, "wo_nsa": 2}
QKV = [2, 3, 0, 1, 4, 5]
LAST_USER = {("qkv", 1): "q0", ("qkv", 3): "q1", ("qkv", 5): "q2", ("uc", 1): "c", ("ub", 1): "b", ("ua", 1): "a",
             ("uz", 1): "z", ("hid",): "w1v", ("yg", 1, 1): "wo_gdn", ("yn", 1, 1): "wo_nsa"}


def slab_plan():
    uses, landed, plan = [0] * SLOTS, [0] * SLOTS, {}
    for i, name in enumerate(SLABS):
        s = i % SLOTS
        landed[s] += 16 * PIECES.get(name, 1)
        plan[name] = (s, landed[s], uses[s])
        uses[s] += 1
    return plan, uses, landed


def expert_plan():
    count, out = [0] * SLOTS, []
    for q in range(12):
        s = (len(SLABS) + q) % SLOTS
        out.append((s, count[s]))
        count[s] += 1
    assert count == [3] * SLOTS
    return out


def attn_steps():
    return [(t, b, g) for t in range(T2) for b in range(2) for g in range(2)]


PROJ = [("qkv", i) for i in QKV[1:]] + [("uz", t) for t in range(T2)]


def pe_front_order():
    j = [("hT", t, i) for t in range(T2) for i in range(2)] + [("vecT",)]
    j += [("uc", t) for t in range(T2)] + [("ub", t) for t in range(T2)]
    j += [("gc",)] + [("gb", t) for t in range(T2)]
    j += [("ua", t) for t in range(T2)] + [("qkv", QKV[0]), ("qT", 0), ("kT", 0)]
    for i, (t, b, g) in enumerate(attn_steps()):
        if i == 3:
            j += [("nat", 0, 1), ("nat", 1, 1), ("qT", 1), ("kT", 1)]
        elif i == 5:
            j += [("xT", 0, 1), ("xT", 1, 1), ("kk", 0), ("kk", 1), ("nat", 0, 0), ("nat", 1, 0)]
        elif i == 7:
            j += [("xT", 0, 0), ("xT", 1, 0), ("qk", 0), ("qk", 1), ("nat", 0, 2), ("nat", 1, 2), ("T0", 0), ("T0", 1)]
        if (b, g) == (0, 0):
            j += [("OT", t)]
        j += [("s", t, b, g, k) for k in range(2)]
        if i > 0:
            tt, bb, gg = attn_steps()[i - 1]
            j += [("pT", tt, bb, gg, s) for s in range(tt + 1)]
        if i < len(PROJ):
            j += [PROJ[i]]
    j += [("pT", 1, 1, 1, 0), ("pT", 1, 1, 1, 1), ("cmpT",)]
    fill = {1: [("hid",)], 2: [("hidT",)], 3: [("cmp2",), ("kcT",)], 4: [("sc", 0), ("sc", 1)], 5: [("pcT", 0)], 6: [("pcT", 1)]}
    for lv in range(1, LEVELS):
        for t in range(T2):
            j += [("P", lv, t)] + ([("UT", lv - 1, t)] if lv > 1 else [])
        j += fill[lv]
        for t in range(T2):
            j += [("TP" if lv < LEVELS - 1 else "PU", lv, t)]
    j += [("uv",), ("wT",), ("ss", 0), ("yn", 0, 0), ("s1",), ("ss", 1), ("yn", 0, 1), ("o", 0), ("v1",), ("yn", 1, 0),
          ("oT", 0), ("o", 1), ("yn", 1, 1), ("yg", 0, 0), ("yg", 0, 1), ("oT", 1), ("x2T", 0, 0), ("x2T", 0, 1),
          ("yg", 1, 0), ("yg", 1, 1), ("lg", 0), ("x2T", 1, 0), ("x2T", 1, 1), ("lg", 1), ("pos",)]
    return j


def bank_plan():
    used, plan, turn = [0] * 8, {}, 0
    for job in pe_front_order():
        if job[0] == "OT":
            b = 6 + job[1]
        else:
            b = turn % 6
            turn += 1
        plan[job] = (b, used[b])
        used[b] += 1
    return plan


def hybrid_block(nc, a, out):
    slab, front_uses, front_landed = slab_plan()
    chunks = expert_plan()
    bank = bank_plan()
    fulls, seen = {}, [0] * 8
    for job in pe_front_order():
        if job not in LAST_USER:
            seen[bank[job][0]] += 1
            fulls[job] = seen[bank[job][0]]

    ctx = ExitStack()
    with ctx:
        def sb(name, cols, dt=F32):
            return ctx.enter_context(nc.sbuf_tensor(name, [P, cols], dt))

        sems = {}

        def sem(name):
            if name not in sems:
                sems[name] = ctx.enter_context(nc.semaphore(name))
            return sems[name]

        ring = sb("ring", SLOTS * 4096)
        cst = sb("cst", C_END)
        bc = sb("bc", B_END)
        vT = sb("vT", V_END)
        w2 = sb("w2", 4 * DH)
        rw = sb("rw", KC * NE)
        btab = sb("btab", D)
        gain = sb("gain", D)
        x = sb("x", T2 * D)
        rA = sb("rA", 2048)
        rB = sb("rB", 2048)
        rC = sb("rC", 12 * (SEQ + 3))
        rD = sb("rD", 3072)
        vn = sb("vn", 1024)
        dec = sb("dec", 1024)
        kgd = sb("kgd", 1024)
        bst = sb("bst", 1024)
        scan = sb("scan", 2560)
        vec = scan[:, 0:P]
        nsa = sb("nsa", 8192)
        attn = sb("attn", 3072)
        st = sb("st", 600)
        cnt_i = sb("cnt_i", 1, I32)

        ident = cst[:, C_ID:C_ID + P]
        ones = cst[:, C_ONE:C_ONE + P]
        xt = x[:, :].rearrange("p (t d) -> p t d", t=T2)
        h = rA[:, :].rearrange("p (t d) -> p t d", t=T2)
        hT = rB[:, :].rearrange("p (c t) -> p c t", c=KC)
        cin = rC[:, :].rearrange("p (m t) -> p m t", m=12)
        cv = rD[:, :].rearrange("p (m t) -> p m t", m=12)
        qkn = rA[:, :].rearrange("p (t h d) -> p t h d", t=T2, h=8)
        qkT = rD[:, 0:2048].rearrange("p (h t) -> p h t", h=8)
        kg = kgd[:, 0:512].rearrange("p (h d) -> p h d", h=4)
        kd = kgd[:, 512:1024].rearrange("p (h d) -> p h d", h=4)
        invT = [rC[:, 512 * t:512 * t + 512].rearrange("p (h s) -> p h s", h=4) for t in range(T2)]
        invU = [rC[:, 1024 + 512 * t:1536 + 512 * t].rearrange("p (h s) -> p h s", h=4) for t in range(T2)]
        invP = [rC[:, 2048 + 512 * t:2560 + 512 * t].rearrange("p (h s) -> p h s", h=4) for t in range(T2)]
        v4 = vn[:, :].rearrange("p (t h d) -> p t h d", t=T2, h=4)
        dec4 = dec[:, :].rearrange("p (t h c) -> p t h c", t=T2, h=4)
        qkm4 = dec4
        Lm = [qkn[:, :, 0:4, :], qkn[:, :, 4:8, :]]
        bst4 = bst[:, :].rearrange("p (t h c) -> p t h c", t=T2, h=4)
        nwT = scan[:, 0:512].rearrange("p (h c) -> p h c", h=4)
        qg = scan[:, 512:1024].rearrange("p (h c) -> p h c", h=4)
        S1 = scan[:, 1024:1536].rearrange("p (h e) -> p h e", h=4)
        vnew = scan[:, 1536:2560].rearrange("p (t h e) -> p t h e", t=T2, h=4)
        og = rC[:, 0:1024].rearrange("p (t h c) -> p t h c", t=T2, h=4)
        osc = rC[:, 2048:3072].rearrange("p (t h c) -> p t h c", t=T2, h=4)
        mixT = rB[:, :].rearrange("p (k t) -> p k t", k=8)
        ub = nsa[:, 0:1024].rearrange("p (t n) -> p t n", t=T2)
        uc = nsa[:, 1024:1344].rearrange("p (t n) -> p t n", t=T2)
        nrm = nsa[:, 1344:2880].rearrange("p (t h d) -> p t h d", t=T2, h=12)
        z = nsa[:, 2880:3904].rearrange("p (t h d) -> p t h d", t=T2, h=4)
        qT = nsa[:, 3904:4928].rearrange("p (k t) -> p k t", k=4)
        kbd = nsa[:, 4928:6976].rearrange("p (b g q s) -> p b g q s", b=2, g=2, q=2)
        pcT = nsa[:, 6976:7488]
        vcb = nsa[:, 7488:7616]
        kcb = nsa[:, 7616:7680].rearrange("p (g q c) -> p g q c", g=2, q=2)
        pc = nsa[:, 7680:7936].rearrange("p (h g c) -> p h g c", h=4, g=2)
        smc = [nsa[:, 7936 + 128 * t:8064 + 128 * t].rearrange("p (h c) -> p h c", h=8) for t in range(T2)]
        pr = [attn[:, 1024 * i:1024 * i + 1024].rearrange("p (h s) -> p h s", h=4) for i in range(2)]
        pT = attn[:, 2048:3072].rearrange("p (s n) -> p s n", s=2)
        cx = attn[:, 0:2048].rearrange("p (v j n) -> p v j n", v=2, j=16)
        cz = attn[:, 2048:3072].rearrange("p (v g t) -> p v g t", v=2, g=2)
        hid = attn[:, 2048:2304]
        hidT = attn[:, 2304:2560].rearrange("p (j n) -> p j n", j=2)
        kv2 = attn[:, 2560:2688]
        kcn = attn[:, 2688:2752]
        oraw = attn[:, 0:1024].rearrange("p (t h n) -> p t h n", t=T2, h=4)
        osq = attn[:, 1024:2048].rearrange("p (t h n) -> p t h n", t=T2, h=4)
        pos_ = [0]

        def stat(n):
            pos_[0] += n
            assert pos_[0] <= 600
            return st[:, pos_[0] - n:pos_[0]]

        ssx, ssx2 = stat(T2), stat(T2)
        sc32 = stat(64).rearrange("p (t n) -> p t n", t=T2)
        gdt = stat(8).rearrange("p (t n) -> p t n", t=T2)
        gg = stat(8).rearrange("p (t n) -> p t n", t=T2)
        gcs = stat(8).rearrange("p (t n) -> p t n", t=T2)
        glast = stat(4)
        eal = stat(4)
        ssq = stat(16).rearrange("p (t n) -> p t n", t=T2)
        ssn = stat(24).rearrange("p (t n) -> p t n", t=T2)
        ssk = stat(1)
        sso = stat(8).rearrange("p (t n) -> p t n", t=T2)
        rsn = stat(T2)
        mx = [stat(4), stat(4)]
        den = [stat(4), stat(4)]
        mc, dc = stat(8), stat(8)
        lg = stat(64).rearrange("p (t n) -> p t n", t=T2)
        m8 = stat(16).rearrange("p (t n) -> p t n", t=T2)
        gt_ = stat(64).rearrange("p (t n) -> p t n", t=T2)
        eq_ = stat(64).rearrange("p (t n) -> p t n", t=T2)
        cum = stat(64).rearrange("p (t n) -> p t n", t=T2)
        need = stat(2)
        posm = stat(2 * (NE + 1)).rearrange("p (t n) -> p t n", t=T2)
        gates = stat(2 * (NE + 1)).rearrange("p (t n) -> p t n", t=T2)
        gsum = stat(2)
        cmax = stat(1)
        h2 = h
        x2T = hT
        m_hg = nsa[:, 0:512]
        m_hT = [nsa[:, 512:1024], nsa[:, 1024:1536]]
        m_g = nsa[:, 1536:2048]
        m_sg = nsa[:, 2048:2560]
        m_gs = nsa[:, 2560:3072]
        m_uc = nsa[:, 3072:3584]
        m_act = nsa[:, 3584:4096]
        m_aT = nsa[:, 4096:4608]
        m_y = nsa[:, 4608:5632]
        m_selw = nsa[:, 5632:5888].rearrange("p (t n) -> p t n", t=T2)
        m_selwT = nsa[:, 5888:6144].rearrange("p (t n) -> p t n", t=T2)
        m_sel = [nsa[:, 6144 + 128 * i:6272 + 128 * i].rearrange("p (t n) -> p t n", t=T2) for i in range(2)]
        m_eb = [nsa[:, 6400 + 192 * i:6592 + 192 * i].rearrange("p (w n) -> p w n", w=3) for i in range(2)]

        ps = [ctx.enter_context(nc.psum_tensor(f"bank{b}", [P, 512], F32)) for b in range(8)]
        bG, bU, bA, bT1, bT2, bD, bS0, bS1 = ps

        bank_full = [sem(f"bank_full{b}") for b in range(8)]
        bank_read = [sem(f"bank_read{b}") for b in range(8)]
        landed = [sem(f"slot_landed{s}") for s in range(SLOTS)]
        freed = [sem(f"slot_freed{s}") for s in range(SLOTS)]

        def ringv(s, **k):
            return ring[:, s * 4096:(s + 1) * 4096]

        def signal_of(job):
            if job in LAST_USER:
                s, _, uses = slab[LAST_USER[job]]
                return freed[s], uses + 1
            b = bank[job][0]
            return bank_full[b], fulls[job]

        def full(eng, job):
            eng.wait_ge(*signal_of(job))
            return ps[bank[job][0]]

        def read(ins, job):
            ins.then_inc(bank_read[bank[job][0]], 1)

        def copied(eng, job):
            b, n = bank[job]
            eng.wait_ge(bank_read[b], n + 1)

        def used(eng, it, q):
            s, k = chunks[q]
            eng.wait_ge(freed[s], it * 3 + (front_uses[s] + k + 1))

        def bcast(ap, shape):
            return ap.to_broadcast(shape)

        def two_heads(ap):
            return ap.rearrange("p a b -> p (a b)")

        w_in = a["w_in"][0]
        wi = w_in.rearrange("(c p) n -> p c n", p=P)
        w_out = a["w_out"][0]
        wexp = [a[n][0].rearrange("e (h c p) f -> e h p c f", h=2, p=P)
                for n in ("exp_w_gate", "exp_w_up", "exp_w_down")]

        block = ctx.enter_context(nc.Block())

        @block.sync
        def _(sp):
            cols = {"q0": 1304, "q1": 1816, "q2": 2328, "b": 512, "a": 0, "z": 2840}

            def load(name):
                s, _, uses = slab[name]
                if uses > 0:
                    sp.wait_ge(freed[s], uses)
                dst = ringv(s)
                v = dst.rearrange("p (c n) -> p c n", c=KC)
                if name in cols:
                    sp.dma_start(v, wi[:, :, cols[name]:cols[name] + 512]).then_inc(landed[s], 16)
                elif name == "c":
                    sp.dma_start(v[:, :, 0:280], wi[:, :, 1024:1304]).then_inc(landed[s], 16)
                    sp.dma_start(v[:, :, 280:288], wi[:, :, 3352:3360]).then_inc(landed[s], 16)
                elif name in ("w1k", "w1v"):
                    src = a["cmp_k_w1" if name == "w1k" else "cmp_v_w1"][0]
                    sp.dma_start(dst.rearrange("p (j n) -> p j n", j=16),
                                 src.rearrange("(j p) n -> p j n", p=P)).then_inc(landed[s], 16)
                elif name == "wo_gdn":
                    sp.dma_start(dst.rearrange("p (k n) -> p k n", k=4),
                                 w_out[512:1024, :].rearrange("(k p) n -> p k n", p=P)).then_inc(landed[s], 16)
                else:
                    v = w_out[0:512, :].rearrange("(g k d) n -> g d k n", g=2, k=4)
                    for g in range(2):
                        sp.dma_start(dst[64 * g:64 * g + 64, :].rearrange("p (k n) -> p k n", k=4),
                                     v[g]).then_inc(landed[s], 16)

            def row(lo, n, name, rep=1, part=(0, P)):
                dst = bc[part[0]:part[0] + part[1], lo:lo + rep * n].rearrange("p (r n) -> p r n", r=rep)
                src = a[name][0].partition_broadcast(part[1]).unsqueeze(1)
                sp.dma_start(dst, src.to_broadcast([part[1], rep, n])).then_inc(sem("bc_landed"), 16)

            xi = a["x"][0].rearrange("(t p) d -> t p d", p=P)
            sp.dma_start(xt[:, 0, :], xi[0]).then_inc(sem("x0_landed"), 16)
            sp.dma_start(gain[:, :], a["attn_norm_g"][0].partition_broadcast(P)).then_inc(sem("gain_landed"), 16)
            sp.dma_start(xt[:, 1, :], xi[1]).then_inc(sem("x1_landed"), 16)
            sp.dma_start(cst[:, :], a["const_table"]).then_inc(sem("const_landed"), 16)
            load("c")
            row(B_DT, 4, "gdn_dt_bias")
            row(B_AL, 4, "gdn_a_log")
            load("b")
            sp.dma_start(vec[V_CONV:V_CONV + 48, :],
                         a["gdn_conv_w"][0].rearrange("j (m p) -> (j m) p", p=P)).then_inc(sem("vec_landed"), 16)
            sp.dma_start(vec[V_OUTG:V_OUTG + 4, :].rearrange("k (g d) -> k g d", g=2),
                         a["nsa_out_norm_g"][0].rearrange("(g k d) -> k g d", g=2, k=4)).then_inc(sem("vec_landed"), 16)
            for v, nm in enumerate(("cmp_k_pos", "cmp_v_pos")):
                sp.dma_start(vec[V_POS + 16 * v:V_POS + 16 * v + 16, :].rearrange("j (i d) -> j i d", i=2),
                             a[nm][0].rearrange("(j i) d -> j i d", i=2)).then_inc(sem("vec_landed"), 16)
            sp.dma_start(vec[V_FG:V_FG + 8, :],
                         a["ffn_norm_g"][0].rearrange("(c p) -> c p", p=P)).then_inc(sem("vec_landed"), 16)
            load("a")
            row(B_G12, DH, "nsa_q_norm_g", rep=8)
            row(B_G12 + 8 * DH, DH, "nsa_ks_norm_g", rep=2)
            row(B_G12 + 10 * DH, DH, "nsa_kw_norm_g", rep=2)
            load("q1")
            row(B_KCG, DH, "nsa_kc_norm_g")
            row(B_GDN, HD, "gdn_out_norm_g")
            row(B_RB, NE, "router_b")
            row(B_B1, 256, "cmp_k_b1", part=(0, 64))
            row(B_B1, 256, "cmp_v_b1", part=(64, 64))
            row(B_B2, DH, "cmp_k_b2")
            row(B_B2 + DH, DH, "cmp_v_b2")
            load("q0")
            for v, nm in enumerate(("cmp_k_w2", "cmp_v_w2")):
                sp.dma_start(w2[:, 2 * v * DH:2 * (v + 1) * DH].rearrange("p (j n) -> p j n", j=2),
                             a[nm][0].rearrange("(j p) n -> p j n", p=P)).then_inc(sem("w2_landed"), 16)
            sp.dma_start(rw[:, :].rearrange("p (c n) -> p c n", c=KC),
                         a["router_w"][0].rearrange("(c p) n -> p c n", p=P)).then_inc(sem("rw_landed"), 16)
            for i, nm in enumerate(("exp_b_gate", "exp_b_down", "exp_b_up")):
                sp.dma_start(btab[NE * i:NE * (i + 1), :], a[nm][0]).then_inc(sem("btab_landed"), 16)
            sp.wait_ge(sem("h_ready"), T2)
            sp.dma_start(gain[:, :], a["ffn_norm_g"][0].partition_broadcast(P)).then_inc(sem("gain2_landed"), 16)
            for name in SLABS[5:]:
                load(name)

            def pair(it, ip):
                for q in range(12):
                    s, k = chunks[q]
                    par, j = q // 6, q % 6
                    sp.wait_ge(freed[s], it * 3 + (front_uses[s] + k))
                    sp.dma_start(ringv(s).rearrange("p (c f) -> p c f", c=4),
                                 wexp[j // 2][ip * 2 + par, j % 2]).then_inc(landed[s], 16)

            with sp.Fori(0, PAIRS) as ip:
                pair(ip, ip)
            sp.wait_ge(sem("counts_ready"), 1)
            most = sp.value_load(cnt_i[0:1, 0:1], min_val=0, max_val=SEQ)
            with sp.Fori(1, ROUNDS) as r:
                with sp.If(most > r * CAP):
                    with sp.Fori(0, PAIRS) as ip:
                        pair(r * PAIRS + ip, ip)
            sp.wait_ge(sem("result_ready"), 1)
            sp.dma_start(out[0].rearrange("(t p) d -> p t d", p=P), xt).then_inc(sem("out_written"), 16)
            sp.wait_ge(sem("out_written"), 16)

        @block.tensor
        def _(pe):
            order = iter(pe_front_order())

            def take(job):
                nxt = next(order)
                assert nxt == job, (nxt, job)
                b, n = bank[job]
                if n > 0:
                    pe.wait_ge(bank_read[b], n)
                return ps[b]

            def done(ins, job):
                ins.then_inc(signal_of(job)[0], 1)

            pe.wait_ge(sem("const_landed"), 16)
            for t in range(T2):
                pe.wait_ge(sem("h_ready"), t + 1)
                for i in range(2):
                    o = take(("hT", t, i))
                    for c in range(4):
                        m = pe.transpose(o[:, c * P:(c + 1) * P], h[:, t, (4 * i + c) * P:(4 * i + c + 1) * P], ident)
                    done(m, ("hT", t, i))
            pe.wait_ge(sem("vec_landed"), 80)
            o = take(("vecT",))
            done(pe.transpose(o[:, 0:V_END], vec[0:V_END, :], ident[0:V_END, 0:V_END]), ("vecT",))

            def natural(job, t, name, n):
                s, val, _ = slab[name]
                w = ringv(s).rearrange("p (c n) -> p c n", c=KC)
                pe.wait_ge(landed[s], val)
                copied(pe, ("hT", t, 0)), copied(pe, ("hT", t, 1))
                o = take((job, t))
                for c in range(KC):
                    m = pe.matmul(o[:, 0:n], hT[:, c, t * P:(t + 1) * P], w[:, c, 0:n],
                                  start=(c == 0), stop=(c == KC - 1))
                done(m, (job, t))

            def qkv(i):
                s, val, _ = slab[f"q{i // 2}"]
                w = ringv(s).rearrange("p (c n) -> p c n", c=KC)
                pe.wait_ge(landed[s], val)
                o = take(("qkv", i))
                for u in range(2):
                    mc0 = (2 * i + u) % 4 * P
                    for c in range(KC):
                        m = pe.matmul(o[:, u * SEQ:(u + 1) * SEQ], w[:, c, mc0:mc0 + P], hT[:, c, :],
                                      start=(c == 0), stop=(c == KC - 1))
                done(m, ("qkv", i))

            def turn4(job, cols):
                o = take(job)
                for hd in range(4):
                    m = pe.transpose(o[:, hd * P:(hd + 1) * P], cols(hd), ident)
                done(m, job)

            def heads(job, lhs, rhs):
                o = take(job)
                for hd in range(4):
                    n = len(lhs)
                    for i in range(n):
                        m = pe.matmul(o[:, hd * P:(hd + 1) * P], lhs[i][:, hd, :], rhs[i][:, hd, :],
                                      start=(i == 0), stop=(i == n - 1))
                done(m, job)

            for name, sl, n in (("uc", "c", 288), ("ub", "b", 512)):
                for t in range(T2):
                    natural(name, t, sl, n)
            pe.wait_ge(sem("g_ready"), 1)
            o = take(("gc",))
            for t in range(T2):
                m = pe.matmul(o[:, 4 * t:4 * t + 4], cst[:, C_TRI:C_TRI + P], gg[:, t, :], start=True, stop=True)
            done(m, ("gc",))
            for t in range(T2):
                o = take(("gb", t))
                for hd in range(4):
                    m = pe.matmul(o[:, hd * P:(hd + 1) * P], bcast(gg[:, t, hd:hd + 1], [P, P]),
                                  cst[:, C_TRI:C_TRI + P], start=True, stop=True)
                done(m, ("gb", t))
            for t in range(T2):
                natural("ua", t, "a", 512)
            qkv(QKV[0])

            def turn_nsa(t):
                pe.wait_ge(sem("nrm_ready"), t + 1)
                turn4(("qT", t), lambda k: two_heads(nrm[:, t, 2 * k:2 * k + 2, :]))
                o = take(("kT", t))
                for b in range(2):
                    m = pe.transpose(o[:, b * P:(b + 1) * P], two_heads(nrm[:, t, 8 + 2 * b:10 + 2 * b, :]), ident)
                done(m, ("kT", t))

            def turn_nat(k):
                pe.wait_ge(sem("silu_ready"), 2 * (QKV.index(2 * k) // 2 + 1))
                for t in range(T2):
                    turn4(("nat", t, k), lambda hd: cv[:, 4 * k + hd, t * P:(t + 1) * P])

            def turn_qk(k):
                for t in range(T2):
                    pe.wait_ge(sem("kn_ready" if k else "qn_ready"), t + 1)
                    turn4(("xT", t, k), lambda hd: qkn[:, t, 4 * k + hd, :])

            def products(name, lo):
                for t in range(T2):
                    copied(pe, ("xT", t, 1 - (lo == 0)))
                    heads((name, t), [qkT[:, 4:8, t * P:(t + 1) * P]], [qkT[:, lo:lo + 4, t * P:(t + 1) * P]])

            steps = attn_steps()

            def turn_weights(i):
                t, b, g = steps[i]
                pe.wait_ge(sem("pr_ready"), i + 1)
                for s in range(t + 1):
                    turn4(("pT", t, b, g, s), lambda hh: pr[i % 2][:, hh, s * P:(s + 1) * P])

            def values(i):
                t, b, g = steps[i]
                for s in range(t + 1):
                    copied(pe, ("pT", t, b, g, s))
                    vals = (ub[:, s, 384 + DH * g:384 + DH * (g + 1)], uc[:, s, DH * g:DH * (g + 1)])[b]
                    m = pe.matmul(ps[6 + t][64 * g:64 * g + 64, :], vals, pT[:, s, :], start=((b, s) == (0, 0)),
                                  stop=False, skip_group_check=True)
                m.then_inc(sem("pT_used"), 1)

            turn_nsa(0)
            for i, (t, b, g) in enumerate(steps):
                if i == 3:
                    turn_nat(1)
                    turn_nsa(1)
                elif i == 5:
                    turn_qk(1)
                    products("kk", 4)
                    turn_nat(0)
                elif i == 7:
                    turn_qk(0)
                    products("qk", 0)
                    turn_nat(2)
                    for tt in range(T2):
                        pe.wait_ge(sem("U_ready"), tt + 1)
                        turn4(("T0", tt), lambda hd: invU[tt][:, hd, :])
                if (b, g) == (0, 0):
                    take(("OT", t))
                    copied(pe, ("qT", t)), copied(pe, ("kT", t))
                for k in range(2):
                    o = take(("s", t, b, g, k))
                    n = P * (t + 1)
                    m = pe.matmul(o[:, 0:2 * n], qT[:, 2 * g + k, t * P:(t + 1) * P], kbd[:, b, g, :, 0:n],
                                  start=True, stop=True)
                    done(m, ("s", t, b, g, k))
                if i > 0:
                    turn_weights(i - 1)
                if i < len(PROJ):
                    name, j = PROJ[i]
                    if name == "qkv":
                        qkv(j)
                    else:
                        natural("uz", j, "z", 512)
                if i > 0:
                    values(i - 1)
            turn_weights(len(steps) - 1)
            o = take(("cmpT",))
            for v in range(2):
                for t in range(T2):
                    m = pe.transpose(o[:, v * SEQ + t * P:v * SEQ + (t + 1) * P], ub[:, t, v * P:(v + 1) * P], ident)
            done(m, ("cmpT",))
            values(len(steps) - 1)

            def cmp_hidden():
                pe.wait_ge(sem("cx_ready"), 1)
                (sk, vk, _), (sv, vv, _) = slab["w1k"], slab["w1v"]
                pe.wait_ge(landed[sk], vk)
                pe.wait_ge(landed[sv], vv)
                o = take(("hid",))
                for j in range(16):
                    for v, s in ((0, sk), (1, sv)):
                        m = pe.matmul(o[64 * v:64 * v + 64, 0:256], cx[:, v, j, :],
                                      ringv(s).rearrange("p (j n) -> p j n", j=16)[:, j, :],
                                      start=(j == 0), stop=(j == 15), skip_group_check=True)
                        if (v, j) == (0, 15):
                            m.then_inc(freed[sk], 1)
                done(m, ("hid",))

            def cmp_hidden_turned():
                pe.wait_ge(sem("hid_ready"), 1)
                o = take(("hidT",))
                for j in range(2):
                    m = pe.transpose(o[:, j * P:(j + 1) * P], hid[:, j * P:(j + 1) * P], ident)
                done(m, ("hidT",))

            def cmp_output():
                copied(pe, ("hidT",))
                pe.wait_ge(sem("w2_landed"), 32)
                o = take(("cmp2",))
                for v in range(2):
                    for j in range(2):
                        m = pe.matmul(o[0:64, v * DH:(v + 1) * DH], hidT[:, j, 64 * v:64 * v + 64],
                                      w2[:, (2 * v + j) * DH:(2 * v + j + 1) * DH], start=(j == 0), stop=(j == 1))
                done(m, ("cmp2",))

            def cmp_keys_turned():
                pe.wait_ge(sem("kcn_ready"), 1)
                o = take(("kcT",))
                done(pe.transpose(o[0:64, 0:64], kcn[0:64, :], ident[0:64, 0:64]), ("kcT",))

            def cmp_scores(t):
                copied(pe, ("kcT",))
                o = take(("sc", t))
                for k in range(4):
                    m = pe.matmul(o[:, 32 * k:32 * k + 32], qT[:, k, t * P:(t + 1) * P], kcb[:, k // 2, :, :],
                                  start=True, stop=True)
                done(m, ("sc", t))

            def cmp_weights(t):
                pe.wait_ge(sem("pc_ready"), t + 1)
                o = take(("pcT", t))
                for k in range(4):
                    m = pe.transpose(o[0:64, k * P:(k + 1) * P], two_heads(pc[:, k, :, :]), ident)
                done(m, ("pcT", t))

            def cmp_values(t):
                copied(pe, ("pcT", t))
                pe.wait_ge(sem("vc_ready"), 1)
                done(pe.matmul(ps[6 + t][:, :], vcb[0:64, :], pcT[0:64, :], start=False, stop=True,
                               skip_group_check=True), ("OT", t))

            for lv in range(1, LEVELS):
                for t in range(T2):
                    copied(pe, ("T0", t) if lv == 1 else ("TP", lv - 1, t))
                    pe.wait_ge(sem("Lm_ready"), 2 * (lv - 1) + t + 1)
                    heads(("P", lv, t), [Lm[lv % 2][:, t]], [invT[t]])
                    if lv > 1:
                        turn4(("UT", lv - 1, t), lambda hd: invT[t][:, hd, :])
                if lv == 1:
                    cmp_hidden()
                elif lv == 2:
                    cmp_hidden_turned()
                elif lv == 3:
                    cmp_output()
                    cmp_keys_turned()
                elif lv == 4:
                    cmp_scores(0)
                    cmp_scores(1)
                elif lv == 5:
                    cmp_weights(0)
                elif lv == 6:
                    cmp_values(0)
                    cmp_weights(1)
                for t in range(T2):
                    copied(pe, ("P", lv, t))
                    if lv > 1:
                        copied(pe, ("UT", lv - 1, t))
                    if lv < LEVELS - 1:
                        heads(("TP", lv, t), [invU[t]], [invP[t]])
                    else:
                        heads(("PU", lv, t), [invP[t]], [invU[t]])
            cmp_values(1)

            def token_norm(t):
                pe.wait_ge(sem("osq_ready"), t + 1)
                o = take(("ss", t))
                for k in range(4):
                    m = pe.matmul(o[:, 0:1], osq[:, t, k, :], ones[:, 0:1], start=(k == 0), stop=(k == 3))
                done(m, ("ss", t))

            def project(name, t, n):
                lo, sl = {"yg": (4, "wo_gdn"), "yn": (0, "wo_nsa")}[name]
                s, val, _ = slab[sl]
                w = ringv(s).rearrange("p (k n) -> p k n", k=4)
                pe.wait_ge(landed[s], val)
                if lo:
                    copied(pe, ("oT", t))
                else:
                    pe.wait_ge(sem("mixn_ready"), t + 1)
                o = take((name, t, n))
                for k in range(4):
                    m = pe.matmul(o[:, :], mixT[:, lo + k, t * P:(t + 1) * P], w[:, k, n * 512:(n + 1) * 512],
                                  start=(k == 0), stop=(k == 3))
                done(m, (name, t, n))

            def turn_gdn(t):
                pe.wait_ge(sem("og_ready"), t + 1)
                turn4(("oT", t), lambda hd: og[:, t, hd, :])

            def turn_x2(t, i):
                copied(pe, ("yg", t, i)), copied(pe, ("yn", t, i))
                turn4(("x2T", t, i), lambda c: xt[:, t, (4 * i + c) * P:(4 * i + c + 1) * P])

            def router(t):
                pe.wait_ge(sem("rw_ready"), 1)
                copied(pe, ("x2T", t, 0)), copied(pe, ("x2T", t, 1))
                o = take(("lg", t))
                for c in range(KC):
                    m = pe.matmul(o[:, 0:NE], x2T[:, c, t * P:(t + 1) * P], rw[:, c * NE:(c + 1) * NE],
                                  start=(c == 0), stop=(c == KC - 1))
                done(m, ("lg", t))

            copied(pe, ("PU", LEVELS - 1, 0))
            copied(pe, ("nat", 0, 2))
            heads(("uv",), [invU[0]], [v4[:, 0]])
            copied(pe, ("PU", LEVELS - 1, 1))
            heads(("wT",), [kg], [invU[1]])
            token_norm(0)
            project("yn", 0, 0)
            copied(pe, ("uv",))
            heads(("s1",), [kd], [vnew[:, 0]])
            token_norm(1)
            project("yn", 0, 1)
            copied(pe, ("qk", 0)), copied(pe, ("qk", 1))
            heads(("o", 0), [qkm4[:, 0]], [vnew[:, 0]])
            copied(pe, ("s1",)), copied(pe, ("wT",)), copied(pe, ("nat", 1, 2))
            heads(("v1",), [invU[1], nwT], [v4[:, 1], S1])
            project("yn", 1, 0)
            turn_gdn(0)
            pe.wait_ge(sem("qg_ready"), 1)
            copied(pe, ("v1",))
            heads(("o", 1), [qg, qkm4[:, 1]], [S1, vnew[:, 1]])
            project("yn", 1, 1)
            project("yg", 0, 0)
            project("yg", 0, 1)
            turn_gdn(1)
            turn_x2(0, 0)
            turn_x2(0, 1)
            project("yg", 1, 0)
            project("yg", 1, 1)
            router(0)
            turn_x2(1, 0)
            turn_x2(1, 1)
            router(1)
            pe.wait_ge(sem("mask_ready"), 1)
            o = take(("pos",))
            pe.matmul(o[:, 0:NE], cst[:, C_STR:C_STR + P], gt_[:, 0, :], start=True, stop=True)
            pe.matmul(o[:, NE:2 * NE], cst[:, C_STR:C_STR + P], gt_[:, 1, :], start=True, stop=False)
            pe.matmul(o[:, NE:2 * NE], ones, gt_[:, 0, :], start=False, stop=True)
            pe.matmul(o[:, 2 * NE:3 * NE], ones, gt_[:, 0, :], start=True, stop=False)
            done(pe.matmul(o[:, 2 * NE:3 * NE], ones, gt_[:, 1, :], start=False, stop=True), ("pos",))
            for b in range(8):
                pe.wait_ge(bank_read[b], max(n for bb, n in bank.values() if bb == b) + 1)
            pe.wait_ge(sem("h2_ready"), T2)
            pe.wait_ge(sem("btab_landed"), 48)
            pe.wait_ge(sem("btab_ready"), 1)

            def gather(buf, m, first=False):
                pe.wait_ge(sem("sel_ready"), m + 1)
                if not first:
                    pe.wait_ge(sem("hg_read"), m)
                for t in range(T2):
                    for hf in range(2):
                        i = pe.matmul(bA[64 * hf:64 * hf + 64, :], m_sel[buf][:, t, :], h2[:, t, 512 * hf:512 * hf + 512],
                                      start=(t == 0), stop=(t == 1), skip_group_check=True)
                i.then_inc(sem("gathered"), 1)

            def turn_rows(m, first=False):
                pe.wait_ge(sem("hg_read"), m + 1)
                if not first:
                    pe.wait_ge(sem("eT_read"), m)
                for j in range(4):
                    i = pe.transpose(bT1[:, j * P:(j + 1) * P], m_hg[:, j * P:(j + 1) * P], ident)
                i.then_inc(sem("rows_turned"), 1)

            def bias(o, buf, w):
                for fh in range(2):
                    pe.matmul(o[64 * fh:64 * fh + 64, :], m_eb[buf][:, w, :], btab[:, 512 * fh:512 * fh + 512],
                              start=True, stop=False, skip_group_check=True)

            def stream(o, it, q0, lhs):
                for q in (q0, q0 + 1):
                    s, k = chunks[q]
                    pe.wait_ge(landed[s], it * 48 + (front_landed[s] + 16 * (k + 1)))
                    w = ringv(s).rearrange("p (c f) -> p c f", c=4)
                    for c in range(4):
                        cc = (q - q0) * 4 + c
                        lt = lhs[:, (cc % 4) * P + (cc // 4) * CAP:(cc % 4) * P + (cc // 4) * CAP + CAP]
                        for fh in range(2):
                            i = pe.matmul(o[64 * fh:64 * fh + 64, :], lt, w[:, c, 512 * fh:512 * fh + 512],
                                          start=False, stop=(cc == 7), skip_group_check=True)
                            if fh == 1 and c == 3:
                                i.then_inc(freed[s], 1)
                return i

            def pair(r, it):
                for par in range(2):
                    n = it * 2 + par
                    m = n + r
                    pe.wait_ge(sem("eT_read"), m + 1)
                    for w, o in enumerate((bG, bU)):
                        bias(o, par, w)
                        stream(o, it, 6 * par + 2 * w, m_hT[par])
                    gather(1 - par, m + 1)
                    if par == 0:
                        pe.wait_ge(sem("selw_ready"), it + 1)
                        for t in range(T2):
                            i = pe.transpose(bS0[:, t * P:(t + 1) * P], m_selw[:, t, :], ident)
                        i.then_inc(sem("selw_turned"), 1)
                    pe.wait_ge(sem("act_ready"), n + 1)
                    for j in range(4):
                        i = pe.transpose(bT2[:, j * P:(j + 1) * P], m_act[:, j * P:(j + 1) * P], ident)
                    i.then_inc(sem("act_turned"), 1)
                    turn_rows(m + 1)
                    pe.wait_ge(sem("aT_read"), n + 1)
                    bias(bD, par, 2)
                    stream(bD, it, 6 * par + 4, m_aT)
                pe.wait_ge(sem("selwT_read"), it + 1)
                pe.wait_ge(sem("y_read"), it * 2 + 2)
                for t in range(T2):
                    for hf in range(2):
                        if t > 0:
                            pe.wait_ge(sem("added"), it * 4 + (hf + 1))
                        pe.matmul((bS0, bS1)[hf][:, :], m_selwT[:, t, :], m_y[:, 512 * hf:512 * hf + 512],
                                  start=True, stop=True).then_inc(sem("scattered"), 1)

            gather(0, 0, first=True)
            turn_rows(0, first=True)
            with pe.Fori(0, PAIRS) as ip:
                pair(0, ip)
            pe.wait_ge(sem("counts_ready"), 1)
            most = pe.value_load(cnt_i[0:1, 0:1], min_val=0, max_val=SEQ)
            with pe.Fori(1, ROUNDS) as r:
                with pe.If(most > r * CAP):
                    gather(0, r * (NE + 1))
                    turn_rows(r * (NE + 1))
                    with pe.Fori(0, PAIRS) as ip:
                        pair(r, r * PAIRS + ip)

        @block.scalar
        def _(act):
            nchain = [0]

            def link(ins):
                nchain[0] += 1
                ins.then_inc(sem("act_chain"), 1)
                act.wait_ge(sem("act_chain"), nchain[0])

            def act_(o, i, f, **k):
                return nc.scalar.activation(o, i, f, **k)

            def copy(o, i):
                return nc.scalar.activation(o, i, ACT.Copy)

            def root(ap, wait, sqrt, n=1):
                act.wait_ge(sem(wait), n)
                act_(ap, ap, ACT.Sqrt).then_inc(sem(sqrt), 1)

            def evac(job, dst, src):
                for d_, s_ in zip(dst, src):
                    ins = copy(d_, s_)
                read(ins, job)

            def evac4(job, dst):
                o = full(act, job)
                evac(job, [dst], [o[:, :].rearrange("p (h d) -> p h d", h=4)])

            for t in range(T2):
                act.wait_ge(sem(f"x{t}_landed"), 16)
                act_(h[:, t, :], xt[:, t, :], ACT.Square, accum_out=ssx[:, t:t + 1]).then_inc(sem("ssx_ready"), 1)
                root(ssx[:, t:t + 1], "msx_ready", "rms_ready", t + 1)
            for t in range(T2):
                evac4(("hT", t, 0), hT[:, 0:4, t * P:(t + 1) * P])
            o = full(act, ("vecT",))
            read(copy(vT[:, :], o[:, 0:V_END]), ("vecT",))
            for t in range(T2):
                o = full(act, ("uc", t))
                evac(("uc", t), [nrm[:, t, 10:12, :], uc[:, t, :]],
                     [o[:, 0:128].rearrange("p (h d) -> p h d", h=2), o[:, 128:288]])
            act.wait_ge(sem("sc_ready"), 1)
            act.wait_ge(sem("bc_landed"), 16 * NBC)
            link(act_(sc32, sc32, ACT.Exp))
            act_(eal, bc[:, B_AL:B_AL + 4], ACT.Exp).then_inc(sem("exp_ready"), 1)
            act.wait_ge(sem("sc1_ready"), 1)
            act_(gdt, sc32[:, :, 24:28], ACT.Ln).then_inc(sem("ln_ready"), 1)
            for t in range(T2):
                o = full(act, ("ub", t))
                evac(("ub", t), [nrm[:, t, 8:10, :], ub[:, t, :]],
                     [o[:, 256:384].rearrange("p (h d) -> p h d", h=2), o[:, :]])
            act.wait_ge(sem("gdiff_ready"), 1)
            act_(dec[:, :], dec[:, :], ACT.Exp)
            act_(qg, qg, ACT.Exp)
            act_(gcs[:, 1, :], gcs[:, 1, :], ACT.Exp)
            act_(glast, glast, ACT.Exp).then_inc(sem("decay_ready"), 1)

            def ev_qkv(i):
                o = full(act, ("qkv", i))
                evac(("qkv", i), [cin[:, 2 * i:2 * i + 2, 3:]], [o[:, :].rearrange("p (u t) -> p u t", u=2)])

            def silu(k):
                act.wait_ge(sem("conv_ready"), QKV.index(2 * k) + 2)
                for i in (2 * k, 2 * k + 1):
                    act_(cv[:, 2 * i:2 * i + 2, :], cv[:, 2 * i:2 * i + 2, :], ACT.Silu).then_inc(sem("silu_ready"), 1)

            def ev_nsa(t):
                o = full(act, ("qT", t))
                evac(("qT", t), [qT[:, :, t * P:(t + 1) * P]], [o[:, :].rearrange("p (k t) -> p k t", k=4)])
                act.wait_ge(sem("zeroed"), 1)
                o = full(act, ("kT", t))
                ov = o[:, 0:256].rearrange("p (b t) -> p b t", b=2)
                evac(("kT", t), [kbd[64 * p:64 * p + 64, :, g, p, t * P:(t + 1) * P] for g in range(2) for p in range(2)],
                     [ov[64 * g:64 * g + 64] for g in range(2) for p in range(2)])

            def ev_nat(k):
                for t in range(T2):
                    evac4(("nat", t, k), qkn[:, t, 4 * k:4 * k + 4, :] if k < 2 else v4[:, t])

            def ev_qk(k):
                for t in range(T2):
                    evac4(("xT", t, k), qkT[:, 4 * k:4 * k + 4, t * P:(t + 1) * P])

            steps = attn_steps()

            def ev_weights(i):
                t, b, g = steps[i]
                if i > 0:
                    act.wait_ge(sem("pT_used"), i)
                for s in range(t + 1):
                    o = full(act, ("pT", t, b, g, s))
                    evac(("pT", t, b, g, s), [pT[:, s, :]], [o[:, :]])

            for t in range(T2):
                o = full(act, ("ua", t))
                evac(("ua", t), [nrm[:, t, 0:8, :]], [o[:, :].rearrange("p (h d) -> p h d", h=8)])
                if t == 0:
                    root(ssn[:, 0, :], "ssn_ready", "sqn_ready")
            act.wait_ge(sem("cin_zeroed"), 1)
            ev_qkv(QKV[0])
            ev_nsa(0)
            root(ssn[:, 1, :], "ssn_ready", "sqn_ready", 2)
            for i, (t, b, g) in enumerate(steps):
                if i == 3:
                    ev_nat(1)
                    ev_nsa(1)
                elif i == 5:
                    ev_qk(1)
                    ev_nat(0)
                elif i == 7:
                    ev_qk(0)
                    ev_nat(2)
                    for tt in range(T2):
                        evac4(("T0", tt), invT[tt])
                if i > 0:
                    ev_weights(i - 1)
                n = P * (t + 1)
                act.wait_ge(sem("max_ready"), i + 1)
                for hh in range(4):
                    ins = act_(pr[i % 2][:, hh, 0:n], pr[i % 2][:, hh, 0:n], ACT.Exp,
                               bias=mx[i % 2][:, hh:hh + 1], accum_out=den[i % 2][:, hh:hh + 1])
                ins.then_inc(sem("exp_done"), 1)
                if i == 2:
                    silu(1)
                elif i == 4:
                    silu(0)
                elif i == 6:
                    silu(2)
                if i < len(PROJ):
                    name, j = PROJ[i]
                    if name == "qkv":
                        ev_qkv(j)
                    else:
                        o = full(act, ("uz", j))
                        read(act_(z[:, j], o[:, :].rearrange("p (h d) -> p h d", h=4), ACT.Silu), ("uz", j))
                if i == 3:
                    root(ssq[:, :, 4:8], "ssq_ready", "sqq_ready", 1)
                elif i == 5:
                    root(ssq[:, :, 0:4], "ssq_ready", "sqq_ready", 2)
            ev_weights(len(steps) - 1)

            def ev_OT(t):
                o = full(act, ("OT", t))
                evac(("OT", t), [oraw[:, t]], [o[:, :].rearrange("p (h n) -> p h n", h=4)])

            for lv in range(1, LEVELS):
                for t in range(T2):
                    evac4(("P", lv, t), invP[t])
                    if lv > 1:
                        evac4(("UT", lv - 1, t), invU[t])
                if lv == 1:
                    copied(act, ("hid",))
                    act_(hid, hid, ACT.Gelu_apprx_tanh).then_inc(sem("hid_ready"), 1)
                elif lv == 2:
                    o = full(act, ("hidT",))
                    evac(("hidT",), [hidT], [o[:, 0:256].rearrange("p (j n) -> p j n", j=2)])
                elif lv == 3:
                    root(ssk[0:64, :], "ssk_ready", "sqk_ready")
                    o = full(act, ("kcT",))
                    evac(("kcT",), [kcb[64 * p:64 * p + 64, g, p, :] for g in range(2) for p in range(2)],
                         [o[0:64, 32 * g:32 * g + 16] for g in range(2) for p in range(2)])
                elif lv == 4:
                    act.wait_ge(sem("smc_ready"), 1)
                    act_(smc[0], smc[0], ACT.Exp).then_inc(sem("ec_ready"), 1)
                elif lv == 5:
                    act.wait_ge(sem("smc_ready"), 2)
                    act_(smc[1], smc[1], ACT.Exp).then_inc(sem("ec_ready"), 1)
                    o = full(act, ("pcT", 0))
                    evac(("pcT", 0), [pcT[0:64, :]], [o[0:64, :]])
                elif lv == 6:
                    o = full(act, ("pcT", 1))
                    full(act, ("OT", 0))
                    evac(("pcT", 1), [pcT[0:64, :]], [o[0:64, :]])
                    ev_OT(0)
            ev_OT(1)
            o = full(act, ("wT",))
            read(nc.scalar.mul(nwT, o[:, :].rearrange("p (h d) -> p h d", h=4), -1.0), ("wT",))
            evac4(("s1",), S1)
            root(rsn[:, 0:1], "rsn_ready", "rsn_sqrt", 1)
            evac4(("o", 0), og[:, 0])
            root(sso[:, 0, :], "sso_ready", "sqo_ready", 1)
            root(rsn[:, 1:2], "rsn_ready", "rsn_sqrt", 2)
            evac4(("oT", 0), mixT[:, 4:8, 0:P])
            evac4(("o", 1), og[:, 1])
            root(sso[:, 1, :], "sso_ready", "sqo_ready", 2)
            for t in range(T2):
                if t:
                    evac4(("oT", 1), mixT[:, 4:8, P:2 * P])
                copied(act, ("yg", t, 1))
                act_(h2[:, t, :], xt[:, t, :], ACT.Square, accum_out=ssx2[:, t:t + 1]).then_inc(sem("ssx2_ready"), 1)
                for i in range(2):
                    evac4(("x2T", t, i), x2T[:, 4 * i:4 * i + 4, t * P:(t + 1) * P])
                    if i == 0:
                        root(ssx2[:, t:t + 1], "msx2_ready", "rms2_ready", t + 1)
            act.wait_ge(sem("lgm_ready"), 1)
            act_(lg, lg, ACT.Exp).then_inc(sem("lge_ready"), 1)

            def rows_out(m, first=False):
                act.wait_ge(sem("gathered"), m + 1)
                if not first:
                    act.wait_ge(sem("rows_turned"), m)
                copy(m_hg, bA[:, :]).then_inc(sem("hg_read"), 1)

            def turned_out(buf, m):
                act.wait_ge(sem("rows_turned"), m + 1)
                copy(m_hT[buf], bT1[:, :]).then_inc(sem("eT_read"), 1)

            def pair(r, it):
                for par in range(2):
                    n = it * 2 + par
                    m = n + r
                    act.wait_ge(sem("gate_read"), n + 1)
                    act_(m_sg, m_g, ACT.Sigmoid, scale=1.702).then_inc(sem("sg_ready"), 1)
                    rows_out(m + 1)
                    if par == 0:
                        act.wait_ge(sem("selw_turned"), it + 1)
                        copy(m_selwT, bS0[:, 0:256].rearrange("p (t n) -> p t n", t=T2)).then_inc(sem("selwT_read"), 1)
                    act.wait_ge(sem("act_turned"), n + 1)
                    copy(m_aT, bT2[:, :]).then_inc(sem("aT_read"), 1)
                    turned_out(1 - par, m + 1)
                    used(act, it, 6 * par + 5)
                    for hf in range(2):
                        i = copy(m_y[64 * par:64 * par + 64, 512 * hf:512 * hf + 512], bD[64 * hf:64 * hf + 64, :])
                    i.then_inc(sem("y_read"), 1)

            rows_out(0, first=True)
            turned_out(0, 0)
            with act.Fori(0, PAIRS) as ip:
                pair(0, ip)
            act.wait_ge(sem("counts_ready"), 1)
            most = act.value_load(cnt_i[0:1, 0:1], min_val=0, max_val=SEQ)
            with act.Fori(1, ROUNDS) as r:
                with act.If(most > r * CAP):
                    rows_out(r * (NE + 1))
                    turned_out(0, r * (NE + 1))
                    with act.Fori(0, PAIRS) as ip:
                        pair(r, r * PAIRS + ip)

        @block.gpsimd
        def _(pool):
            nchain = [0]

            def link(ins):
                nchain[0] += 1
                ins.then_inc(sem("pool_chain"), 1)
                pool.wait_ge(sem("pool_chain"), nchain[0])

            G = nc.gpsimd
            told = {}

            def link_as(ins, name):
                told[name] = told.get(name, 0) + 1
                ins.then_inc(sem(name), 1)
                pool.wait_ge(sem(name), told[name])

            link_as(G.memset(cin[:, :, 0:3], 0.0), "cin_zeroed")
            for v in (vcb, kcb, pc):
                link(G.memset(v, 0.0))
            link_as(G.memset(kbd, 0.0), "zeroed")
            link_as(G.memset(btab[96:128, :], 0.0), "btab_ready")
            pool.wait_ge(sem("rw_landed"), 16)
            copied(pool, ("vecT",))
            rw8 = rw[:, :].rearrange("p (c n) -> p c n", c=KC)
            link_as(G.tensor_tensor(rw8, rw8, bcast(vT[:, V_FG:V_FG + 8].unsqueeze(2), [P, KC, NE]), ALU.mult), "rw_ready")
            for lv in range(1, LEVELS):
                mask = bcast(cst[:, C_LV + (lv - 1) * P:C_LV + lv * P].unsqueeze(1), [P, 4, P])
                for t in range(T2):
                    if lv == 1:
                        copied(pool, ("kk", t))
                        pool.wait_ge(sem("kgd_ready"), 1)
                    elif lv == 2:
                        full(pool, ("xT", t, 0))
                    else:
                        full(pool, ("P", lv - 2, t))
                    link_as(G.tensor_tensor(Lm[lv % 2][:, t], bst4[:, t], mask, ALU.mult), "Lm_ready")
                if lv == 1:
                    full(pool, ("pT", 1, 1, 1, 1))
                    for g in range(2):
                        link(G.memset(cx[:, :, :, 32 * g + NCMP:32 * g + 32], 0.0))
                    pool.wait_ge(sem("pT_used"), len(attn_steps()))
                    link_as(G.memset(cz[64:128, :, :, SEQ - 1:SEQ], 0.0), "cx_zeroed")

        @block.vector
        def _(dve):
            nchain = [0]
            V = nc.vector

            def link(ins):
                nchain[0] += 1
                ins.then_inc(sem("dve_chain"), 1)
                dve.wait_ge(sem("dve_chain"), nchain[0])

            told = {}

            def link_as(ins, name):
                told[name] = told.get(name, 0) + 1
                ins.then_inc(sem(name), 1)
                dve.wait_ge(sem(name), told[name])

            def link_read(ins, job):
                read(ins, job)
                copied(dve, job)

            def rstd(ap, n, wait, sqrt):
                link_as(V.tensor_scalar(ap, ap, 1.0 / n, EPS, ALU.mult, ALU.add), wait)
                dve.wait_ge(sem(sqrt), told[wait])
                link(V.reciprocal(ap, ap))

            def h4(ap):
                return ap.rearrange("p (h s) -> p h s", h=4)

            for t in range(T2):
                dve.wait_ge(sem("ssx_ready"), t + 1)
                rstd(ssx[:, t:t + 1], D, "msx_ready", "rms_ready")
                dve.wait_ge(sem("gain_landed"), 16)
                link_as(V.scalar_tensor_tensor(out=h[:, t, :], in0=xt[:, t, :], scalar=ssx[:, t:t + 1], in1=gain[:, :],
                                               op0=ALU.mult, op1=ALU.mult), "h_ready")
            for t in range(T2):
                o = full(dve, ("hT", t, 1))
                read(V.tensor_copy(hT[:, 4:8, t * P:(t + 1) * P], h4(o[:, :])), ("hT", t, 1))

            def conv(i):
                copied(dve, ("qkv", i))
                for tap in range(4):
                    for u in range(2):
                        m = 2 * i + u
                        w = vT[:, V_CONV + 12 * tap + m:V_CONV + 12 * tap + m + 1]
                        src = cin[:, m, tap:tap + SEQ]
                        if tap == 0:
                            ins = V.tensor_scalar(cv[:, m, :], src, w, None, ALU.mult)
                        else:
                            ins = V.scalar_tensor_tensor(out=cv[:, m, :], in0=src, scalar=w, in1=cv[:, m, :],
                                                         op0=ALU.mult, op1=ALU.add)
                    if tap < 3:
                        link(ins)
                    else:
                        link_as(ins, "conv_ready")

            copied(dve, ("uc", 0)), copied(dve, ("uc", 1))
            dve.wait_ge(sem("bc_landed"), 16 * NBC)
            link(V.tensor_tensor(gdt, uc[:, :, 152:156], bcast(bc[:, B_DT:B_DT + 4].unsqueeze(1), [P, T2, 4]), ALU.add))
            V.tensor_scalar(sc32[:, :, 0:24], uc[:, :, 128:152], -1.0, None, ALU.mult)
            V.tensor_scalar(sc32[:, :, 28:32], uc[:, :, 156:160], -1.0, None, ALU.mult)
            link(V.scalar_tensor_tensor(out=sc32[:, :, 24:28], in0=gdt, scalar=-1.0, in1=gdt, op0=ALU.mult, op1=ALU.min))
            link_as(V.tensor_scalar(gg, gdt, 0.0, None, ALU.max), "sc_ready")
            dve.wait_ge(sem("exp_ready"), 1)
            link_as(V.tensor_scalar(sc32, sc32, 1.0, None, ALU.add), "sc1_ready")
            dve.wait_ge(sem("ln_ready"), 1)
            link(V.tensor_tensor(gg, gg, gdt, ALU.add))
            link_as(V.scalar_tensor_tensor(out=gg, in0=gg, scalar=-1.0, in1=bcast(eal.unsqueeze(1), [P, T2, 4]),
                                        op0=ALU.mult, op1=ALU.mult), "g_ready")
            link(V.reciprocal(sc32, sc32))
            for t in range(T2):
                link(V.tensor_copy(bst4[:, t], bcast(sc32[:, t, 28:32].unsqueeze(2), [P, 4, P])))
                link(V.tensor_tensor(bst4[:, t], bst4[:, t],
                                     bcast(cst[:, C_STR:C_STR + P].unsqueeze(1), [P, 4, P]), ALU.mult))
            o = full(dve, ("gc",))
            link_read(V.tensor_copy(gcs, o[:, 0:8].rearrange("p (t n) -> p t n", t=T2)), ("gc",))
            for t in range(T2):
                o = full(dve, ("gb", t))
                ov = h4(o[:, :])
                if t == 0:
                    V.tensor_copy(glast, ov[:, :, P - 1])
                else:
                    V.tensor_copy(qg, ov)
                link_read(V.tensor_tensor(dec4[:, t], ov, bcast(cst[:, C_DM:C_DM + P].unsqueeze(1), [P, 4, P]), ALU.add), ("gb", t))
                link(V.tensor_tensor(dec4[:, t], dec4[:, t], bcast(gcs[:, t, :].unsqueeze(2), [P, 4, P]), ALU.subtract))
            link_as(V.tensor_tensor(glast, glast, gcs[:, 0, :], ALU.subtract), "gdiff_ready")
            dve.wait_ge(sem("decay_ready"), 1)
            for t in range(T2):
                link(V.tensor_tensor(bst4[:, t], bst4[:, t], dec4[:, t], ALU.mult))

            def nsa_norm(t):
                sq = scan[:, 1536:1536 + 768].rearrange("p (h d) -> p h d", h=12)
                copied(dve, ("ua", t))
                link(V.tensor_tensor(sq, nrm[:, t], nrm[:, t], ALU.mult))
                link(V.tensor_reduce(ssn[:, t, :], sq, AX.X, ALU.add))
                rstd(ssn[:, t, :], DH, "ssn_ready", "sqn_ready")
                link(V.tensor_tensor(nrm[:, t], nrm[:, t], bcast(ssn[:, t, :].unsqueeze(2), [P, 12, DH]), ALU.mult))
                link_as(V.tensor_tensor(nrm[:, t], nrm[:, t],
                                        bc[:, B_G12:B_G12 + 768].rearrange("p (h d) -> p h d", h=12), ALU.mult), "nrm_ready")

            def l2_squares(k):
                sq = scan[:, 1536:2560].rearrange("p (t h d) -> p t h d", t=T2, h=4)
                part = qkn[:, :, 4 * k:4 * k + 4, :]
                copied(dve, ("nat", 0, k)), copied(dve, ("nat", 1, k))
                link(V.tensor_tensor(sq, part, part, ALU.mult))
                s_ = ssq[:, :, 4 * k:4 * k + 4]
                link(V.tensor_reduce(s_, sq, AX.X, ALU.add))
                c = 1.0 if k else float(HD)
                link_as(V.tensor_scalar(s_, s_, c, c * EPS, ALU.mult, ALU.add), "ssq_ready")

            def l2_scale(k):
                s_ = ssq[:, :, 4 * k:4 * k + 4]
                dve.wait_ge(sem("sqq_ready"), told["ssq_ready"])
                link(V.reciprocal(s_, s_))
                for t in range(T2):
                    part = qkn[:, t, 4 * k:4 * k + 4, :]
                    link_as(V.tensor_tensor(part, part, bcast(s_[:, t, :].unsqueeze(2), [P, 4, HD]), ALU.mult),
                            "kn_ready" if k else "qn_ready")

            def gate(t, b):
                return sc32[:, t, 0:24].rearrange("p (h b) -> p h b", b=3)[:, :, b]

            steps = attn_steps()

            def step_scores(i):
                t, b, g = steps[i]
                n = P * (t + 1)
                p_ = pr[i % 2]
                if i > 1:
                    tt, bb, gg_ = steps[i - 2]
                    full(dve, ("pT", tt, bb, gg_, tt))
                mask = cst[:, C_CM + 2 * P - n:C_CM + 2 * P]
                for k in range(2):
                    o = full(dve, ("s", t, b, g, k))
                    link_read(V.scalar_tensor_tensor(out=p_[:, 2 * k:2 * k + 2, 0:n],
                                                     in0=o[:, 0:2 * n].rearrange("p (q s) -> p q s", q=2),
                                                     scalar=DH ** -0.5, in1=bcast(mask.unsqueeze(1), [P, 2, n]),
                                                     op0=ALU.mult, op1=ALU.add), ("s", t, b, g, k))
                link(V.tensor_reduce(mx[i % 2], p_[:, :, 0:n], AX.X, ALU.max))
                link_as(V.tensor_scalar(mx[i % 2], mx[i % 2], -1.0, None, ALU.mult), "max_ready")

            def step_weights(i):
                t, b, g = steps[i]
                n = P * (t + 1)
                p_, d_ = pr[i % 2], den[i % 2]
                dve.wait_ge(sem("exp_done"), i + 1)
                link(V.reciprocal(d_, d_))
                link(V.tensor_tensor(d_, d_, gate(t, 1 + b)[:, 4 * g:4 * g + 4], ALU.mult))
                link_as(V.tensor_tensor(p_[:, :, 0:n], p_[:, :, 0:n], bcast(d_.unsqueeze(2), [P, 4, n]), ALU.mult), "pr_ready")

            nsa_norm(0)
            for i in range(len(steps)):
                if i == 7:
                    for t in range(T2):
                        ov = h4(full(dve, ("qk", t))[:, :])
                        link_read(V.tensor_tensor(qkm4[:, t], ov, dec4[:, t], ALU.mult), ("qk", t))
                step_scores(i)
                if i < 6:
                    conv(QKV[i])
                if i == 0:
                    nsa_norm(1)
                elif i == 3:
                    l2_squares(1)
                elif i == 4:
                    l2_scale(1)
                    V.tensor_tensor(kg, qkn[:, 1, 4:8, :], bcast(gcs[:, 1, :].unsqueeze(2), [P, 4, HD]), ALU.mult)
                    link_as(V.tensor_tensor(kd, qkn[:, 0, 4:8, :], bcast(glast.unsqueeze(2), [P, 4, HD]), ALU.mult), "kgd_ready")
                elif i == 5:
                    for t in range(T2):
                        ov = h4(full(dve, ("kk", t))[:, :])
                        link_read(V.tensor_tensor(bst4[:, t], ov, bst4[:, t], ALU.mult), ("kk", t))
                    l2_squares(0)
                elif i == 6:
                    l2_scale(0)
                    for t in range(T2):
                        link(V.tensor_tensor(invP[t], bst4[:, t], bcast(cst[:, C_M0:C_M0 + P].unsqueeze(1), [P, 4, P]), ALU.mult))
                        link_as(V.tensor_tensor(invU[t], bcast(ident.unsqueeze(1), [P, 4, P]), invP[t], ALU.subtract), "U_ready")
                step_weights(i)
            link_as(V.tensor_tensor(qg, qg, qkT[:, 0:4, P:2 * P], ALU.mult), "qg_ready")
            dve.wait_ge(sem("pT_used"), len(steps))
            dve.wait_ge(sem("cx_zeroed"), 1)
            o = full(dve, ("cmpT",))
            ov = o[:, :].rearrange("p (v t) -> p v t", v=2)
            for g in range(2):
                V.tensor_copy(cz[0:64, :, g, :], ov[64 * g:64 * g + 64])
                ins = V.tensor_copy(cz[64:128, :, g, 0:SEQ - 1], ov[64 * g:64 * g + 64, :, 1:SEQ])
            link_read(ins, ("cmpT",))
            for v in range(2):
                for g in range(2):
                    pairs = cz[:, v, g, :].rearrange("p (c j i) -> p j c i", j=8, i=2)[:, :, :, 0]
                    for u in range(2):
                        rows = vT[:, V_POS + 16 * v + 8 * u:V_POS + 16 * v + 8 * u + 8].unsqueeze(2)
                        ins = V.tensor_tensor(cx[:, v, 8 * u:8 * u + 8, 32 * g:32 * g + NCMP],
                                              pairs[:, :, u:u + NCMP], bcast(rows, [P, 8, NCMP]), ALU.add)
            link_as(ins, "cx_ready")

            def cmp_scores(t):
                ov = full(dve, ("sc", t))[:, 0:128].rearrange("p (h c) -> p h c", h=8)
                link_read(V.scalar_tensor_tensor(out=smc[t], in0=ov, scalar=DH ** -0.5,
                                                 in1=bcast(cst[:, C_CA + 16 * t:C_CA + 16 * t + 16].unsqueeze(1), [P, 8, 16]),
                                                 op0=ALU.mult, op1=ALU.add), ("sc", t))
                link(V.tensor_reduce(mc, smc[t], AX.X, ALU.max))
                link_as(V.tensor_tensor(smc[t], smc[t], bcast(mc.unsqueeze(2), [P, 8, 16]), ALU.subtract), "smc_ready")

            def cmp_weights(t):
                dve.wait_ge(sem("ec_ready"), t + 1)
                link(V.tensor_tensor(smc[t], smc[t], bcast(cst[:, C_CX + 16 * t:C_CX + 16 * t + 16].unsqueeze(1), [P, 8, 16]),
                                     ALU.mult))
                link(V.tensor_reduce(dc, smc[t], AX.X, ALU.add))
                link(V.tensor_scalar(dc, dc, 1e-30, None, ALU.max))
                link(V.reciprocal(dc, dc))
                link(V.tensor_tensor(dc, dc, gate(t, 0), ALU.mult))
                if t:
                    full(dve, ("pcT", t - 1))
                for g in range(2):
                    ins = V.tensor_tensor(pc[:, :, g, 0:16], smc[t][:, 4 * g:4 * g + 4, :],
                                          bcast(dc[:, 4 * g:4 * g + 4].unsqueeze(2), [P, 4, 16]), ALU.mult)
                link_as(ins, "pc_ready")

            def nsa_out(t):
                copied(dve, ("OT", t))
                link_as(V.tensor_tensor(osq[:, t], oraw[:, t], oraw[:, t], ALU.mult), "osq_ready")
                link_as(V.tensor_tensor(mixT[:, 0:4, t * P:(t + 1) * P], oraw[:, t],
                                        bcast(vT[:, V_OUTG:V_OUTG + 4].unsqueeze(2), [P, 4, P]), ALU.mult), "mixn_ready")

            for lv in range(1, LEVELS):
                if lv == 1:
                    o = full(dve, ("hid",))
                    link_read(V.tensor_tensor(hid, o[:, 0:256], bc[:, B_B1:B_B1 + 256], ALU.add), ("hid",))
                elif lv == 3:
                    o = full(dve, ("cmp2",))
                    link_read(V.tensor_tensor(kv2[0:64, :], o[0:64, 0:128], bc[0:64, B_B2:B_B2 + 128], ALU.add), ("cmp2",))
                    link(V.tensor_tensor(kcn[0:64, :], kv2[0:64, 0:64], kv2[0:64, 0:64], ALU.mult))
                    link(V.tensor_reduce(ssk[0:64, :], kcn[0:64, :], AX.X, ALU.add))
                    rstd(ssk[0:64, :], DH, "ssk_ready", "sqk_ready")
                    link_as(V.scalar_tensor_tensor(out=kcn[0:64, :], in0=kv2[0:64, 0:64], scalar=ssk[0:64, :],
                                                   in1=bc[0:64, B_KCG:B_KCG + DH], op0=ALU.mult, op1=ALU.mult), "kcn_ready")
                    for g in range(2):
                        ins = V.tensor_copy(vcb[32 * g:32 * g + 32, 64 * g:64 * g + 64], kv2[32 * g:32 * g + 32, 64:128])
                    link_as(ins, "vc_ready")
                for t in range(T2):
                    if lv < LEVELS - 1:
                        tp = h4(full(dve, ("TP", lv, t))[:, :])
                        link_read(V.tensor_tensor(invT[t], invT[t], tp, ALU.subtract), ("TP", lv, t))
                    else:
                        pu = h4(full(dve, ("PU", lv, t))[:, :])
                        link_read(V.tensor_tensor(invU[t], invU[t], pu, ALU.subtract), ("PU", lv, t))
                if lv == 4:
                    cmp_scores(0)
                    cmp_scores(1)
                    cmp_weights(0)
                elif lv == 5:
                    cmp_weights(1)

            def vnew_(t, job):
                ov = h4(full(dve, job)[:, :])
                link_read(V.tensor_tensor(vnew[:, t], ov, bcast(sc32[:, t, 28:32].unsqueeze(2), [P, 4, HD]), ALU.mult), job)

            def nsa_rstd(t):
                o = full(dve, ("ss", t))
                link_read(V.tensor_copy(rsn[:, t:t + 1], o[:, 0:1]), ("ss", t))
                rstd(rsn[:, t:t + 1], 512, "rsn_ready", "rsn_sqrt")

            def gdn_squares(t):
                copied(dve, ("o", t))
                link(V.tensor_tensor(osc[:, t], og[:, t], og[:, t], ALU.mult))
                link(V.tensor_reduce(sso[:, t, :], osc[:, t], AX.X, ALU.add))

            def gdn_out(t):
                rstd(sso[:, t, :], HD, "sso_ready", "sqo_ready")
                link(V.tensor_tensor(og[:, t], og[:, t], bcast(sso[:, t, :].unsqueeze(2), [P, 4, HD]), ALU.mult))
                link_as(V.tensor_tensor(og[:, t], og[:, t], z[:, t], ALU.mult), "og_ready")

            def add_nsa(t, n):
                o = full(dve, ("yn", t, n))
                xs = xt[:, t, n * 512:(n + 1) * 512]
                link_read(V.scalar_tensor_tensor(out=xs, in0=o[:, :], scalar=rsn[:, t:t + 1], in1=xs,
                                                 op0=ALU.mult, op1=ALU.add), ("yn", t, n))

            def add_gdn(t, n):
                o = full(dve, ("yg", t, n))
                xs = xt[:, t, n * 512:(n + 1) * 512]
                link_read(V.tensor_tensor(xs, xs, o[:, :], ALU.add), ("yg", t, n))

            def router(t):
                dve.wait_ge(sem("ssx2_ready"), t + 1)
                rstd(ssx2[:, t:t + 1], D, "msx2_ready", "rms2_ready")
                o = full(dve, ("lg", t))
                link_read(V.scalar_tensor_tensor(out=lg[:, t, :], in0=o[:, 0:NE], scalar=ssx2[:, t:t + 1],
                                                 in1=bc[:, B_RB:B_RB + NE], op0=ALU.mult, op1=ALU.add), ("lg", t))
                link(V.max(m8[:, t, :], lg[:, t, :]))

            def second_norm(t):
                dve.wait_ge(sem("gain2_landed"), 16)
                link_as(V.scalar_tensor_tensor(out=h2[:, t, :], in0=xt[:, t, :], scalar=ssx2[:, t:t + 1], in1=gain[:, :],
                                               op0=ALU.mult, op1=ALU.mult), "h2_ready")

            vnew_(0, ("uv",))
            nsa_out(0)
            nsa_out(1)
            for t in range(T2):
                link(V.tensor_tensor(z[:, t], z[:, t], bcast(bc[:, B_GDN:B_GDN + HD].unsqueeze(1), [P, 4, HD]), ALU.mult))
            nsa_rstd(0)
            add_nsa(0, 0)
            gdn_squares(0)
            vnew_(1, ("v1",))
            gdn_out(0)
            nsa_rstd(1)
            add_nsa(0, 1)
            add_nsa(1, 0)
            gdn_squares(1)
            gdn_out(1)
            add_nsa(1, 1)
            add_gdn(0, 0)
            add_gdn(0, 1)
            router(0)
            second_norm(0)
            add_gdn(1, 0)
            add_gdn(1, 1)
            router(1)
            thr = bcast(m8[:, :, 3:4], [P, T2, NE])
            link(V.tensor_tensor(gt_, lg, thr, ALU.is_gt))
            link(V.tensor_tensor(eq_, lg, thr, ALU.is_equal))
            link(V.tensor_reduce(need, gt_, AX.X, ALU.add))
            link(V.tensor_scalar(need, need, -1.0, 4.0, ALU.mult, ALU.add))
            for t in range(T2):
                link(V.tensor_tensor_scan(cum[:, t, :], ones[:, 0:NE], eq_[:, t, :], 0.0, ALU.mult, ALU.add))
            link(V.tensor_tensor(cum, cum, bcast(need.unsqueeze(2), [P, T2, NE]), ALU.is_le))
            link(V.tensor_tensor(eq_, eq_, cum, ALU.mult))
            link_as(V.tensor_tensor(gt_, gt_, eq_, ALU.add), "mask_ready")
            link_as(V.tensor_tensor(lg, lg, bcast(m8[:, :, 0:1], [P, T2, NE]), ALU.subtract), "lgm_ready")
            second_norm(1)
            link(V.memset(posm, 0.0))
            link(V.memset(gates, 0.0))
            o = full(dve, ("pos",))
            link(V.scalar_tensor_tensor(out=posm[:, :, 0:NE], in0=o[:, 0:64].rearrange("p (t n) -> p t n", t=T2),
                                        scalar=1.0, in1=gt_, op0=ALU.add, op1=ALU.mult))
            link_read(V.tensor_reduce(cmax, o[:, 64:96], AX.X, ALU.max), ("pos",))
            link(V.tensor_scalar(posm, posm, -1.0, None, ALU.add))

            iota = cst[:, C_IO:C_IO + CAP]

            def select(buf, e):
                for t in range(T2):
                    V.tensor_scalar(m_sel[buf][:, t, :], iota, posm[:, t, bass.ds(e, 1)], None, ALU.is_equal)
                V.tensor_copy(m_eb[buf][:, 0, :], bcast(ident[:, bass.ds(e, 1)], [P, CAP]))
                V.tensor_copy(m_eb[buf][:, 2, :], bcast(cst[:, bass.ds(e + (C_ID + NE), 1)], [P, CAP]))
                V.tensor_copy(m_eb[buf][:, 1, :], bcast(cst[:, bass.ds(e + (C_ID + 2 * NE), 1)], [P, CAP]))\
                    .then_inc(sem("sel_ready"), 1)

            def pair(r, it, ip):
                for par in range(2):
                    n = it * 2 + par
                    if par == 0:
                        for t in range(T2):
                            for u in range(2):
                                ins = V.tensor_scalar(m_selw[:, t, u * CAP:(u + 1) * CAP], iota,
                                                      posm[:, t, bass.ds(ip * 2 + u, 1)],
                                                      gates[:, t, bass.ds(ip * 2 + u, 1)], ALU.is_equal, ALU.mult)
                        ins.then_inc(sem("selw_ready"), 1)
                    used(dve, it, 6 * par + 1)
                    V.tensor_scalar(m_g, bG[:, :], 7.0, None, ALU.min).then_inc(sem("gate_read"), 1)
                    select(1 - par, ip * 2 + (par + 1))
                    dve.wait_ge(sem("sg_ready"), n + 1)
                    V.tensor_tensor(m_gs, m_g, m_sg, ALU.mult).then_inc(sem("gs_done"), 1)
                    used(dve, it, 6 * par + 3)
                    V.tensor_scalar(m_uc, bU[:, :], -7.0, 7.0, ALU.max, ALU.min).then_inc(sem("up_read"), 1)
                    dve.wait_ge(sem("gs_done"), n + 1)
                    dve.wait_ge(sem("up_read"), n + 1)
                    V.scalar_tensor_tensor(out=m_act, in0=m_uc, scalar=1.0, in1=m_gs, op0=ALU.add, op1=ALU.mult)\
                        .then_inc(sem("act_ready"), 1)
                for t in range(T2):
                    for hf in range(2):
                        dve.wait_ge(sem("scattered"), it * 4 + (2 * t + hf + 1))
                        xs = xt[:, t, 512 * hf:512 * hf + 512]
                        V.tensor_tensor(xs, xs, (bS0, bS1)[hf][:, :], ALU.add).then_inc(sem("added"), 1)
                dve.wait_ge(sem("added"), it * 4 + 4)

            select(0, 0)
            link_as(V.tensor_copy(cnt_i[:, :], cmax), "counts_ready")
            dve.wait_ge(sem("lge_ready"), 1)
            link(V.tensor_tensor(lg, lg, gt_, ALU.mult))
            link(V.tensor_reduce(gsum, lg, AX.X, ALU.add))
            link(V.reciprocal(gsum, gsum))
            link(V.tensor_tensor(gates[:, :, 0:NE], lg, bcast(gsum.unsqueeze(2), [P, T2, NE]), ALU.mult))
            with dve.Fori(0, PAIRS) as ip:
                pair(0, ip, ip)
            most = dve.value_load(cnt_i[0:1, 0:1], min_val=0, max_val=SEQ)
            with dve.Fori(1, ROUNDS) as r:
                with dve.If(most > r * CAP):
                    dve.wait_ge(sem("gathered"), r * (NE + 1))
                    V.tensor_scalar(posm, posm, float(-CAP), None, ALU.add).then_inc(sem("shifted"), 1)
                    dve.wait_ge(sem("shifted"), r)
                    select(0, 0)
                    with dve.Fori(0, PAIRS) as ip:
                        pair(r, r * PAIRS + ip, ip)
            V.memset(cmax, 0.0).then_inc(sem("result_ready"), 1)


NBC = 12


_INS = ['x', 'attn_norm_g', 'w_in', 'nsa_q_norm_g', 'nsa_kc_norm_g', 'nsa_ks_norm_g', 'nsa_kw_norm_g',
        'cmp_k_pos', 'cmp_k_w1', 'cmp_k_b1', 'cmp_k_w2', 'cmp_k_b2', 'cmp_v_pos', 'cmp_v_w1', 'cmp_v_b1',
        'cmp_v_w2', 'cmp_v_b2', 'nsa_out_norm_g', 'gdn_conv_w', 'gdn_a_log', 'gdn_dt_bias', 'gdn_out_norm_g',
        'w_out', 'ffn_norm_g', 'router_w', 'router_b', 'exp_w_gate', 'exp_b_gate', 'exp_w_up', 'exp_b_up',
        'exp_w_down', 'exp_b_down']


def const_table():
    import numpy as np
    c = np.zeros((P, C_END), np.float32)
    i, j = np.arange(P)[:, None], np.arange(P)[None, :]
    c[:, C_ID:C_ID + P] = i == j
    c[:, C_ONE:C_ONE + P] = 1.0
    c[:, C_TRI:C_TRI + P] = i <= j
    c[:, C_STR:C_STR + P] = i < j
    c[:, C_CM + P:C_CM + 2 * P] = np.where(j <= i, 0.0, -BIG)
    c[:, C_DM:C_DM + P] = np.where(i <= j, 0.0, -BIG)
    for lv in range(1, LEVELS):
        b = 1 << lv
        c[:, C_LV + (lv - 1) * P:C_LV + lv * P] = ((j // b) % 2 == 1) & (i // b == j // b - 1)
    c[:, C_M0:C_M0 + P] = (j % 2 == 1) & (i == j - 1)
    blk = np.arange(16)[None, :]
    for t in range(T2):
        seen = (blk < NCMP) & (16 * blk + 31 <= t * P + np.arange(P)[:, None])
        c[:, C_CA + 16 * t:C_CA + 16 * t + 16] = np.where(seen, 0.0, -BIG)
        c[:, C_CX + 16 * t:C_CX + 16 * t + 16] = seen
    c[:, C_IO:C_IO + CAP] = np.arange(CAP)[None, :]
    return c


def kernel(**inputs):
    import numpy as _np
    import concourse.bacc as _bacc
    from concourse import mybir as _mybir
    from concourse.bass_utils import run_bass_kernel_spmd as _run

    nc = _bacc.Bacc("TRN2", target_bir_lowering=False, num_devices=1)
    arrays, aps = {}, {}
    for name in _INS + ["const_table"]:
        v = const_table() if name == "const_table" else _np.ascontiguousarray(inputs[name])
        arrays[f"in_{name}_dram"] = v
        aps[name] = nc.dram_tensor(f"in_{name}_dram", v.shape, _mybir.dt.from_np(v.dtype), kind="ExternalInput").ap()
    out = nc.dram_tensor("out_0_dram", (1, SEQ, D), _mybir.dt.from_np(_np.dtype("float32")), kind="ExternalOutput").ap()
    hybrid_block(nc, aps, out)
    r = _run(nc, [arrays], core_ids=[0])
    return r.results[0]["out_0_dram"]
```

```python
from contextlib import ExitStack

import concourse.bass as bass
from concourse import mybir

F32 = mybir.dt.float32
I32 = mybir.dt.int32
ACT = mybir.ActivationFunctionType
ALU = mybir.AluOpType
AX = mybir.AxisListType

P = 128
SEQ = 256
D = 1024
T2 = SEQ // P
KC = D // P
EPS = 1e-6
BIG = 1e30
DH = 64
NE = 32
CAP = 64
ROUNDS = SEQ // CAP
FRONT_SLOTS = 4
SLOTS = 10
PAIRS = NE // 2
QUADS = NE // 4
CHUNKS = 24
HD = 128
LEVELS = 7
NCMP = 15

C_ID = 0
C_IO = C_ID + P
C_ONE = C_IO + CAP
C_TRI = C_ONE + P
C_STR = C_TRI + P
C_CM = C_STR + P
C_DM = C_CM + 2 * P
C_LV = C_DM + P
C_M0 = C_LV + (LEVELS - 1) * P
C_CA = C_M0 + P
C_CX = C_CA + 2 * 16
C_END = C_CX + 2 * 16

V_CONV = 0
V_OUTG = 48
V_POS = 52
V_FG = 84
V_END = 92

B_G12 = 0
B_KCG = B_G12 + 12 * DH
B_GDN = B_KCG + DH
B_RB = B_GDN + HD
B_AL = B_RB + NE
B_DT = B_AL + 4
B_END = B_DT + 4
B_B1 = 0
B_B2 = B_B1 + 256
B_CEND = B_B2 + 2 * DH

SLABS = ["c", "b", "a", "q1", "q0", "q2", "z", "w1k", "w1v", "wo_nsa", "wo_gdn"]
PIECES = {"c": 2, "wo_nsa": 2}
QKV = [2, 3, 0, 1, 4, 5]
LAST_USER = {("qkv", 1): "q0", ("qkv", 3): "q1", ("qkv", 5): "q2", ("uc", 1): "c", ("ub", 1): "b", ("ua", 1): "a",
             ("uz", 1): "z", ("hid",): "w1v", ("yg", 1, 1): "wo_gdn", ("yn", 1, 1): "wo_nsa",
             ("s1",): "qk_turned", ("ss", 1): "attention", ("o", 1): "scan", ("oT", 1): "inverse",
             ("lg", 1): "turned_input", ("pos",): "tables"}
REGIONS = {"qk_turned": 4, "attention": 5, "inverse": 6, "scan": 7, "turned_input": 8, "tables": 9}
EXPERT_RING = [3, 0, 4, 5, 7, 1, 6, 2]
ONCE = [8, 9]


def slab_plan():
    uses, landed, plan = [0] * SLOTS, [0] * SLOTS, {}
    for i, name in enumerate(SLABS):
        s = i % FRONT_SLOTS
        landed[s] += 16 * PIECES.get(name, 1)
        plan[name] = (s, landed[s], uses[s])
        uses[s] += 1
    for name, s in REGIONS.items():
        plan[name] = (s, 0, 0)
        uses[s] += 1
    return plan, uses, landed


def expert_plan(uses, landed):
    uses, landed, out = list(uses), list(landed), []
    n = len(EXPERT_RING)
    order = EXPERT_RING + ONCE + [EXPERT_RING[q % n] for q in range(n, 2 * CHUNKS - len(ONCE))]
    for s in order:
        landed[s] += 16
        out.append((s, uses[s], landed[s]))
        uses[s] += 1
    return out[:CHUNKS], out[CHUNKS:]


def attn_steps():
    return [(t, b, g) for t in range(T2) for b in range(2) for g in range(2)]


PROJ = [("qkv", i) for i in QKV[1:]] + [("uz", t) for t in range(T2)]


def pe_front_order():
    j = [("hT", t, i) for t in range(T2) for i in range(2)]
    j += [("uc", t) for t in range(T2)] + [("vecT",)] + [("ub", t) for t in range(T2)]
    j += [("ua", 0), ("gc",), ("gb", 0), ("gb", 1), ("ua", 1)] + [("qkv", QKV[0]), ("qT", 0), ("kT", 0)]
    for i, (t, b, g) in enumerate(attn_steps()):
        if i == 3:
            j += [("nat", 0, 1), ("nat", 1, 1), ("qT", 1), ("kT", 1)]
        elif i == 5:
            j += [("xT", 0, 1), ("xT", 1, 1), ("kk", 0), ("kk", 1), ("nat", 0, 0), ("nat", 1, 0)]
        elif i == 6:
            j += [("cmpT",)]
        elif i == 7:
            j += [("xT", 0, 0), ("xT", 1, 0), ("qk", 0), ("qk", 1), ("nat", 0, 2), ("nat", 1, 2), ("T0", 0), ("T0", 1)]
        if (b, g) == (0, 0):
            j += [("OT", t)]
        j += [("s", t, b, g, k) for k in range(2)]
        if i > 0:
            tt, bb, gg = attn_steps()[i - 1]
            j += [("pT", tt, bb, gg, s) for s in range(tt + 1)]
        if i < len(PROJ):
            j += [PROJ[i]]
    j += [("hid",), ("P", 1, 0), ("P", 1, 1), ("pT", 1, 1, 1, 0), ("pT", 1, 1, 1, 1)]
    fill = {1: [], 2: [("hidT",)], 3: [("cmp2",)], 4: [("kcT",)], 5: [], 6: [("pcT", 0)]}
    for lv in range(1, LEVELS):
        for t in range(T2):
            j += [("P", lv, t), ("UT", lv - 1, t)] if lv > 1 else []
        j += fill[lv]
        for t in range(T2):
            j += [("TP" if lv < LEVELS - 1 else "PU", lv, t)]
        if lv == 4:
            j += [("sc", 0), ("sc", 1)]
    j += [("uv",), ("wT",), ("pcT", 1), ("s1",), ("o", 0), ("v1",), ("ss", 0), ("yn", 0, 0), ("ss", 1), ("oT", 0), ("yn", 0, 1),
          ("o", 1), ("yn", 1, 0), ("yn", 1, 1), ("yg", 0, 0), ("oT", 1), ("yg", 0, 1),
          ("yg", 1, 0), ("x2T", 0, 0), ("x2T", 0, 1), ("yg", 1, 1), ("lg", 0), ("x2T", 1, 0), ("x2T", 1, 1), ("lg", 1), ("pos",)]
    return j


def bank_plan():
    used, plan, turn = [0] * 8, {}, 0
    for job in pe_front_order():
        if job[0] == "OT":
            b = 6 + job[1]
        else:
            b = turn % 6
            turn += 1
        plan[job] = (b, used[b])
        used[b] += 1
    return plan


def hybrid_block(nc, a, out):
    slab, front_uses, front_landed = slab_plan()
    first_chunks, next_chunks = expert_plan(front_uses, front_landed)
    bank = bank_plan()
    fulls, seen = {}, [0] * 8
    for job in pe_front_order():
        if job not in LAST_USER:
            seen[bank[job][0]] += 1
            fulls[job] = seen[bank[job][0]]

    ctx = ExitStack()
    with ctx:
        def sb(name, cols, dt=F32):
            return ctx.enter_context(nc.sbuf_tensor(name, [P, cols], dt))

        sems = {}

        def sem(name):
            if name not in sems:
                sems[name] = ctx.enter_context(nc.semaphore(name))
            return sems[name]

        ring = sb("ring", 8 * 4096)
        btab = sb("btab", D)
        x = sb("x", T2 * D)
        rA = sb("rA", 2048)
        nsa = sb("nsa", 8192 + 2048)
        rB = nsa[:, 8192:]
        late = {8: nsa[:, 6144:]}
        tables = sb("tables", C_ONE + 4096)
        late[9] = tables[:, C_ONE:]
        cst = tables[:, 0:C_END]
        bc = tables[:, C_END:C_END + B_END]
        rw = tables[:, C_END + B_END:C_END + B_END + KC * NE]
        vnew_ = tables[:, C_ONE + 3072:]
        assert C_END + B_END + KC * NE <= C_ONE + 3072
        st = sb("st", 664)
        cnt_i = sb("cnt_i", 1, I32)

        def at(name, lo, n):
            return ring[:, REGIONS[name] * 4096 + lo:REGIONS[name] * 4096 + lo + n]

        rD = at("qk_turned", 0, 3072)
        kgd = at("qk_turned", 3072, 1024)
        attn = at("attention", 0, 3072)
        bst = at("attention", 3072, 1024)
        rC = at("inverse", 0, 12 * (SEQ + 3))
        vT = at("inverse", 3108, V_END)
        bcc = at("inverse", 3200, B_CEND)
        w2 = at("inverse", 3840, 4 * DH)
        vn = at("scan", 0, 1024)
        dec = at("scan", 1024, 1024)
        scan = at("scan", 2048, 1536)
        vec = at("scan", 2048, P)
        gain = nsa[:, 3904:4928]
        gain2 = nsa[:, 0:1024]

        ident = cst[:, C_ID:C_ID + P]
        ones = cst[:, C_ONE:C_ONE + P]
        xt = x[:, :].rearrange("p (t d) -> p t d", t=T2)
        h = rA[:, :].rearrange("p (t d) -> p t d", t=T2)
        hT = rB[:, :].rearrange("p (c t) -> p c t", c=KC)
        cin = rC[:, :].rearrange("p (m t) -> p m t", m=12)
        cv = rD[:, :].rearrange("p (m t) -> p m t", m=12)
        qkn = rA[:, :].rearrange("p (t h d) -> p t h d", t=T2, h=8)
        qkT = rD[:, 0:2048].rearrange("p (h t) -> p h t", h=8)
        kg = kgd[:, 0:512].rearrange("p (h d) -> p h d", h=4)
        kd = kgd[:, 512:1024].rearrange("p (h d) -> p h d", h=4)
        invT = [rC[:, 512 * t:512 * t + 512].rearrange("p (h s) -> p h s", h=4) for t in range(T2)]
        invU = [rC[:, 1024 + 512 * t:1536 + 512 * t].rearrange("p (h s) -> p h s", h=4) for t in range(T2)]
        invP = [rC[:, 2048 + 512 * t:2560 + 512 * t].rearrange("p (h s) -> p h s", h=4) for t in range(T2)]
        v4 = vn[:, :].rearrange("p (t h d) -> p t h d", t=T2, h=4)
        dec4 = dec[:, :].rearrange("p (t h c) -> p t h c", t=T2, h=4)
        qkm4 = dec4
        Lm = [qkn[:, :, 0:4, :], qkn[:, :, 4:8, :]]
        bst4 = bst[:, :].rearrange("p (t h c) -> p t h c", t=T2, h=4)
        nwT = scan[:, 0:512].rearrange("p (h c) -> p h c", h=4)
        qg = scan[:, 512:1024].rearrange("p (h c) -> p h c", h=4)
        S1 = scan[:, 1024:1536].rearrange("p (h e) -> p h e", h=4)
        vnew = vnew_[:, :].rearrange("p (t h e) -> p t h e", t=T2, h=4)
        og = rC[:, 0:1024].rearrange("p (t h c) -> p t h c", t=T2, h=4)
        osc = rC[:, 2048:3072].rearrange("p (t h c) -> p t h c", t=T2, h=4)
        mixT = rB[:, :].rearrange("p (k t) -> p k t", k=8)
        ub = nsa[:, 0:1024].rearrange("p (t n) -> p t n", t=T2)
        uc = nsa[:, 1024:1344].rearrange("p (t n) -> p t n", t=T2)
        nrm = nsa[:, 1344:2880].rearrange("p (t h d) -> p t h d", t=T2, h=12)
        z = nsa[:, 2880:3904].rearrange("p (t h d) -> p t h d", t=T2, h=4)
        qT = nsa[:, 3904:4928].rearrange("p (k t) -> p k t", k=4)
        kbd = nsa[:, 4928:6976].rearrange("p (b g q s) -> p b g q s", b=2, g=2, q=2)
        pcT = nsa[:, 6976:7488]
        vcb = nsa[:, 7488:7616]
        kcb = nsa[:, 7616:7680].rearrange("p (g q c) -> p g q c", g=2, q=2)
        pc = nsa[:, 7680:7936].rearrange("p (h g c) -> p h g c", h=4, g=2)
        smc = [nsa[:, 7936 + 128 * t:8064 + 128 * t].rearrange("p (h c) -> p h c", h=8) for t in range(T2)]
        pr = [attn[:, 1024 * i:1024 * i + 1024].rearrange("p (h s) -> p h s", h=4) for i in range(2)]

        def pT(t, g):
            if t == 0:
                v = attn[:, 2048 + 512 * g:2560 + 512 * g]
            else:
                v = (attn[:, 2048:3072], nsa[:, 1344:2368])[g]
            return v.rearrange("p (s n) -> p s n", s=t + 1)

        cx = rB[:, 0:1024].rearrange("p (v j g c) -> p v j g c", v=2, j=16, g=2)
        cz = rC[:, 2048:3072].rearrange("p (v g t) -> p v g t", v=2, g=2)
        hid = rB[:, 1024:1280]
        hidT = rB[:, 1280:1536].rearrange("p (j n) -> p j n", j=2)
        kv2 = rB[:, 1536:1664]
        kcn = rB[:, 1664:1728]
        oraw = attn[:, 0:1024].rearrange("p (t h n) -> p t h n", t=T2, h=4)
        osq = attn[:, 1024:2048].rearrange("p (t h n) -> p t h n", t=T2, h=4)
        pos_ = [0]

        def stat(n):
            pos_[0] += n
            assert pos_[0] <= 664
            return st[:, pos_[0] - n:pos_[0]]

        ssx, ssx2 = stat(T2), stat(T2)
        sc32 = stat(64).rearrange("p (t n) -> p t n", t=T2)
        gdt = stat(8).rearrange("p (t n) -> p t n", t=T2)
        gg = stat(8).rearrange("p (t n) -> p t n", t=T2)
        gcs = stat(8).rearrange("p (t n) -> p t n", t=T2)
        glast = stat(4)
        eal = stat(4)
        ssq = stat(16).rearrange("p (t n) -> p t n", t=T2)
        ssn = stat(24).rearrange("p (t n) -> p t n", t=T2)
        ssk = stat(1)
        sso = stat(8).rearrange("p (t n) -> p t n", t=T2)
        rsn = stat(T2)
        mx = [stat(4), stat(4)]
        den = [stat(4), stat(4)]
        mc, dc = stat(8), stat(8)
        lg = stat(64).rearrange("p (t n) -> p t n", t=T2)
        m8 = stat(16).rearrange("p (t n) -> p t n", t=T2)
        gt_ = stat(64).rearrange("p (t n) -> p t n", t=T2)
        eq_ = stat(64).rearrange("p (t n) -> p t n", t=T2)
        chosen = stat(64).rearrange("p (t n) -> p t n", t=T2)
        cum = stat(64).rearrange("p (t n) -> p t n", t=T2)
        need = stat(2)
        posm = stat(2 * (NE + 1)).rearrange("p (t n) -> p t n", t=T2)
        gates = stat(2 * (NE + 1)).rearrange("p (t n) -> p t n", t=T2)
        gsum = stat(2)
        cmax = stat(1)
        h2 = h
        x2T = hT
        m_hg = nsa[:, 0:512]
        m_hT = [nsa[:, 512:1024], nsa[:, 1024:1536]]
        m_g = nsa[:, 1536:2048]
        m_sg = nsa[:, 2048:2560]
        m_gs = m_g
        m_uc = nsa[:, 2560:3072]
        m_act = m_uc
        m_aT = nsa[:, 3072:3584]
        m_y = nsa[:, 3584:4608]
        m_selw = nsa[:, 4608:4864].rearrange("p (t n) -> p t n", t=T2)
        m_selwT = nsa[:, 4864:5120].rearrange("p (t n) -> p t n", t=T2)
        m_sel = [nsa[:, 5120 + 128 * i:5248 + 128 * i].rearrange("p (t n) -> p t n", t=T2) for i in range(2)]
        m_eb = [nsa[:, 5376 + 192 * i:5568 + 192 * i].rearrange("p (w n) -> p w n", w=3) for i in range(2)]

        ps = [ctx.enter_context(nc.psum_tensor(f"bank{b}", [P, 512], F32)) for b in range(8)]
        bG, bU, bA, bT1, bT2, bD, bS0, bS1 = ps
        scatter_bank = ((bS0, bT2), (bS1, bT1))

        bank_full = [sem(f"bank_full{b}") for b in range(8)]
        bank_read = [sem(f"bank_read{b}") for b in range(8)]
        landed = [sem(f"slot_landed{s}") for s in range(SLOTS)]
        freed = [sem(f"slot_freed{s}") for s in range(SLOTS)]

        def ringv(s):
            return late[s] if s in late else ring[:, s * 4096:(s + 1) * 4096]

        def signal_of(job):
            if job in LAST_USER:
                s, _, uses = slab[LAST_USER[job]]
                return freed[s], uses + 1
            b = bank[job][0]
            return bank_full[b], fulls[job]

        def full(eng, job):
            eng.wait_ge(*signal_of(job))
            return ps[bank[job][0]]

        def read(ins, job):
            ins.then_inc(bank_read[bank[job][0]], 1)

        def copied(eng, job):
            b, n = bank[job]
            eng.wait_ge(bank_read[b], n + 1)

        def chunk(quad, q, first):
            if first:
                return first_chunks[q]
            s, uses, val = next_chunks[q]
            return s, quad * 3 + (uses - 3), quad * 48 + (val - 48)

        def used(eng, quad, q, first):
            s, uses, _ = chunk(quad, q, first)
            eng.wait_ge(freed[s], uses + 1)

        def bcast(ap, shape):
            return ap.to_broadcast(shape)

        def two_heads(ap):
            return ap.rearrange("p a b -> p (a b)")

        w_in = a["w_in"][0]
        wi = w_in.rearrange("(c p) n -> p c n", p=P)
        w_out = a["w_out"][0]
        wexp = [a[n][0].rearrange("e (h c p) f -> e h p c f", h=2, p=P)
                for n in ("exp_w_gate", "exp_w_up", "exp_w_down")]

        block = ctx.enter_context(nc.Block())

        @block.sync
        def _(sp):
            cols = {"q0": 1304, "q1": 1816, "q2": 2328, "b": 512, "a": 0, "z": 2840}

            def load(name):
                s, _, uses = slab[name]
                if uses > 0:
                    sp.wait_ge(freed[s], uses)
                dst = ringv(s)
                v = dst.rearrange("p (c n) -> p c n", c=KC)
                if name in cols:
                    sp.dma_start(v, wi[:, :, cols[name]:cols[name] + 512]).then_inc(landed[s], 16)
                elif name == "c":
                    sp.dma_start(v[:, :, 0:280], wi[:, :, 1024:1304]).then_inc(landed[s], 16)
                    sp.dma_start(v[:, :, 280:288], wi[:, :, 3352:3360]).then_inc(landed[s], 16)
                elif name in ("w1k", "w1v"):
                    src = a["cmp_k_w1" if name == "w1k" else "cmp_v_w1"][0]
                    sp.dma_start(dst.rearrange("p (j n) -> p j n", j=16),
                                 src.rearrange("(j p) n -> p j n", p=P)).then_inc(landed[s], 16)
                elif name == "wo_gdn":
                    sp.dma_start(dst.rearrange("p (k n) -> p k n", k=4),
                                 w_out[512:1024, :].rearrange("(k p) n -> p k n", p=P)).then_inc(landed[s], 16)
                else:
                    v = w_out[0:512, :].rearrange("(g k d) n -> g d k n", g=2, k=4)
                    for g in range(2):
                        sp.dma_start(dst[64 * g:64 * g + 64, :].rearrange("p (k n) -> p k n", k=4),
                                     v[g]).then_inc(landed[s], 16)

            def row(lo, n, name, rep=1, part=(0, P), table=bc):
                dst = table[part[0]:part[0] + part[1], lo:lo + rep * n].rearrange("p (r n) -> p r n", r=rep)
                src = a[name][0].partition_broadcast(part[1]).unsqueeze(1)
                sp.dma_start(dst, src.to_broadcast([part[1], rep, n])).then_inc(sem("bc_landed"), 16)

            xi = a["x"][0].rearrange("(t p) d -> t p d", p=P)
            sp.dma_start(xt[:, 0, :], xi[0]).then_inc(sem("x0_landed"), 16)
            sp.dma_start(gain, a["attn_norm_g"][0].partition_broadcast(P)).then_inc(sem("gain_landed"), 16)
            sp.dma_start(xt[:, 1, :], xi[1]).then_inc(sem("x1_landed"), 16)
            sp.dma_start(cst[:, 0:C_ONE], a["const_table"][:, 0:C_ONE]).then_inc(sem("ident_landed"), 16)
            load("c")
            row(B_DT, 4, "gdn_dt_bias")
            row(B_AL, 4, "gdn_a_log")
            load("b")
            sp.dma_start(cst[:, C_ONE:], a["const_table"][:, C_ONE:]).then_inc(sem("const_landed"), 16)
            sp.dma_start(vec[V_CONV:V_CONV + 48, :],
                         a["gdn_conv_w"][0].rearrange("j (m p) -> (j m) p", p=P)).then_inc(sem("vec_landed"), 16)
            sp.dma_start(vec[V_OUTG:V_OUTG + 4, :].rearrange("k (g d) -> k g d", g=2),
                         a["nsa_out_norm_g"][0].rearrange("(g k d) -> k g d", g=2, k=4)).then_inc(sem("vec_landed"), 16)
            for v, nm in enumerate(("cmp_k_pos", "cmp_v_pos")):
                sp.dma_start(vec[V_POS + 16 * v:V_POS + 16 * v + 16, :].rearrange("j (i d) -> j i d", i=2),
                             a[nm][0].rearrange("(j i) d -> j i d", i=2)).then_inc(sem("vec_landed"), 16)
            sp.dma_start(vec[V_FG:V_FG + 8, :],
                         a["ffn_norm_g"][0].rearrange("(c p) -> c p", p=P)).then_inc(sem("vec_landed"), 16)
            load("a")
            row(B_G12, DH, "nsa_q_norm_g", rep=8)
            row(B_G12 + 8 * DH, DH, "nsa_ks_norm_g", rep=2)
            row(B_G12 + 10 * DH, DH, "nsa_kw_norm_g", rep=2)
            load("q1")
            row(B_KCG, DH, "nsa_kc_norm_g")
            row(B_GDN, HD, "gdn_out_norm_g")
            row(B_RB, NE, "router_b")
            row(B_B1, 256, "cmp_k_b1", part=(0, 64), table=bcc)
            row(B_B1, 256, "cmp_v_b1", part=(64, 64), table=bcc)
            row(B_B2, DH, "cmp_k_b2", table=bcc)
            row(B_B2 + DH, DH, "cmp_v_b2", table=bcc)
            load("q0")
            for v, nm in enumerate(("cmp_k_w2", "cmp_v_w2")):
                sp.dma_start(w2[:, 2 * v * DH:2 * (v + 1) * DH].rearrange("p (j n) -> p j n", j=2),
                             a[nm][0].rearrange("(j p) n -> p j n", p=P)).then_inc(sem("w2_landed"), 16)
            sp.dma_start(rw[:, :].rearrange("p (c n) -> p c n", c=KC),
                         a["router_w"][0].rearrange("(c p) n -> p c n", p=P)).then_inc(sem("rw_landed"), 16)
            for i, nm in enumerate(("exp_b_gate", "exp_b_down", "exp_b_up")):
                sp.dma_start(btab[NE * i:NE * (i + 1), :], a[nm][0]).then_inc(sem("btab_landed"), 16)
            for name in SLABS[5:]:
                load(name)
            full(sp, ("hidT",))
            sp.dma_start(gain2, a["ffn_norm_g"][0].partition_broadcast(P)).then_inc(sem("gain2_landed"), 16)

            def quad(it, ip, first=False):
                for q in range(CHUNKS):
                    s, uses, _ = chunk(it, q, first)
                    sp.wait_ge(freed[s], uses)
                    sp.dma_start(ringv(s).rearrange("p (c f) -> p c f", c=4),
                                 wexp[q % 6 // 2][ip * 4 + q // 6, q % 2]).then_inc(landed[s], 16)

            quad(0, 0, first=True)
            with sp.Fori(1, QUADS) as ip:
                quad(ip, ip)
            oo = out[0].rearrange("(t p) d -> t p d", p=P)
            for hf in range(2):
                for t in range(T2):
                    sp.wait_ge(sem("added"), 4 * (PAIRS - 1) + 2 * hf + t + 1)
                    sp.dma_start(oo[t][:, 512 * hf:512 * hf + 512], xt[:, t, 512 * hf:512 * hf + 512])\
                        .then_inc(sem("out_written"), 16)
            sp.wait_ge(sem("counts_ready"), 1)
            most = sp.value_load(cnt_i[0:1, 0:1], min_val=0, max_val=SEQ)
            with sp.Fori(1, ROUNDS) as r:
                with sp.If(most > r * CAP):
                    with sp.Fori(0, QUADS) as ip:
                        quad(r * QUADS + ip, ip)
                    sp.wait_ge(sem("added"), (r + 1) * (4 * PAIRS))
                    sp.wait_ge(sem("out_written"), (r + 3) * 16)
                    sp.dma_start(out[0].rearrange("(t p) d -> p t d", p=P), xt).then_inc(sem("out_written"), 16)
            sp.wait_ge(sem("out_written"), 4 * 16)

        @block.tensor
        def _(pe):
            order = iter(pe_front_order())

            def take(job):
                nxt = next(order)
                assert nxt == job, (nxt, job)
                b, n = bank[job]
                if n > 0:
                    pe.wait_ge(bank_read[b], n)
                return ps[b]

            def done(ins, job):
                ins.then_inc(signal_of(job)[0], 1)

            pe.wait_ge(sem("ident_landed"), 16)
            for t in range(T2):
                pe.wait_ge(sem("h_ready"), t + 1)
                for i in range(2):
                    o = take(("hT", t, i))
                    for c in range(4):
                        m = pe.transpose(o[:, c * P:(c + 1) * P], h[:, t, (4 * i + c) * P:(4 * i + c + 1) * P], ident)
                    done(m, ("hT", t, i))

            def natural(job, t, name, n):
                s, val, _ = slab[name]
                w = ringv(s).rearrange("p (c n) -> p c n", c=KC)
                pe.wait_ge(landed[s], val)
                copied(pe, ("hT", t, 0)), copied(pe, ("hT", t, 1))
                o = take((job, t))
                for c in range(KC):
                    m = pe.matmul(o[:, 0:n], hT[:, c, t * P:(t + 1) * P], w[:, c, 0:n],
                                  start=(c == 0), stop=(c == KC - 1))
                done(m, (job, t))

            def qkv(i):
                s, val, _ = slab[f"q{i // 2}"]
                w = ringv(s).rearrange("p (c n) -> p c n", c=KC)
                pe.wait_ge(landed[s], val)
                o = take(("qkv", i))
                for u in range(2):
                    mc0 = (2 * i + u) % 4 * P
                    for c in range(KC):
                        m = pe.matmul(o[:, u * SEQ:(u + 1) * SEQ], w[:, c, mc0:mc0 + P], hT[:, c, :],
                                      start=(c == 0), stop=(c == KC - 1))
                done(m, ("qkv", i))

            def turn4(job, cols):
                o = take(job)
                for hd in range(4):
                    m = pe.transpose(o[:, hd * P:(hd + 1) * P], cols(hd), ident)
                done(m, job)

            def heads(job, lhs, rhs):
                o = take(job)
                for hd in range(4):
                    n = len(lhs)
                    for i in range(n):
                        m = pe.matmul(o[:, hd * P:(hd + 1) * P], lhs[i][:, hd, :], rhs[i][:, hd, :],
                                      start=(i == 0), stop=(i == n - 1))
                done(m, job)

            for t in range(T2):
                natural("uc", t, "c", 288)
            pe.wait_ge(sem("vec_landed"), 80)
            o = take(("vecT",))
            done(pe.transpose(o[:, 0:V_END], vec[0:V_END, :], ident[0:V_END, 0:V_END]), ("vecT",))
            for t in range(T2):
                natural("ub", t, "b", 512)
            natural("ua", 0, "a", 512)
            pe.wait_ge(sem("const_landed"), 16)
            pe.wait_ge(sem("g_ready"), 1)
            o = take(("gc",))
            for t in range(T2):
                m = pe.matmul(o[:, 4 * t:4 * t + 4], cst[:, C_TRI:C_TRI + P], gg[:, t, :], start=True, stop=True)
            done(m, ("gc",))
            for t in range(T2):
                o = take(("gb", t))
                for hd in range(4):
                    m = pe.matmul(o[:, hd * P:(hd + 1) * P], bcast(gg[:, t, hd:hd + 1], [P, P]),
                                  cst[:, C_TRI:C_TRI + P], start=True, stop=True)
                done(m, ("gb", t))
            natural("ua", 1, "a", 512)
            qkv(QKV[0])

            def turn_nsa(t):
                pe.wait_ge(sem("nrm_ready"), t + 1)
                turn4(("qT", t), lambda k: two_heads(nrm[:, t, 2 * k:2 * k + 2, :]))
                o = take(("kT", t))
                for b in range(2):
                    m = pe.transpose(o[:, b * P:(b + 1) * P], two_heads(nrm[:, t, 8 + 2 * b:10 + 2 * b, :]), ident)
                done(m, ("kT", t))

            def turn_nat(k):
                pe.wait_ge(sem("silu_ready"), 2 * (QKV.index(2 * k) // 2 + 1))
                for t in range(T2):
                    turn4(("nat", t, k), lambda hd: cv[:, 4 * k + hd, t * P:(t + 1) * P])

            def turn_qk(k):
                for t in range(T2):
                    pe.wait_ge(sem("kn_ready" if k else "qn_ready"), t + 1)
                    turn4(("xT", t, k), lambda hd: qkn[:, t, 4 * k + hd, :])

            def products(name, lo):
                for t in range(T2):
                    copied(pe, ("xT", t, 1 - (lo == 0)))
                    heads((name, t), [qkT[:, 4:8, t * P:(t + 1) * P]], [qkT[:, lo:lo + 4, t * P:(t + 1) * P]])

            steps = attn_steps()

            def turn_weights(i):
                t, b, g = steps[i]
                pe.wait_ge(sem("pr_ready"), i + 1)
                for s in range(t + 1):
                    turn4(("pT", t, b, g, s), lambda hh: pr[i % 2][:, hh, s * P:(s + 1) * P])

            def values(p):
                t, b, _ = steps[2 * p]
                for s in range(t + 1):
                    for g in range(2):
                        copied(pe, ("pT", t, b, g, s))
                        vals = (ub[:, s, 384 + DH * g:384 + DH * (g + 1)], uc[:, s, DH * g:DH * (g + 1)])[b]
                        m = pe.matmul(ps[6 + t][64 * g:64 * g + 64, :], vals, pT(t, g)[:, s, :],
                                      start=((b, s) == (0, 0)), stop=False, skip_group_check=True)
                m.then_inc(sem("pT_used"), 1)

            def cmp_hidden():
                pe.wait_ge(sem("cx_ready"), 1)
                (sk, vk, _), (sv, vv, _) = slab["w1k"], slab["w1v"]
                pe.wait_ge(landed[sk], vk)
                pe.wait_ge(landed[sv], vv)
                o = take(("hid",))
                for j in range(8):
                    for hf in range(2):
                        for v, s in ((0, sk), (1, sv)):
                            row = 64 * v + 32 * hf
                            m = pe.matmul(o[row:row + 32, 0:256], two_heads(cx[:, v, 8 * hf + j]),
                                          ringv(s).rearrange("p (j n) -> p j n", j=16)[:, 8 * hf + j, :],
                                          start=(j == 0), stop=(j == 7), skip_group_check=True)
                            if (v, hf, j) == (0, 1, 7):
                                m.then_inc(freed[sk], 1)
                done(m, ("hid",))

            turn_nsa(0)
            for i, (t, b, g) in enumerate(steps):
                if i == 3:
                    turn_nat(1)
                    turn_nsa(1)
                elif i == 5:
                    turn_qk(1)
                    products("kk", 4)
                    turn_nat(0)
                elif i == 6:
                    o = take(("cmpT",))
                    for v in range(2):
                        for tt in range(T2):
                            m = pe.transpose(o[:, v * SEQ + tt * P:v * SEQ + (tt + 1) * P],
                                             ub[:, tt, v * P:(v + 1) * P], ident)
                    done(m, ("cmpT",))
                elif i == 7:
                    turn_qk(0)
                    products("qk", 0)
                    turn_nat(2)
                    for tt in range(T2):
                        pe.wait_ge(sem("U_ready"), tt + 1)
                        turn4(("T0", tt), lambda hd: invU[tt][:, hd, :])
                if (b, g) == (0, 0):
                    take(("OT", t))
                    copied(pe, ("qT", t)), copied(pe, ("kT", t))
                for k in range(2):
                    o = take(("s", t, b, g, k))
                    n = P * (t + 1)
                    m = pe.matmul(o[:, 0:2 * n], qT[:, 2 * g + k, t * P:(t + 1) * P], kbd[:, b, g, :, 0:n],
                                  start=True, stop=True)
                    done(m, ("s", t, b, g, k))
                if i > 0:
                    turn_weights(i - 1)
                if i < len(PROJ):
                    name, j = PROJ[i]
                    if name == "qkv":
                        qkv(j)
                    else:
                        natural("uz", j, "z", 512)
                if i > 0 and i % 2 == 0:
                    values(i // 2 - 1)
            cmp_hidden()

            def level_input(lv, t):
                copied(pe, ("T0", t) if lv == 1 else ("TP", lv - 1, t))
                pe.wait_ge(sem("Lm_ready"), 2 * (lv - 1) + t + 1)
                heads(("P", lv, t), [Lm[lv % 2][:, t]], [invT[t]])

            for t in range(T2):
                level_input(1, t)
            turn_weights(len(steps) - 1)
            def cmp_hidden_turned():
                pe.wait_ge(sem("hid_ready"), 1)
                o = take(("hidT",))
                for j in range(2):
                    m = pe.transpose(o[:, j * P:(j + 1) * P], hid[:, j * P:(j + 1) * P], ident)
                done(m, ("hidT",))

            def cmp_output():
                copied(pe, ("hidT",))
                pe.wait_ge(sem("w2_landed"), 32)
                o = take(("cmp2",))
                for v in range(2):
                    for j in range(2):
                        m = pe.matmul(o[0:64, v * DH:(v + 1) * DH], hidT[:, j, 64 * v:64 * v + 64],
                                      w2[:, (2 * v + j) * DH:(2 * v + j + 1) * DH], start=(j == 0), stop=(j == 1))
                done(m, ("cmp2",))

            def cmp_keys_turned():
                pe.wait_ge(sem("kcn_ready"), 1)
                o = take(("kcT",))
                done(pe.transpose(o[0:64, 0:64], kcn[0:64, :], ident[0:64, 0:64]), ("kcT",))

            def cmp_scores(t):
                copied(pe, ("kcT",))
                o = take(("sc", t))
                for k in range(4):
                    m = pe.matmul(o[:, 32 * k:32 * k + 32], qT[:, k, t * P:(t + 1) * P], kcb[:, k // 2, :, :],
                                  start=True, stop=True)
                done(m, ("sc", t))

            def cmp_weights(t):
                pe.wait_ge(sem("pc_ready"), t + 1)
                o = take(("pcT", t))
                for k in range(4):
                    m = pe.transpose(o[0:64, k * P:(k + 1) * P], two_heads(pc[:, k, :, :]), ident)
                done(m, ("pcT", t))

            def cmp_values(t):
                copied(pe, ("pcT", t))
                pe.wait_ge(sem("vc_ready"), 1)
                done(pe.matmul(ps[6 + t][:, :], vcb[0:64, :], pcT[0:64, :], start=False, stop=True,
                               skip_group_check=True), ("OT", t))

            for lv in range(1, LEVELS):
                if lv > 1:
                    for t in range(T2):
                        level_input(lv, t)
                        turn4(("UT", lv - 1, t), lambda hd: invT[t][:, hd, :])
                if lv == 2:
                    cmp_hidden_turned()
                elif lv == 3:
                    cmp_output()
                elif lv == 4:
                    cmp_keys_turned()
                elif lv == 6:
                    cmp_weights(0)
                for t in range(T2):
                    copied(pe, ("P", lv, t))
                    if lv > 1:
                        copied(pe, ("UT", lv - 1, t))
                    if lv < LEVELS - 1:
                        heads(("TP", lv, t), [invU[t]], [invP[t]])
                    else:
                        heads(("PU", lv, t), [invP[t]], [invU[t]])
                if lv == 1:
                    values(len(steps) // 2 - 1)
                elif lv == 4:
                    cmp_scores(0)
                    cmp_scores(1)

            def token_norm(t):
                pe.wait_ge(sem("mixn_ready"), t + 1)
                copied(pe, ("OT", t))
                o = take(("ss", t))
                for k in range(4):
                    m = pe.matmul(o[:, 0:1], osq[:, t, k, :], ones[:, 0:1], start=(k == 0), stop=(k == 3))
                done(m, ("ss", t))

            def project(name, t, n):
                lo, sl = {"yg": (4, "wo_gdn"), "yn": (0, "wo_nsa")}[name]
                s, val, _ = slab[sl]
                w = ringv(s).rearrange("p (k n) -> p k n", k=4)
                pe.wait_ge(landed[s], val)
                if lo:
                    copied(pe, ("oT", t))
                else:
                    pe.wait_ge(sem("mixn_ready"), t + 1)
                o = take((name, t, n))
                for k in range(4):
                    m = pe.matmul(o[:, :], mixT[:, lo + k, t * P:(t + 1) * P], w[:, k, n * 512:(n + 1) * 512],
                                  start=(k == 0), stop=(k == 3))
                done(m, (name, t, n))

            def turn_gdn(t):
                pe.wait_ge(sem("og_ready"), t + 1)
                turn4(("oT", t), lambda hd: og[:, t, hd, :])

            def turn_x2(t, i):
                copied(pe, ("yg", t, i)), copied(pe, ("yn", t, i))
                turn4(("x2T", t, i), lambda c: xt[:, t, (4 * i + c) * P:(4 * i + c + 1) * P])

            def router(t):
                pe.wait_ge(sem("rw_ready"), 1)
                copied(pe, ("x2T", t, 0)), copied(pe, ("x2T", t, 1))
                o = take(("lg", t))
                for c in range(KC):
                    m = pe.matmul(o[:, 0:NE], x2T[:, c, t * P:(t + 1) * P], rw[:, c * NE:(c + 1) * NE],
                                  start=(c == 0), stop=(c == KC - 1))
                done(m, ("lg", t))

            copied(pe, ("PU", LEVELS - 1, 0))
            copied(pe, ("nat", 0, 2))
            heads(("uv",), [invU[0]], [v4[:, 0]])
            copied(pe, ("PU", LEVELS - 1, 1))
            pe.wait_ge(sem("kgd_ready"), 1)
            heads(("wT",), [kg], [invU[1]])
            cmp_values(0)
            cmp_weights(1)
            copied(pe, ("uv",))
            pe.wait_ge(sem("qg_ready"), 1)
            heads(("s1",), [kd], [vnew[:, 0]])
            heads(("o", 0), [qkm4[:, 0]], [vnew[:, 0]])
            cmp_values(1)
            copied(pe, ("s1",)), copied(pe, ("wT",)), copied(pe, ("nat", 1, 2))
            heads(("v1",), [invU[1], nwT], [v4[:, 1], S1])
            token_norm(0)
            project("yn", 0, 0)
            token_norm(1)
            turn_gdn(0)
            project("yn", 0, 1)
            copied(pe, ("v1",))
            heads(("o", 1), [qg, qkm4[:, 1]], [S1, vnew[:, 1]])
            project("yn", 1, 0)
            project("yn", 1, 1)
            project("yg", 0, 0)
            turn_gdn(1)
            project("yg", 0, 1)
            project("yg", 1, 0)
            turn_x2(0, 0)
            turn_x2(0, 1)
            project("yg", 1, 1)
            router(0)
            turn_x2(1, 0)
            turn_x2(1, 1)
            router(1)
            strict = cst[:, C_STR:C_STR + P]
            pe.wait_ge(sem("mask_ready"), 1)
            o = take(("pos",))
            pe.matmul(o[:, 0:NE], strict, chosen[:, 0, :], start=True, stop=True)
            pe.matmul(o[:, NE:3 * NE].rearrange("p (w n) -> p w n", w=2), ones,
                      bcast(chosen[:, 0:1, :], [P, 2, NE]), start=True, stop=False, skip_group_check=True)
            pe.wait_ge(sem("mask_ready"), T2)
            pe.matmul(o[:, NE:2 * NE], strict, chosen[:, 1, :], start=False, stop=True, skip_group_check=True)
            m = pe.matmul(o[:, 2 * NE:3 * NE], ones, chosen[:, 1, :], start=False, stop=True, skip_group_check=True)
            done(m, ("pos",))

            def banks_out(*bs):
                for b in bs:
                    pe.wait_ge(bank_read[b], max(n for bb, n in bank.values() if bb == b) + 1)

            banks_out(2, 3)
            pe.wait_ge(sem("h2_ready"), T2)
            pe.wait_ge(sem("btab_landed"), 48)
            pe.wait_ge(sem("btab_ready"), 1)

            def gather(buf, m, first=False):
                pe.wait_ge(sem("sel_ready"), m + 1)
                if not first:
                    pe.wait_ge(sem("hg_read"), m)
                for t in range(T2):
                    for hf in range(2):
                        i = pe.matmul(bA[64 * hf:64 * hf + 64, :], m_sel[buf][:, t, :], h2[:, t, 512 * hf:512 * hf + 512],
                                      start=(t == 0), stop=(t == 1), skip_group_check=True)
                i.then_inc(sem("gathered"), 1)

            def turn_rows(m, first=False):
                pe.wait_ge(sem("hg_read"), m + 1)
                if not first:
                    pe.wait_ge(sem("eT_read"), m)
                for j in range(4):
                    i = pe.transpose(bT1[:, j * P:(j + 1) * P], m_hg[:, j * P:(j + 1) * P], ident)
                i.then_inc(sem("rows_turned"), 1)

            def bias(o, buf, w):
                for fh in range(2):
                    pe.matmul(o[64 * fh:64 * fh + 64, :], m_eb[buf][:, w, :], btab[:, 512 * fh:512 * fh + 512],
                              start=True, stop=False, skip_group_check=True)

            def stream(o, quad, q0, lhs, first):
                for q in (q0, q0 + 1):
                    s, _, val = chunk(quad, q, first)
                    pe.wait_ge(landed[s], val)
                    w = ringv(s).rearrange("p (c f) -> p c f", c=4)
                    for c in range(4):
                        cc = (q - q0) * 4 + c
                        lt = lhs[:, (cc % 4) * P + (cc // 4) * CAP:(cc % 4) * P + (cc // 4) * CAP + CAP]
                        for fh in range(2):
                            i = pe.matmul(o[64 * fh:64 * fh + 64, :], lt, w[:, c, 512 * fh:512 * fh + 512],
                                          start=False, stop=(cc == 7), skip_group_check=True)
                            if fh == 1 and c == 3:
                                i.then_inc(freed[s], 1)
                return i

            def pair(r, quad, half, first=False):
                it = quad * 2 + half
                q0 = 12 * half
                for par in range(2):
                    n = it * 2 + par
                    m = n + r
                    pe.wait_ge(sem("eb_ready"), m + 1)
                    for w, o in enumerate((bG, bU)):
                        bias(o, par, w)
                        if w == 0:
                            pe.wait_ge(sem("eT_read"), m + 1)
                        stream(o, quad, q0 + 6 * par + 2 * w, m_hT[par], first)
                    gather(1 - par, m + 1)
                    if par == 0:
                        pe.wait_ge(sem("selw_ready"), it + 1)
                        for t in range(T2):
                            i = pe.transpose(bS0[:, t * P:(t + 1) * P], m_selw[:, t, :], ident)
                        i.then_inc(sem("selw_turned"), 1)
                    pe.wait_ge(sem("act_ready"), n + 1)
                    for j in range(4):
                        i = pe.transpose(bT2[:, j * P:(j + 1) * P], m_act[:, j * P:(j + 1) * P], ident)
                    i.then_inc(sem("act_turned"), 1)
                    turn_rows(m + 1)
                    pe.wait_ge(sem("aT_read"), n + 1)
                    bias(bD, par, 2)
                    stream(bD, quad, q0 + 6 * par + 4, m_aT, first)
                pe.wait_ge(sem("selwT_read"), it + 1)
                pe.wait_ge(sem("eT_read"), it * 2 + (r + 3))
                for hf, y_ready in enumerate(("y0_read", "y1_read")):
                    pe.wait_ge(sem(y_ready), it * 2 + 2)
                    for t in range(T2):
                        pe.matmul(scatter_bank[hf][t][:, :], m_selwT[:, t, :], m_y[:, 512 * hf:512 * hf + 512],
                                  start=True, stop=True).then_inc(sem("scattered"), 1)

            gather(0, 0, first=True)
            turn_rows(0, first=True)
            banks_out(0, 1, 4, 5, 6, 7)
            for half in range(2):
                pair(0, 0, half, first=True)
            with pe.Fori(1, QUADS) as ip:
                for half in range(2):
                    pair(0, ip, half)
            pe.wait_ge(sem("counts_ready"), 1)
            most = pe.value_load(cnt_i[0:1, 0:1], min_val=0, max_val=SEQ)
            with pe.Fori(1, ROUNDS) as r:
                with pe.If(most > r * CAP):
                    gather(0, r * (NE + 1))
                    turn_rows(r * (NE + 1))
                    with pe.Fori(0, QUADS) as ip:
                        for half in range(2):
                            pair(r, r * QUADS + ip, half)

        @block.scalar
        def _(act):
            nchain = [0]

            def link(ins):
                nchain[0] += 1
                ins.then_inc(sem("act_chain"), 1)
                act.wait_ge(sem("act_chain"), nchain[0])

            def act_(o, i, f, **k):
                return nc.scalar.activation(o, i, f, **k)

            def copy(o, i):
                return nc.scalar.activation(o, i, ACT.Copy)

            def root(ap, wait, sqrt, n=1):
                act.wait_ge(sem(wait), n)
                act_(ap, ap, ACT.Sqrt).then_inc(sem(sqrt), 1)

            def evac(job, dst, src):
                for d_, s_ in zip(dst, src):
                    ins = copy(d_, s_)
                read(ins, job)

            def evac4(job, dst):
                o = full(act, job)
                evac(job, [dst], [o[:, :].rearrange("p (h d) -> p h d", h=4)])

            for t in range(T2):
                act.wait_ge(sem(f"x{t}_landed"), 16)
                act_(h[:, t, :], xt[:, t, :], ACT.Square, accum_out=ssx[:, t:t + 1]).then_inc(sem("ssx_ready"), 1)
                root(ssx[:, t:t + 1], "msx_ready", "rms_ready", t + 1)
            for t in range(T2):
                evac4(("hT", t, 0), hT[:, 0:4, t * P:(t + 1) * P])
            for t in range(T2):
                o = full(act, ("uc", t))
                evac(("uc", t), [nrm[:, t, 10:12, :], uc[:, t, :]],
                     [o[:, 0:128].rearrange("p (h d) -> p h d", h=2), o[:, 128:288]])
            o = full(act, ("vecT",))
            read(copy(vT[:, :], o[:, 0:V_END]), ("vecT",))
            act.wait_ge(sem("sc_ready"), 1)
            act.wait_ge(sem("bc_landed"), 16 * NBC)
            link(act_(sc32, sc32, ACT.Exp))
            act_(eal, bc[:, B_AL:B_AL + 4], ACT.Exp).then_inc(sem("exp_ready"), 1)
            act.wait_ge(sem("sc1_ready"), 1)
            act_(gdt, sc32[:, :, 24:28], ACT.Ln).then_inc(sem("ln_ready"), 1)
            for t in range(T2):
                o = full(act, ("ub", t))
                evac(("ub", t), [nrm[:, t, 8:10, :], ub[:, t, :]],
                     [o[:, 256:384].rearrange("p (h d) -> p h d", h=2), o[:, :]])
            act.wait_ge(sem("gdiff_ready"), 1)
            act_(dec[:, :], dec[:, :], ACT.Exp)
            act_(qg, qg, ACT.Exp)
            act_(gcs[:, 1, :], gcs[:, 1, :], ACT.Exp)
            act_(glast, glast, ACT.Exp).then_inc(sem("decay_ready"), 1)

            def ev_qkv(i):
                o = full(act, ("qkv", i))
                evac(("qkv", i), [cin[:, 2 * i:2 * i + 2, 3:]], [o[:, :].rearrange("p (u t) -> p u t", u=2)])

            def silu(k):
                act.wait_ge(sem("conv_ready"), QKV.index(2 * k) + 2)
                for i in (2 * k, 2 * k + 1):
                    act_(cv[:, 2 * i:2 * i + 2, :], cv[:, 2 * i:2 * i + 2, :], ACT.Silu).then_inc(sem("silu_ready"), 1)

            def ev_nsa(t):
                o = full(act, ("qT", t))
                evac(("qT", t), [qT[:, :, t * P:(t + 1) * P]], [o[:, :].rearrange("p (k t) -> p k t", k=4)])
                act.wait_ge(sem("zeroed"), 1)
                o = full(act, ("kT", t))
                ov = o[:, 0:256].rearrange("p (b t) -> p b t", b=2)
                evac(("kT", t), [kbd[64 * p:64 * p + 64, :, g, p, t * P:(t + 1) * P] for g in range(2) for p in range(2)],
                     [ov[64 * g:64 * g + 64] for g in range(2) for p in range(2)])

            def ev_nat(k):
                for t in range(T2):
                    evac4(("nat", t, k), qkn[:, t, 4 * k:4 * k + 4, :] if k < 2 else v4[:, t])

            def ev_qk(k):
                for t in range(T2):
                    evac4(("xT", t, k), qkT[:, 4 * k:4 * k + 4, t * P:(t + 1) * P])

            steps = attn_steps()

            def ev_weights(i):
                t, b, g = steps[i]
                if i > 1:
                    act.wait_ge(sem("pT_used"), i // 2)
                for s in range(t + 1):
                    o = full(act, ("pT", t, b, g, s))
                    evac(("pT", t, b, g, s), [pT(t, g)[:, s, :]], [o[:, :]])

            for t in range(T2):
                o = full(act, ("ua", t))
                evac(("ua", t), [nrm[:, t, 0:8, :]], [o[:, :].rearrange("p (h d) -> p h d", h=8)])
                if t == 0:
                    root(ssn[:, 0, :], "ssn_ready", "sqn_ready")
            act.wait_ge(sem("cin_zeroed"), 1)
            ev_qkv(QKV[0])
            ev_nsa(0)
            root(ssn[:, 1, :], "ssn_ready", "sqn_ready", 2)
            for i, (t, b, g) in enumerate(steps):
                if i == 3:
                    ev_nat(1)
                    ev_nsa(1)
                elif i == 5:
                    ev_qk(1)
                    ev_nat(0)
                elif i == 6:
                    act.wait_ge(sem("conv_ready"), 6)
                    o = full(act, ("cmpT",))
                    ov = o[:, :].rearrange("p (v t) -> p v t", v=2)
                    evac(("cmpT",), [c_ for g_ in range(2) for c_ in (cz[0:64, :, g_, :], cz[64:128, :, g_, 0:SEQ - 1])],
                         [c_ for g_ in range(2) for c_ in (ov[64 * g_:64 * g_ + 64], ov[64 * g_:64 * g_ + 64, :, 1:SEQ])])
                elif i == 7:
                    ev_qk(0)
                    ev_nat(2)
                    for tt in range(T2):
                        evac4(("T0", tt), invT[tt])
                if i > 0:
                    ev_weights(i - 1)
                n = P * (t + 1)
                act.wait_ge(sem("max_ready"), i + 1)
                for hh in range(4):
                    ins = act_(pr[i % 2][:, hh, 0:n], pr[i % 2][:, hh, 0:n], ACT.Exp,
                               bias=mx[i % 2][:, hh:hh + 1], accum_out=den[i % 2][:, hh:hh + 1])
                ins.then_inc(sem("exp_done"), 1)
                if i == 2:
                    silu(1)
                elif i == 4:
                    silu(0)
                elif i == 6:
                    silu(2)
                if i < len(PROJ):
                    name, j = PROJ[i]
                    if name == "qkv":
                        ev_qkv(j)
                    else:
                        o = full(act, ("uz", j))
                        read(act_(z[:, j], o[:, :].rearrange("p (h d) -> p h d", h=4), ACT.Silu), ("uz", j))
                if i == 3:
                    root(ssq[:, :, 4:8], "ssq_ready", "sqq_ready", 1)
                elif i == 5:
                    root(ssq[:, :, 0:4], "ssq_ready", "sqq_ready", 2)
            for t in range(T2):
                evac4(("P", 1, t), invP[t])
            ev_weights(len(steps) - 1)

            def ev_OT(t):
                o = full(act, ("OT", t))
                copy(oraw[:, t], o[:, :].rearrange("p (h n) -> p h n", h=4))
                read(act_(osq[:, t], o[:, :].rearrange("p (h n) -> p h n", h=4), ACT.Square), ("OT", t))

            for lv in range(1, LEVELS):
                if lv > 1:
                    for t in range(T2):
                        evac4(("P", lv, t), invP[t])
                        evac4(("UT", lv - 1, t), invU[t])
                if lv == 1:
                    copied(act, ("hid",))
                    act_(hid, hid, ACT.Gelu_apprx_tanh).then_inc(sem("hid_ready"), 1)
                elif lv == 2:
                    o = full(act, ("hidT",))
                    packed = [o[:, P * j:P * j + P].rearrange("p (v w) -> p v w", v=2)[:, :, 0:32] for j in range(2)]
                    evac(("hidT",), [hidT[:, j, :].rearrange("p (v g c) -> p v g c", v=2, g=2)[:, :, :, 0:16] for j in range(2)],
                         [p_.rearrange("p v (g c) -> p v g c", g=2) for p_ in packed])
                elif lv == 3:
                    root(ssk[0:64, :], "ssk_ready", "sqk_ready")
                elif lv == 4:
                    o = full(act, ("kcT",))
                    evac(("kcT",), [kcb[64 * p:64 * p + 64, g, p, :] for g in range(2) for p in range(2)],
                         [o[0:64, 32 * g:32 * g + 16] for g in range(2) for p in range(2)])
                elif lv == 5:
                    for t in range(T2):
                        act.wait_ge(sem("smc_ready"), t + 1)
                        act_(smc[t], smc[t], ACT.Exp).then_inc(sem("ec_ready"), 1)
                elif lv == 6:
                    o = full(act, ("pcT", 0))
                    evac(("pcT", 0), [pcT[0:64, :]], [o[0:64, :]])
            o = full(act, ("wT",))
            read(nc.scalar.mul(nwT, o[:, :].rearrange("p (h d) -> p h d", h=4), -1.0), ("wT",))
            o = full(act, ("pcT", 1))
            full(act, ("OT", 0))
            evac(("pcT", 1), [pcT[0:64, :]], [o[0:64, :]])
            evac4(("s1",), S1)
            evac4(("o", 0), og[:, 0])
            ev_OT(0)
            ev_OT(1)
            root(sso[:, 0, :], "sso_ready", "sqo_ready", 1)
            root(rsn[:, 0:1], "rsn_ready", "rsn_sqrt", 1)
            root(rsn[:, 1:2], "rsn_ready", "rsn_sqrt", 2)
            evac4(("oT", 0), mixT[:, 4:8, 0:P])
            evac4(("o", 1), og[:, 1])
            root(sso[:, 1, :], "sso_ready", "sqo_ready", 2)
            evac4(("oT", 1), mixT[:, 4:8, P:2 * P])
            for t in range(T2):
                copied(act, ("yg", t, 1))
                act_(h2[:, t, :], xt[:, t, :], ACT.Square, accum_out=ssx2[:, t:t + 1]).then_inc(sem("ssx2_ready"), 1)
                for i in range(2):
                    evac4(("x2T", t, i), x2T[:, 4 * i:4 * i + 4, t * P:(t + 1) * P])
                root(ssx2[:, t:t + 1], "msx2_ready", "rms2_ready", t + 1)
                act.wait_ge(sem("rstd2_ready"), t + 1)
                nc.scalar.mul(h2[:, t, :], xt[:, t, :], ssx2[:, t:t + 1]).then_inc(sem("h2_scaled"), 1)
            act.wait_ge(sem("lgm_ready"), 1)
            act_(lg, lg, ACT.Exp).then_inc(sem("lge_ready"), 1)

            def rows_out(m, first=False):
                act.wait_ge(sem("gathered"), m + 1)
                if not first:
                    act.wait_ge(sem("rows_turned"), m)
                copy(m_hg, bA[:, :]).then_inc(sem("hg_read"), 1)

            def turned_out(buf, m):
                act.wait_ge(sem("rows_turned"), m + 1)
                copy(m_hT[buf], bT1[:, :]).then_inc(sem("eT_read"), 1)

            def pair(r, quad, half, first=False):
                it = quad * 2 + half
                for par in range(2):
                    n = it * 2 + par
                    m = n + r
                    act.wait_ge(sem("gate_read"), n + 1)
                    act_(m_sg, m_g, ACT.Sigmoid, scale=1.702).then_inc(sem("sg_ready"), 1)
                    rows_out(m + 1)
                    if par == 0:
                        act.wait_ge(sem("selw_turned"), it + 1)
                        copy(m_selwT, bS0[:, 0:256].rearrange("p (t n) -> p t n", t=T2)).then_inc(sem("selwT_read"), 1)
                    act.wait_ge(sem("act_turned"), n + 1)
                    copy(m_aT, bT2[:, :]).then_inc(sem("aT_read"), 1)
                    turned_out(1 - par, m + 1)
                    used(act, quad, 12 * half + 6 * par + 5, first)
                    copy(m_y[64 * par:64 * par + 64, 0:512], bD[0:64, :]).then_inc(sem("y0_read"), 1)

            rows_out(0, first=True)
            turned_out(0, 0)
            for half in range(2):
                pair(0, 0, half, first=True)
            with act.Fori(1, QUADS) as ip:
                for half in range(2):
                    pair(0, ip, half)
            act.wait_ge(sem("counts_ready"), 1)
            most = act.value_load(cnt_i[0:1, 0:1], min_val=0, max_val=SEQ)
            with act.Fori(1, ROUNDS) as r:
                with act.If(most > r * CAP):
                    rows_out(r * (NE + 1))
                    turned_out(0, r * (NE + 1))
                    with act.Fori(0, QUADS) as ip:
                        for half in range(2):
                            pair(r, r * QUADS + ip, half)

        @block.gpsimd
        def _(pool):
            nchain = [0]

            def link(ins):
                nchain[0] += 1
                ins.then_inc(sem("pool_chain"), 1)
                pool.wait_ge(sem("pool_chain"), nchain[0])

            G = nc.gpsimd
            told = {}

            def link_as(ins, name):
                told[name] = told.get(name, 0) + 1
                ins.then_inc(sem(name), 1)
                pool.wait_ge(sem(name), told[name])

            link_as(G.memset(cin[:, :, 0:3], 0.0), "cin_zeroed")
            for v in (vcb, kcb, pc):
                link(G.memset(v, 0.0))
            link_as(G.memset(kbd, 0.0), "zeroed")
            link_as(G.memset(btab[96:128, :], 0.0), "btab_ready")
            pool.wait_ge(sem("rw_landed"), 16)
            copied(pool, ("vecT",))
            rw8 = rw[:, :].rearrange("p (c n) -> p c n", c=KC)
            link_as(G.tensor_tensor(rw8, rw8, bcast(vT[:, V_FG:V_FG + 8].unsqueeze(2), [P, KC, NE]), ALU.mult), "rw_ready")
            pool.wait_ge(sem("decay_ready"), 1)
            pool.wait_ge(sem("kn_ready"), T2)
            link(G.tensor_tensor(kg, qkn[:, 1, 4:8, :], bcast(gcs[:, 1, :].unsqueeze(2), [P, 4, HD]), ALU.mult))
            link_as(G.tensor_tensor(kd, qkn[:, 0, 4:8, :], bcast(glast.unsqueeze(2), [P, 4, HD]), ALU.mult), "kgd_ready")
            pool.wait_ge(sem("const_landed"), 16)
            for lv in range(1, LEVELS):
                mask = bcast(cst[:, C_LV + (lv - 1) * P:C_LV + lv * P].unsqueeze(1), [P, 4, P])
                for t in range(T2):
                    if lv == 1:
                        copied(pool, ("kk", t))
                    elif lv == 2:
                        full(pool, ("xT", t, 0))
                    else:
                        full(pool, ("P", lv - 2, t))
                    link_as(G.tensor_tensor(Lm[lv % 2][:, t], bst4[:, t], mask, ALU.mult), "Lm_ready")
                if lv == 1:
                    full(pool, ("uz", 1))
                    copied(pool, ("cmpT",))
                    for v in range(2):
                        link(G.memset(cx[:, v, :, :, NCMP:16], 0.0))
                    link(G.memset(hid, 0.0))
                    link(G.memset(hidT, 0.0))
                    for v in range(2):
                        for g in range(2):
                            pairs = cz[:, v, g, :].rearrange("p (c j i) -> p j c i", j=8, i=2)[:, :, :, 0]
                            for u in range(2):
                                rows = vT[:, V_POS + 16 * v + 8 * u:V_POS + 16 * v + 8 * u + 8].unsqueeze(2)
                                ins = G.tensor_tensor(cx[:, v, 8 * u:8 * u + 8, g, 0:NCMP],
                                                      pairs[:, :, u:u + NCMP], bcast(rows, [P, 8, NCMP]), ALU.add)
                                if (v, g, u) == (1, 1, 1):
                                    link_as(ins, "cx_ready")
                                else:
                                    link(ins)
                if lv == 2:
                    copied(pool, ("xT", 1, 0))
                    link_as(G.tensor_tensor(qg, qg, qkT[:, 0:4, P:2 * P], ALU.mult), "qg_ready")
                elif lv == 3:
                    for t in range(T2):
                        copied(pool, ("uz", t))
                        link_as(G.tensor_tensor(z[:, t], z[:, t], bcast(bc[:, B_GDN:B_GDN + HD].unsqueeze(1), [P, 4, HD]),
                                                ALU.mult), "z_ready")
            for t in range(T2):
                copied(pool, ("OT", t))
                link_as(G.tensor_tensor(mixT[:, 0:4, t * P:(t + 1) * P], oraw[:, t],
                                        bcast(vT[:, V_OUTG:V_OUTG + 4].unsqueeze(2), [P, 4, P]), ALU.mult), "mixn_ready")
            pool.wait_ge(sem("gain2_landed"), 16)
            for t in range(T2):
                pool.wait_ge(sem("h2_scaled"), t + 1)
                link_as(G.tensor_tensor(h2[:, t, :], h2[:, t, :], gain2, ALU.mult), "h2_ready")

        @block.vector
        def _(dve):
            nchain = [0]
            V = nc.vector

            def link(ins):
                nchain[0] += 1
                ins.then_inc(sem("dve_chain"), 1)
                dve.wait_ge(sem("dve_chain"), nchain[0])

            told = {}

            def link_as(ins, name):
                told[name] = told.get(name, 0) + 1
                ins.then_inc(sem(name), 1)
                dve.wait_ge(sem(name), told[name])

            def link_read(ins, job):
                read(ins, job)
                copied(dve, job)

            def rstd(ap, n, wait, sqrt, name=None):
                link_as(V.tensor_scalar(ap, ap, 1.0 / n, EPS, ALU.mult, ALU.add), wait)
                dve.wait_ge(sem(sqrt), told[wait])
                if name:
                    link_as(V.reciprocal(ap, ap), name)
                else:
                    link(V.reciprocal(ap, ap))

            def h4(ap):
                return ap.rearrange("p (h s) -> p h s", h=4)

            for t in range(T2):
                dve.wait_ge(sem("ssx_ready"), t + 1)
                rstd(ssx[:, t:t + 1], D, "msx_ready", "rms_ready")
                dve.wait_ge(sem("gain_landed"), 16)
                link_as(V.scalar_tensor_tensor(out=h[:, t, :], in0=xt[:, t, :], scalar=ssx[:, t:t + 1], in1=gain,
                                               op0=ALU.mult, op1=ALU.mult), "h_ready")
            for t in range(T2):
                o = full(dve, ("hT", t, 1))
                read(V.tensor_copy(hT[:, 4:8, t * P:(t + 1) * P], h4(o[:, :])), ("hT", t, 1))

            def conv(i):
                copied(dve, ("qkv", i))
                for tap in range(4):
                    for u in range(2):
                        m = 2 * i + u
                        w = vT[:, V_CONV + 12 * tap + m:V_CONV + 12 * tap + m + 1]
                        src = cin[:, m, tap:tap + SEQ]
                        if tap == 0:
                            ins = V.tensor_scalar(cv[:, m, :], src, w, None, ALU.mult)
                        else:
                            ins = V.scalar_tensor_tensor(out=cv[:, m, :], in0=src, scalar=w, in1=cv[:, m, :],
                                                         op0=ALU.mult, op1=ALU.add)
                    if tap < 3:
                        link(ins)
                    else:
                        link_as(ins, "conv_ready")

            dve.wait_ge(sem("const_landed"), 16)
            copied(dve, ("uc", 0)), copied(dve, ("uc", 1))
            dve.wait_ge(sem("bc_landed"), 16 * NBC)
            link(V.tensor_tensor(gdt, uc[:, :, 152:156], bcast(bc[:, B_DT:B_DT + 4].unsqueeze(1), [P, T2, 4]), ALU.add))
            V.tensor_scalar(sc32[:, :, 0:24], uc[:, :, 128:152], -1.0, None, ALU.mult)
            V.tensor_scalar(sc32[:, :, 28:32], uc[:, :, 156:160], -1.0, None, ALU.mult)
            link(V.scalar_tensor_tensor(out=sc32[:, :, 24:28], in0=gdt, scalar=-1.0, in1=gdt, op0=ALU.mult, op1=ALU.min))
            link_as(V.tensor_scalar(gg, gdt, 0.0, None, ALU.max), "sc_ready")
            dve.wait_ge(sem("exp_ready"), 1)
            link_as(V.tensor_scalar(sc32, sc32, 1.0, None, ALU.add), "sc1_ready")
            dve.wait_ge(sem("ln_ready"), 1)
            link(V.tensor_tensor(gg, gg, gdt, ALU.add))
            link_as(V.scalar_tensor_tensor(out=gg, in0=gg, scalar=-1.0, in1=bcast(eal.unsqueeze(1), [P, T2, 4]),
                                        op0=ALU.mult, op1=ALU.mult), "g_ready")
            link(V.reciprocal(sc32, sc32))
            for t in range(T2):
                link(V.tensor_copy(bst4[:, t], bcast(sc32[:, t, 28:32].unsqueeze(2), [P, 4, P])))
                link(V.tensor_tensor(bst4[:, t], bst4[:, t],
                                     bcast(cst[:, C_STR:C_STR + P].unsqueeze(1), [P, 4, P]), ALU.mult))
            o = full(dve, ("gc",))
            link_read(V.tensor_copy(gcs, o[:, 0:8].rearrange("p (t n) -> p t n", t=T2)), ("gc",))
            for t in range(T2):
                o = full(dve, ("gb", t))
                ov = h4(o[:, :])
                if t == 0:
                    V.tensor_copy(glast, ov[:, :, P - 1])
                else:
                    V.tensor_copy(qg, ov)
                link_read(V.tensor_tensor(dec4[:, t], ov, bcast(cst[:, C_DM:C_DM + P].unsqueeze(1), [P, 4, P]), ALU.add), ("gb", t))
                link(V.tensor_tensor(dec4[:, t], dec4[:, t], bcast(gcs[:, t, :].unsqueeze(2), [P, 4, P]), ALU.subtract))
            link_as(V.tensor_tensor(glast, glast, gcs[:, 0, :], ALU.subtract), "gdiff_ready")
            dve.wait_ge(sem("decay_ready"), 1)
            for t in range(T2):
                link(V.tensor_tensor(bst4[:, t], bst4[:, t], dec4[:, t], ALU.mult))

            def nsa_norm(t):
                sq = vnew_[:, 0:768].rearrange("p (h d) -> p h d", h=12)
                copied(dve, ("ua", t))
                link(V.tensor_tensor(sq, nrm[:, t], nrm[:, t], ALU.mult))
                link(V.tensor_reduce(ssn[:, t, :], sq, AX.X, ALU.add))
                rstd(ssn[:, t, :], DH, "ssn_ready", "sqn_ready")
                link(V.tensor_tensor(nrm[:, t], nrm[:, t], bcast(ssn[:, t, :].unsqueeze(2), [P, 12, DH]), ALU.mult))
                link_as(V.tensor_tensor(nrm[:, t], nrm[:, t],
                                        bc[:, B_G12:B_G12 + 768].rearrange("p (h d) -> p h d", h=12), ALU.mult), "nrm_ready")

            def l2_squares(k):
                sq = vnew_[:, :].rearrange("p (t h d) -> p t h d", t=T2, h=4)
                part = qkn[:, :, 4 * k:4 * k + 4, :]
                copied(dve, ("nat", 0, k)), copied(dve, ("nat", 1, k))
                link(V.tensor_tensor(sq, part, part, ALU.mult))
                s_ = ssq[:, :, 4 * k:4 * k + 4]
                link(V.tensor_reduce(s_, sq, AX.X, ALU.add))
                c = 1.0 if k else float(HD)
                link_as(V.tensor_scalar(s_, s_, c, c * EPS, ALU.mult, ALU.add), "ssq_ready")

            def l2_scale(k):
                s_ = ssq[:, :, 4 * k:4 * k + 4]
                dve.wait_ge(sem("sqq_ready"), told["ssq_ready"])
                link(V.reciprocal(s_, s_))
                for t in range(T2):
                    part = qkn[:, t, 4 * k:4 * k + 4, :]
                    link_as(V.tensor_tensor(part, part, bcast(s_[:, t, :].unsqueeze(2), [P, 4, HD]), ALU.mult),
                            "kn_ready" if k else "qn_ready")

            def gate(t, b):
                return sc32[:, t, 0:24].rearrange("p (h b) -> p h b", b=3)[:, :, b]

            steps = attn_steps()

            def step_scores(i):
                t, b, g = steps[i]
                n = P * (t + 1)
                p_ = pr[i % 2]
                if i > 1:
                    tt, bb, gg_ = steps[i - 2]
                    full(dve, ("pT", tt, bb, gg_, tt))
                mask = cst[:, C_CM + 2 * P - n:C_CM + 2 * P]
                for k in range(2):
                    o = full(dve, ("s", t, b, g, k))
                    link_read(V.scalar_tensor_tensor(out=p_[:, 2 * k:2 * k + 2, 0:n],
                                                     in0=o[:, 0:2 * n].rearrange("p (q s) -> p q s", q=2),
                                                     scalar=DH ** -0.5, in1=bcast(mask.unsqueeze(1), [P, 2, n]),
                                                     op0=ALU.mult, op1=ALU.add), ("s", t, b, g, k))
                link(V.tensor_reduce(mx[i % 2], p_[:, :, 0:n], AX.X, ALU.max))
                link_as(V.tensor_scalar(mx[i % 2], mx[i % 2], -1.0, None, ALU.mult), "max_ready")

            def step_weights(i):
                t, b, g = steps[i]
                n = P * (t + 1)
                p_, d_ = pr[i % 2], den[i % 2]
                dve.wait_ge(sem("exp_done"), i + 1)
                link(V.reciprocal(d_, d_))
                link(V.tensor_tensor(d_, d_, gate(t, 1 + b)[:, 4 * g:4 * g + 4], ALU.mult))
                link_as(V.tensor_tensor(p_[:, :, 0:n], p_[:, :, 0:n], bcast(d_.unsqueeze(2), [P, 4, n]), ALU.mult), "pr_ready")

            nsa_norm(0)
            nsa_norm(1)
            for i in range(len(steps)):
                if i == 5:
                    for t in range(T2):
                        ov = h4(full(dve, ("kk", t))[:, :])
                        link_read(V.tensor_tensor(bst4[:, t], ov, bst4[:, t], ALU.mult), ("kk", t))
                elif i == 7:
                    for t in range(T2):
                        ov = h4(full(dve, ("qk", t))[:, :])
                        link_read(V.tensor_tensor(qkm4[:, t], ov, dec4[:, t], ALU.mult), ("qk", t))
                step_scores(i)
                if i < 6:
                    conv(QKV[i])
                if i == 3:
                    l2_squares(1)
                elif i == 4:
                    l2_scale(1)
                elif i == 5:
                    l2_squares(0)
                elif i == 6:
                    l2_scale(0)
                    for t in range(T2):
                        m0 = vnew[:, t]
                        link(V.tensor_tensor(m0, bst4[:, t], bcast(cst[:, C_M0:C_M0 + P].unsqueeze(1), [P, 4, P]), ALU.mult))
                        link_as(V.tensor_tensor(invU[t], bcast(ident.unsqueeze(1), [P, 4, P]), m0, ALU.subtract), "U_ready")
                step_weights(i)

            def cmp_scores(t):
                ov = full(dve, ("sc", t))[:, 0:128].rearrange("p (h c) -> p h c", h=8)
                link_read(V.scalar_tensor_tensor(out=smc[t], in0=ov, scalar=DH ** -0.5,
                                                 in1=bcast(cst[:, C_CA + 16 * t:C_CA + 16 * t + 16].unsqueeze(1), [P, 8, 16]),
                                                 op0=ALU.mult, op1=ALU.add), ("sc", t))
                link(V.tensor_reduce(mc, smc[t], AX.X, ALU.max))
                link_as(V.tensor_tensor(smc[t], smc[t], bcast(mc.unsqueeze(2), [P, 8, 16]), ALU.subtract), "smc_ready")

            def cmp_weights(t):
                dve.wait_ge(sem("ec_ready"), t + 1)
                link(V.tensor_tensor(smc[t], smc[t], bcast(cst[:, C_CX + 16 * t:C_CX + 16 * t + 16].unsqueeze(1), [P, 8, 16]),
                                     ALU.mult))
                link(V.tensor_reduce(dc, smc[t], AX.X, ALU.add))
                link(V.tensor_scalar(dc, dc, 1e-30, None, ALU.max))
                link(V.reciprocal(dc, dc))
                link(V.tensor_tensor(dc, dc, gate(t, 0), ALU.mult))
                if t:
                    full(dve, ("pcT", t - 1))
                for g in range(2):
                    ins = V.tensor_tensor(pc[:, :, g, 0:16], smc[t][:, 4 * g:4 * g + 4, :],
                                          bcast(dc[:, 4 * g:4 * g + 4].unsqueeze(2), [P, 4, 16]), ALU.mult)
                link_as(ins, "pc_ready")

            for lv in range(1, LEVELS):
                if lv == 1:
                    o = full(dve, ("hid",))
                    for v in range(2):
                        r0 = 64 * v
                        link(V.tensor_tensor(hid[r0:r0 + 32, :], o[r0:r0 + 32, 0:256], bcc[r0:r0 + 32, B_B1:B_B1 + 256],
                                             ALU.add))
                    for v in range(2):
                        r0 = 64 * v
                        ins = V.tensor_tensor(hid[r0:r0 + 32, :], hid[r0:r0 + 32, :], o[r0 + 32:r0 + 64, 0:256], ALU.add)
                    link_read(ins, ("hid",))
                elif lv == 5:
                    cmp_scores(0)
                    cmp_scores(1)
                elif lv == 6:
                    cmp_weights(1)
                for t in range(T2):
                    if lv < LEVELS - 1:
                        tp = h4(full(dve, ("TP", lv, t))[:, :])
                        link_read(V.tensor_tensor(invT[t], invT[t], tp, ALU.subtract), ("TP", lv, t))
                    else:
                        pu = h4(full(dve, ("PU", lv, t))[:, :])
                        link_read(V.tensor_tensor(invU[t], invU[t], pu, ALU.subtract), ("PU", lv, t))
                if lv == 5:
                    cmp_weights(0)
                elif lv == 3:
                    o = full(dve, ("cmp2",))
                    link_read(V.tensor_tensor(kv2[0:64, :], o[0:64, 0:128], bcc[0:64, B_B2:B_B2 + 128], ALU.add), ("cmp2",))
                    link(V.tensor_tensor(kcn[0:64, :], kv2[0:64, 0:64], kv2[0:64, 0:64], ALU.mult))
                    link(V.tensor_reduce(ssk[0:64, :], kcn[0:64, :], AX.X, ALU.add))
                    rstd(ssk[0:64, :], DH, "ssk_ready", "sqk_ready")
                    link_as(V.scalar_tensor_tensor(out=kcn[0:64, :], in0=kv2[0:64, 0:64], scalar=ssk[0:64, :],
                                                   in1=bc[0:64, B_KCG:B_KCG + DH], op0=ALU.mult, op1=ALU.mult), "kcn_ready")
                    for g in range(2):
                        ins = V.tensor_copy(vcb[32 * g:32 * g + 32, 64 * g:64 * g + 64], kv2[32 * g:32 * g + 32, 64:128])
                    link_as(ins, "vc_ready")

            def new_values(t, job):
                ov = h4(full(dve, job)[:, :])
                link_read(V.tensor_tensor(vnew[:, t], ov, bcast(sc32[:, t, 28:32].unsqueeze(2), [P, 4, HD]), ALU.mult), job)

            def nsa_rstd(t):
                o = full(dve, ("ss", t))
                link_read(V.tensor_copy(rsn[:, t:t + 1], o[:, 0:1]), ("ss", t))
                rstd(rsn[:, t:t + 1], 512, "rsn_ready", "rsn_sqrt")

            def gdn_squares(t):
                copied(dve, ("o", t))
                link(V.tensor_tensor(osc[:, t], og[:, t], og[:, t], ALU.mult))
                link(V.tensor_reduce(sso[:, t, :], osc[:, t], AX.X, ALU.add))

            def gdn_out(t):
                rstd(sso[:, t, :], HD, "sso_ready", "sqo_ready")
                link(V.tensor_tensor(og[:, t], og[:, t], bcast(sso[:, t, :].unsqueeze(2), [P, 4, HD]), ALU.mult))
                dve.wait_ge(sem("z_ready"), t + 1)
                link_as(V.tensor_tensor(og[:, t], og[:, t], z[:, t], ALU.mult), "og_ready")

            def add_nsa(t, n):
                o = full(dve, ("yn", t, n))
                xs = xt[:, t, n * 512:(n + 1) * 512]
                link_read(V.scalar_tensor_tensor(out=xs, in0=o[:, :], scalar=rsn[:, t:t + 1], in1=xs,
                                                 op0=ALU.mult, op1=ALU.add), ("yn", t, n))

            def add_gdn(t, n):
                o = full(dve, ("yg", t, n))
                xs = xt[:, t, n * 512:(n + 1) * 512]
                link_read(V.tensor_tensor(xs, xs, o[:, :], ALU.add), ("yg", t, n))

            def second_rstd(t):
                dve.wait_ge(sem("ssx2_ready"), t + 1)
                rstd(ssx2[:, t:t + 1], D, "msx2_ready", "rms2_ready", "rstd2_ready")

            def logits(t):
                o = full(dve, ("lg", t))
                link_read(V.scalar_tensor_tensor(out=lg[:, t, :], in0=o[:, 0:NE], scalar=ssx2[:, t:t + 1],
                                                 in1=bc[:, B_RB:B_RB + NE], op0=ALU.mult, op1=ALU.add), ("lg", t))

            def choose(t):
                link(V.max(m8[:, t, :], lg[:, t, :]))
                thr = bcast(m8[:, t, 3:4], [P, NE])
                V.tensor_tensor(eq_[:, t, :], lg[:, t, :], thr, ALU.is_equal)
                link(V.tensor_tensor(gt_[:, t, :], lg[:, t, :], thr, ALU.is_gt))
                link(V.tensor_reduce(need[:, t:t + 1], gt_[:, t, :], AX.X, ALU.add))
                link(V.tensor_tensor_scan(cum[:, t, :], ones[:, 0:NE], eq_[:, t, :], need[:, t:t + 1], ALU.mult, ALU.add))
                link(V.scalar_tensor_tensor(out=eq_[:, t, :], in0=cum[:, t, :], scalar=4.0, in1=eq_[:, t, :],
                                            op0=ALU.is_le, op1=ALU.mult))
                link_as(V.tensor_tensor(chosen[:, t, :], gt_[:, t, :], eq_[:, t, :], ALU.add), "mask_ready")

            new_values(0, ("uv",))
            gdn_squares(0)
            new_values(1, ("v1",))
            gdn_out(0)
            nsa_rstd(0)
            add_nsa(0, 0)
            nsa_rstd(1)
            add_nsa(0, 1)
            gdn_squares(1)
            gdn_out(1)
            add_nsa(1, 0)
            add_nsa(1, 1)
            add_gdn(0, 0)
            add_gdn(0, 1)
            add_gdn(1, 0)
            second_rstd(0)
            add_gdn(1, 1)
            link(V.memset(posm, 0.0))
            link(V.memset(gates, 0.0))
            logits(0)
            choose(0)
            second_rstd(1)
            logits(1)
            choose(1)
            link_as(V.tensor_tensor(lg, lg, bcast(m8[:, :, 0:1], [P, T2, NE]), ALU.subtract), "lgm_ready")
            o = full(dve, ("pos",))
            link(V.scalar_tensor_tensor(out=posm[:, :, 0:NE], in0=o[:, 0:64].rearrange("p (t n) -> p t n", t=T2),
                                        scalar=1.0, in1=chosen, op0=ALU.add, op1=ALU.mult))

            iota = cst[:, C_IO:C_IO + CAP]

            def select(buf, e):
                for t in range(T2):
                    ins = V.tensor_scalar(m_sel[buf][:, t, :], iota, posm[:, t, bass.ds(e, 1)], None, ALU.is_equal)
                ins.then_inc(sem("sel_ready"), 1)
                V.tensor_copy(m_eb[buf][:, 0, :], bcast(ident[:, bass.ds(e, 1)], [P, CAP]))
                V.tensor_copy(m_eb[buf][:, 2, :], bcast(cst[:, bass.ds(e + (C_ID + NE), 1)], [P, CAP]))
                V.tensor_copy(m_eb[buf][:, 1, :], bcast(cst[:, bass.ds(e + (C_ID + 2 * NE), 1)], [P, CAP]))\
                    .then_inc(sem("eb_ready"), 1)

            def pair(r, quad, ip, half, first=False):
                it = quad * 2 + half
                e0 = ip * 4 + 2 * half
                for par in range(2):
                    n = it * 2 + par
                    if par == 0:
                        for t in range(T2):
                            for u in range(2):
                                ins = V.tensor_scalar(m_selw[:, t, u * CAP:(u + 1) * CAP], iota,
                                                      posm[:, t, bass.ds(e0 + u, 1)],
                                                      gates[:, t, bass.ds(e0 + u, 1)], ALU.is_equal, ALU.mult)
                        ins.then_inc(sem("selw_ready"), 1)
                    used(dve, quad, 12 * half + 6 * par + 1, first)
                    V.tensor_scalar(m_g, bG[:, :], 7.0, None, ALU.min).then_inc(sem("gate_read"), 1)
                    select(1 - par, e0 + (par + 1))
                    dve.wait_ge(sem("sg_ready"), n + 1)
                    V.tensor_tensor(m_gs, m_g, m_sg, ALU.mult).then_inc(sem("gs_done"), 1)
                    used(dve, quad, 12 * half + 6 * par + 3, first)
                    V.tensor_scalar(m_uc, bU[:, :], -7.0, 7.0, ALU.max, ALU.min).then_inc(sem("up_read"), 1)
                    dve.wait_ge(sem("gs_done"), n + 1)
                    dve.wait_ge(sem("up_read"), n + 1)
                    V.scalar_tensor_tensor(out=m_act, in0=m_uc, scalar=1.0, in1=m_gs, op0=ALU.add, op1=ALU.mult)\
                        .then_inc(sem("act_ready"), 1)
                    used(dve, quad, 12 * half + 6 * par + 5, first)
                    V.tensor_copy(m_y[64 * par:64 * par + 64, 512:1024], bD[64:128, :]).then_inc(sem("y1_read"), 1)
                for hf in range(2):
                    for t in range(T2):
                        dve.wait_ge(sem("scattered"), it * 4 + (2 * hf + t + 1))
                        xs = xt[:, t, 512 * hf:512 * hf + 512]
                        V.tensor_tensor(xs, xs, scatter_bank[hf][t][:, :], ALU.add).then_inc(sem("added"), 1)
                dve.wait_ge(sem("added"), it * 4 + 4)

            select(0, 0)
            link_read(V.tensor_reduce(cmax, full(dve, ("pos",))[:, 64:96], AX.X, ALU.max), ("pos",))
            link_as(V.tensor_copy(cnt_i[:, :], cmax), "counts_ready")
            dve.wait_ge(sem("lge_ready"), 1)
            link(V.tensor_tensor(lg, lg, chosen, ALU.mult))
            link(V.tensor_reduce(gsum, lg, AX.X, ALU.add))
            link(V.reciprocal(gsum, gsum))
            link(V.tensor_tensor(gates[:, :, 0:NE], lg, bcast(gsum.unsqueeze(2), [P, T2, NE]), ALU.mult))
            for half in range(2):
                pair(0, 0, 0, half, first=True)
            with dve.Fori(1, QUADS) as ip:
                for half in range(2):
                    pair(0, ip, ip, half)
            most = dve.value_load(cnt_i[0:1, 0:1], min_val=0, max_val=SEQ)
            with dve.Fori(1, ROUNDS) as r:
                with dve.If(most > r * CAP):
                    dve.wait_ge(sem("out_written"), (r + 3) * 16)
                    dve.wait_ge(sem("gathered"), r * (NE + 1))
                    V.tensor_scalar(posm, posm, float(-CAP), None, ALU.add).then_inc(sem("shifted"), 1)
                    dve.wait_ge(sem("shifted"), r)
                    select(0, 0)
                    with dve.Fori(0, QUADS) as ip:
                        for half in range(2):
                            pair(r, r * QUADS + ip, ip, half)
                    dve.wait_ge(sem("out_written"), (r + 4) * 16)
                    V.tensor_scalar(cmax, cmax, 1.0, None, ALU.mult)


NBC = 12


_INS = ['x', 'attn_norm_g', 'w_in', 'nsa_q_norm_g', 'nsa_kc_norm_g', 'nsa_ks_norm_g', 'nsa_kw_norm_g',
        'cmp_k_pos', 'cmp_k_w1', 'cmp_k_b1', 'cmp_k_w2', 'cmp_k_b2', 'cmp_v_pos', 'cmp_v_w1', 'cmp_v_b1',
        'cmp_v_w2', 'cmp_v_b2', 'nsa_out_norm_g', 'gdn_conv_w', 'gdn_a_log', 'gdn_dt_bias', 'gdn_out_norm_g',
        'w_out', 'ffn_norm_g', 'router_w', 'router_b', 'exp_w_gate', 'exp_b_gate', 'exp_w_up', 'exp_b_up',
        'exp_w_down', 'exp_b_down']


def const_table():
    import numpy as np
    c = np.zeros((P, C_END), np.float32)
    i, j = np.arange(P)[:, None], np.arange(P)[None, :]
    c[:, C_ID:C_ID + P] = i == j
    c[:, C_ONE:C_ONE + P] = 1.0
    c[:, C_TRI:C_TRI + P] = i <= j
    c[:, C_STR:C_STR + P] = i < j
    c[:, C_CM + P:C_CM + 2 * P] = np.where(j <= i, 0.0, -BIG)
    c[:, C_DM:C_DM + P] = np.where(i <= j, 0.0, -BIG)
    for lv in range(1, LEVELS):
        b = 1 << lv
        c[:, C_LV + (lv - 1) * P:C_LV + lv * P] = ((j // b) % 2 == 1) & (i // b == j // b - 1)
    c[:, C_M0:C_M0 + P] = (j % 2 == 1) & (i == j - 1)
    blk = np.arange(16)[None, :]
    for t in range(T2):
        seen = (blk < NCMP) & (16 * blk + 31 <= t * P + np.arange(P)[:, None])
        c[:, C_CA + 16 * t:C_CA + 16 * t + 16] = np.where(seen, 0.0, -BIG)
        c[:, C_CX + 16 * t:C_CX + 16 * t + 16] = seen
    c[:, C_IO:C_IO + CAP] = 1 + np.arange(CAP)[None, :]
    return c


def kernel(**inputs):
    import numpy as _np
    import concourse.bacc as _bacc
    from concourse import mybir as _mybir
    from concourse.bass_utils import run_bass_kernel_spmd as _run

    nc = _bacc.Bacc("TRN2", target_bir_lowering=False, num_devices=1)
    arrays, aps = {}, {}
    for name in _INS + ["const_table"]:
        v = const_table() if name == "const_table" else _np.ascontiguousarray(inputs[name])
        arrays[f"in_{name}_dram"] = v
        aps[name] = nc.dram_tensor(f"in_{name}_dram", v.shape, _mybir.dt.from_np(v.dtype), kind="ExternalInput").ap()
    out = nc.dram_tensor("out_0_dram", (1, SEQ, D), _mybir.dt.from_np(_np.dtype("float32")), kind="ExternalOutput").ap()
    hybrid_block(nc, aps, out)
    r = _run(nc, [arrays], core_ids=[0])
    return r.results[0]["out_0_dram"]
```
